# Optimizing a Trainium2 kernel written in Bass

```python
import math, functools
import jax, jax.numpy as jnp
from jax import lax
import numpy as np

D_MODEL = 1024
BATCH = 1
SEQ = 256
DEPTH = 1

CHUNK = 64
DN_HEADS = 8
DN_HEAD_DIM = 64
DN_WIDTH = DN_HEADS * DN_HEAD_DIM
CONV_WIDTH = 4
POOL_GROUPS = 4
POOL_WINDOWS = (2, 4, 8, 16)
POOL_WIDTH = D_MODEL // 2
POOL_GROUP_DIM = POOL_WIDTH // POOL_GROUPS
N_BRANCH = 2
IN_WIDTH = 3 * DN_WIDTH + DN_WIDTH + 2 * DN_HEADS + POOL_WIDTH + N_BRANCH * D_MODEL
N_EXPERTS = 32
TOP_K = 4
D_FF = D_MODEL
SWIGLU_LIMIT = 7.0
SWIGLU_ALPHA = 1.702
NORM_EPS = 1e-6

kernel_name = "hybrid_deltanet_pool_moe_block"

def rms_norm(x, g):
    xf = x.astype(jnp.float32)
    y = xf * lax.rsqrt(jnp.mean(xf * xf, axis=-1, keepdims=True) + NORM_EPS)
    return (y * g.astype(jnp.float32)).astype(x.dtype)

def l2_normalize(t):
    return t * lax.rsqrt(jnp.sum(t * t, axis=-1, keepdims=True) + NORM_EPS)

def causal_depthwise_conv(u, w):
    K = w.shape[0]
    L = u.shape[1]
    up = jnp.pad(u, ((0, 0), (K - 1, 0), (0, 0)))
    return sum(up[:, j:j + L] * w[j] for j in range(K))

def chunked_gated_delta_rule(q, k, v, beta, g):
    B, H, L, dk = q.shape
    dv = v.shape[-1]
    n = L // CHUNK
    rs = lambda t: t.reshape(B, H, n, CHUNK, *t.shape[3:])
    q, k, v, beta, g = rs(q), rs(k), rs(v), rs(beta), rs(g)
    G = jnp.cumsum(g, axis=-1)
    causal = jnp.tril(jnp.ones((CHUNK, CHUNK), dtype=bool))
    strict = jnp.tril(jnp.ones((CHUNK, CHUNK), dtype=bool), -1)
    decay = jnp.exp(jnp.where(causal, G[..., :, None] - G[..., None, :], -jnp.inf))
    kk = jnp.einsum('bhncd,bhned->bhnce', k, k)
    A = jnp.where(strict, beta[..., :, None] * kk * decay, 0.0)
    eye = jnp.eye(CHUNK, dtype=jnp.float32)
    T = lax.linalg.triangular_solve(eye + A, jnp.broadcast_to(eye, A.shape),
                                    left_side=True, lower=True)
    eG = jnp.exp(G)
    W = jnp.einsum('bhnce,bhned->bhncd', T, k * (beta * eG)[..., None])
    U = jnp.einsum('bhnce,bhned->bhncd', T, v * beta[..., None])
    qk = jnp.einsum('bhncd,bhned->bhnce', q, k) * decay
    qg = q * eG[..., None]
    kd = k * jnp.exp(G[..., -1:] - G)[..., None]
    glast = jnp.exp(G[..., -1])

    def step(S, inp):
        Wc, Uc, qkc, qgc, kdc, gc = inp
        v_new = Uc - jnp.einsum('bhcd,bhdv->bhcv', Wc, S)
        o = jnp.einsum('bhcd,bhdv->bhcv', qgc, S) + jnp.einsum('bhce,bhev->bhcv', qkc, v_new)
        S = S * gc[..., None, None] + jnp.einsum('bhcd,bhcv->bhdv', kdc, v_new)
        return S, o

    xs = tuple(jnp.moveaxis(t, 2, 0) for t in (W, U, qk, qg, kd, glast))
    S0 = jnp.zeros((B, H, dk, dv), jnp.float32)
    _, o = lax.scan(step, S0, xs)
    return jnp.moveaxis(o, 0, 2).reshape(B, H, L, dv)

def trailing_mean(u, w):
    L = u.shape[1]
    cs = jnp.cumsum(u.astype(jnp.float32), axis=1)
    cs = jnp.pad(cs, ((0, 0), (w, 0), (0, 0)))
    window_sum = cs[:, w:] - cs[:, :L]
    count = jnp.minimum(jnp.arange(L) + 1, w).astype(jnp.float32)
    return (window_sum / count[None, :, None]).astype(u.dtype)

def multiscale_pool(u, pool_w, pool_scale):
    B, L, _ = u.shape
    ug = u.reshape(B, L, POOL_GROUPS, POOL_GROUP_DIM)
    pooled = jnp.stack([trailing_mean(ug[:, :, i], POOL_WINDOWS[i]) for i in range(POOL_GROUPS)],
                       axis=2) - ug
    y = jnp.einsum('blgc,gcd->blgd', pooled, pool_w)
    return y.reshape(B, L, POOL_WIDTH) * pool_scale

def moe_ffn(h, w_router, b_router, w_gate_up, b_gate_up, w_down, b_down):
    B, L, D = h.shape
    t = h.reshape(B * L, D)
    logits = (t @ w_router + b_router).astype(jnp.float32)
    top_v, top_i = lax.top_k(logits, TOP_K)
    top_w = jax.nn.softmax(top_v, axis=-1)
    comb = jnp.sum(jax.nn.one_hot(top_i, N_EXPERTS, dtype=jnp.float32) * top_w[..., None],
                   axis=1).astype(h.dtype)
    y = jnp.zeros_like(t)
    for e in range(N_EXPERTS):
        gu = t @ w_gate_up[e] + b_gate_up[e]
        gate, up = gu[:, :D_FF], gu[:, D_FF:]
        gate = jnp.minimum(gate, SWIGLU_LIMIT)
        up = jnp.clip(up, -SWIGLU_LIMIT, SWIGLU_LIMIT)
        act = gate * jax.nn.sigmoid(SWIGLU_ALPHA * gate) * (up + 1.0)
        y = y + comb[:, e:e + 1] * (act @ w_down[e] + b_down[e])
    return y.reshape(B, L, D)

def setup_inputs(seed: int = 0) -> dict:
    key = jax.random.key(seed)
    ks = jax.random.split(key, 24)
    f32 = jnp.float32
    nrm = lambda k, shape, s: jax.random.normal(k, shape, f32) * s
    dt = jnp.exp(jax.random.uniform(ks[4], (DEPTH, DN_HEADS), f32,
                                    math.log(1e-3), math.log(1e-1)))
    return {
        "x": jax.random.normal(ks[0], (BATCH, SEQ, D_MODEL), f32),
        "g_mix": 1.0 + nrm(ks[1], (DEPTH, D_MODEL), 0.02),
        "w_in": nrm(ks[2], (DEPTH, D_MODEL, IN_WIDTH), D_MODEL ** -0.5),
        "conv_w": nrm(ks[3], (DEPTH, CONV_WIDTH, 3 * DN_WIDTH), CONV_WIDTH ** -0.5),
        "a_log": jnp.log(jax.random.uniform(ks[5], (DEPTH, DN_HEADS), f32, 1.0, 16.0)),
        "dt_bias": dt + jnp.log(-jnp.expm1(-dt)),
        "dn_norm": 1.0 + nrm(ks[6], (DEPTH, DN_HEAD_DIM), 0.02),
        "w_up_a": nrm(ks[7], (DEPTH, DN_WIDTH, D_MODEL), DN_WIDTH ** -0.5),
        "pool_w": nrm(ks[8], (DEPTH, POOL_GROUPS, POOL_GROUP_DIM, POOL_GROUP_DIM), POOL_GROUP_DIM ** -0.5),
        "pool_scale": 1.0 + nrm(ks[9], (DEPTH, POOL_WIDTH), 0.02),
        "w_up_b": nrm(ks[10], (DEPTH, POOL_WIDTH, D_MODEL), POOL_WIDTH ** -0.5),
        "w_out": nrm(ks[11], (DEPTH, D_MODEL, D_MODEL), D_MODEL ** -0.5),
        "g_ffn": 1.0 + nrm(ks[12], (DEPTH, D_MODEL), 0.02),
        "w_router": nrm(ks[13], (DEPTH, D_MODEL, N_EXPERTS), D_MODEL ** -0.5),
        "b_router": nrm(ks[14], (DEPTH, N_EXPERTS), 0.01),
        "w_gate_up": nrm(ks[15], (DEPTH, N_EXPERTS, D_MODEL, 2 * D_FF), D_MODEL ** -0.5),
        "b_gate_up": nrm(ks[16], (DEPTH, N_EXPERTS, 2 * D_FF), 0.01),
        "w_down": nrm(ks[17], (DEPTH, N_EXPERTS, D_FF, D_MODEL), D_FF ** -0.5),
        "b_down": nrm(ks[18], (DEPTH, N_EXPERTS, D_MODEL), 0.01),
        "g_final": 1.0 + nrm(ks[19], (D_MODEL,), 0.02),
    }

def reference(x, g_mix, w_in, conv_w, a_log, dt_bias, dn_norm, w_up_a, pool_w, pool_scale,
              w_up_b, w_out, g_ffn, w_router, b_router, w_gate_up, b_gate_up, w_down, b_down,
              g_final):
    f32 = jnp.float32
    B, L, D = x.shape
    sizes = [3 * DN_WIDTH, DN_WIDTH, DN_HEADS, DN_HEADS, POOL_WIDTH]
    split_idx = [int(s) for s in np.cumsum(sizes)]
    for l in range(DEPTH):
        h = rms_norm(x, g_mix[l])
        p = h @ w_in[l]
        qkv, z, b_raw, a_raw, u, gates = jnp.split(p, split_idx, axis=-1)

        qkv = jax.nn.silu(causal_depthwise_conv(qkv, conv_w[l]))
        q, k, v = jnp.split(qkv, 3, axis=-1)
        heads = lambda t: t.reshape(B, L, DN_HEADS, DN_HEAD_DIM).transpose(0, 2, 1, 3).astype(f32)
        q = l2_normalize(heads(q)) * (DN_HEAD_DIM ** -0.5)
        k = l2_normalize(heads(k))
        v = heads(v)
        beta = jax.nn.sigmoid(b_raw.astype(f32)).transpose(0, 2, 1)
        g = (-jnp.exp(a_log[l].astype(f32))
             * jax.nn.softplus(a_raw.astype(f32) + dt_bias[l].astype(f32))).transpose(0, 2, 1)
        o = chunked_gated_delta_rule(q, k, v, beta, g).transpose(0, 2, 1, 3)
        o = rms_norm(o, dn_norm[l]) * jax.nn.silu(z.reshape(B, L, DN_HEADS, DN_HEAD_DIM).astype(f32))
        y_a = o.reshape(B, L, DN_WIDTH).astype(x.dtype) @ w_up_a[l]

        y_b = multiscale_pool(u, pool_w[l], pool_scale[l]) @ w_up_b[l]

        gate_a, gate_b = jnp.split(jax.nn.sigmoid(gates), N_BRANCH, axis=-1)
        x = x + (gate_a * y_a + gate_b * y_b) @ w_out[l]

        x = x + moe_ffn(rms_norm(x, g_ffn[l]), w_router[l], b_router[l], w_gate_up[l],
                        b_gate_up[l], w_down[l], b_down[l])
    return rms_norm(x, g_final)


_drawn_inputs = setup_inputs


def setup_inputs(seed=0):
    import zlib

    import numpy as np

    out = dict(_drawn_inputs(seed))
    spreads = {}
    factors = {'dn_norm': 2.827,
     'b_gate_up': 8.0,
     'b_down': 24.017,
     'g_final': 23.0,
     'pool_scale': 3.717,
     'b_router': 3.071}
    for name, (base, spread) in spreads.items():
        noise = np.random.default_rng([zlib.crc32(name.encode()), seed]).standard_normal(out[name].shape)
        drawn = base * np.exp(spread * noise) if base else spread * noise
        out[name] = __import__('jax').numpy.asarray(drawn.astype(out[name].dtype))
    for name, factor in factors.items():
        out[name] = (out[name] * factor).astype(out[name].dtype)
    return out
```

```python
from contextlib import ExitStack

import concourse.bass as bass
import numpy as np
from concourse import mybir

F32 = mybir.dt.float32
I32 = mybir.dt.int32
ALU = mybir.AluOpType
ACT = mybir.ActivationFunctionType
AX = mybir.AxisListType

P = 128
D = 1024
L = 256
TT = L // P
KD = D // P
HEADS, HD = 8, 64
HP = HEADS // 2
C = 64
NCH = L // C
SLOTS = HP * NCH
HALF = SLOTS // 2
DN = HEADS * HD
TAPS = 4
POOLS = (2, 4, 8, 16)
UPAD = 16
E = 32
TOP_K = 4
F = D
LIMIT, ALPHA = 7.0, 1.702
EPS = 1e-6
CAP = 64
ROUNDS = L // CAP
UNIT = 2 * D
GU_UNITS = KD
WD_UNITS = F // P // 2
LEVELS = (2, 4, 8, 16, 32)

CONSTS, _at = {}, 0
for _n, _w in (("ident", P), ("tri", P), ("ones_blk", P), ("ones", P), ("before", P), ("iota", P),
               ("eye", C), ("lower", C), ("upper", C), ("m1", C), ("m1t", C),
               ("lt2", C), ("lt4", C), ("lt8", C), ("lt16", C), ("lt32", C), ("inv", 4 * UPAD)):
    CONSTS[_n] = (_at, _w)
    _at += _w
NCONST = _at
PARAMS, _at = {}, 0
for _n, _w in (("conv", 12 * TAPS), ("dn", 1), ("pscale", 4), ("alog", HEADS), ("dtb", HEADS),
               ("brouter", E), ("gmix", KD), ("gffn", KD)):
    PARAMS[_n] = (_at, _w)
    _at += _w
NPARAM = _at
MARK, GONE = -3.2e38, -3.3e38


def const_table():
    t = np.zeros((P, NCONST), np.float32)
    p = np.arange(P)[:, None]
    j = np.arange(P)[None, :]
    e = np.arange(C)[None, :]
    r, c = p // C, p % C

    def put(name, value):
        a, w = CONSTS[name]
        t[:, a:a + w] = value

    put("ident", p == j)
    put("tri", (r == j // C) & (c <= j % C))
    put("ones_blk", r == j // C)
    put("ones", 1.0)
    put("before", p < j)
    put("iota", np.broadcast_to(j % CAP, (P, P)))
    put("eye", c == e)
    put("lower", e < c)
    put("upper", e >= c)
    put("m1", (c % 2 == 1) & (e == c - 1))
    put("m1t", (e % 2 == 1) & (c == e - 1))
    for b in LEVELS:
        put(f"lt{b}", ((e // b) % 2 == 1) & (c // b == e // b - 1))
    tok = np.arange(UPAD)
    put("inv", np.concatenate([1.0 / np.minimum(tok + 1, w) for w in POOLS])[None, :])
    return t


K0, Q0, V0, Z0, BA0, U0, GA0 = DN, 0, 2 * DN, 3 * DN, 4 * DN, 4 * DN + 16, 4 * DN + 16 + D // 2
GB0 = GA0 + D
GROUPS = ([("k", K0), ("k", K0 + 256), ("q", Q0), ("q", Q0 + 256), ("v", V0), ("v", V0 + 256),
           ("u", U0), ("u", U0 + 256), ("z", Z0), ("z", Z0 + 256)]
          + [("gb", GB0 + 256 * i) for i in range(4)] + [("ga", GA0 + 256 * i) for i in range(4)])
W_SLOTS = 2

WUSE = ([("in", g) for g in range(14)] + [("pool", 0), ("pool", 1)] + [("ub", i) for i in range(4)]
        + [("in", g) for g in range(14, 18)] + [("ua", i) for i in range(4)]
        + [("wo", i) for i in range(4)])
W_ON_DVE = ("ub", "ua", "wo")


def wuse(kind, i):
    n = WUSE.index((kind, i))
    dve = kind in W_ON_DVE
    return n, sum((k in W_ON_DVE) == dve for k, _ in WUSE[:n + 1])


JOBS = ([(n, h) for n in ("KT", "VT", "KK", "KQ", "AT") for h in (0, 1)]
        + [j for b in LEVELS for j in
           [(f"M{b}", 0), (f"M{b}", 1)]
           + ([(f"TN{b}", 0), (f"TN{b}", 1)] if b != LEVELS[-1] else [])
           + [(f"NT{b}", 0), (f"NT{b}", 1)]]
        + [(n, h) for n in ("WT", "U") for h in (0, 1)]
        + [("O", 0), ("DS", 0), ("WS", 1), ("O", 1), ("DS", 1), ("WS", 2), ("O", 2), ("DS", 2),
           ("WS", 3), ("O", 3)])
JOB = {j: n for n, j in enumerate(JOBS)}


def schedule():
    blocks = iter([("in", g, b) for g in range(6, 14) for b in range(2)]
                  + [("pool", i, 1) for i in range(2)] + [("ub", i, 1) for i in range(4)]
                  + [("in", g, b) for g in range(14, 18) for b in range(2)])
    order = []

    def jobs(*names):
        order.extend(("job",) + n for n in names)

    def filler(count=1):
        order.extend(b for b in [next(blocks, None) for _ in range(count)] if b)

    for name in ("KT", "VT", "KK"):
        jobs((name, 0), (name, 1))
        filler()
    jobs(("KQ", 0), ("KQ", 1), ("AT", 0), ("AT", 1))
    filler(2)
    for b in LEVELS:
        jobs((f"M{b}", 0), (f"M{b}", 1))
        filler()
        if b != LEVELS[-1]:
            jobs((f"TN{b}", 0), (f"TN{b}", 1))
        jobs((f"NT{b}", 0), (f"NT{b}", 1))
        filler()
    jobs(("WT", 0), ("WT", 1), ("U", 0), ("U", 1))
    filler()
    for n in range(NCH):
        if n:
            jobs(("WS", n))
            filler()
        jobs(("O", n))
        if n < NCH - 1:
            jobs(("DS", n))
            filler()
    order.append(("osquare",))
    filler()
    order.append(("osum",))
    filler(2)
    order.append(("onorm",))
    filler(30)
    return order


ORDER = schedule()


def on_act(job):
    return job[0][0:2] in ("KT", "VT", "AT", "TN", "NT", "WT", "U", "O")


def act_number(job):
    return sum(on_act(j) for j in JOBS[:JOB[job] + 1])


def build_program(nc, x, consts, params, w_in, pool_w, w_up_a, w_up_b, w_out, w_router,
                  w_gate_up, b_gate_up, w_down, b_down, g_final, out):
    with ExitStack() as ctx:
        def sb(name, shape, dt=F32):
            return ctx.enter_context(nc.sbuf_tensor(name, shape, dt))

        def sem(name):
            return ctx.enter_context(nc.semaphore(name))

        ps = ctx.enter_context(nc.psum_tensor("ps", [P, 8, 512], F32))

        ring = sb("ring", [P, GU_UNITS + WD_UNITS, UNIT])
        cst = sb("cst", [P, NCONST])
        par = sb("par", [P, NPARAM])
        xs = sb("xs", [P, TT, D])
        hT = sb("hT", [P, KD, L])
        wring = sb("wring", [P, W_SLOTS, KD, 256])
        wout = sb("wout", [P, KD, D])
        gates = sb("gates", [P, 2, KD, L])
        zT = sb("zT", [P, HP, L])
        ub = sb("ub", [P, 2, 4, UPAD + L])
        TTm = sb("TTm", [P, SLOTS, C])
        w_ba = sb("w_ba", [P, KD, 2 * HEADS])
        poolw = sb("poolw", [P, 4, P])
        wrt = sb("wrt", [P, KD, E])
        state = sb("state", [P, 3, HP, C])
        sm = sb("sm", [P, 512])
        flag = sb("flag", [1, 2], I32)
        scr = ring[:, 0:GU_UNITS, :].rearrange("p u n -> p (u n)")
        CP = 4 + L
        cpad = scr[:, 0:12 * CP].rearrange("p (b n) -> p b n", b=12)
        o = 12 * CP
        cq = scr[:, o:o + 12 * L].rearrange("p (b n) -> p b n", b=12)
        kT, qT, vT = cq[:, 0:4], cq[:, 4:8], cq[:, 8:12]
        o += 12 * L

        def slots(at):
            return scr[:, at:at + SLOTS * C].rearrange("p (s n) -> p s n", s=SLOTS)

        Kb, kd, vtok, F1, F2, A, qkT, egr = (slots(o + i * SLOTS * C) for i in range(8))
        o += 8 * SLOTS * C
        LT = [slots(o), slots(0)]
        AT, N = slots(SLOTS * C), slots(2 * SLOTS * C)
        T = gates[:, 0, 0:4].rearrange("p b n -> p (b n)").rearrange("p (s n) -> p s n", s=SLOTS)
        ktok = gates[:, 0, 4:8].rearrange("p b n -> p (b n)").rearrange("p (s n) -> p s n", s=SLOTS)
        WT, U = A, AT
        xn = cq.rearrange("p b n -> p (b n)")[:, 0:TT * D].rearrange("p (t n) -> p t n", t=TT)
        sq = TTm.rearrange("p s n -> p (s n)").rearrange("p (b n) -> p b n", b=HP)
        sg = zT[:, 0:2, :]
        zsig = F1.rearrange("p s n -> p (s n)").rearrange("p (b n) -> p b n", b=HP)
        usum = F2.rearrange("p s n -> p (s n)")[:, 0:3 * (UPAD + L)].rearrange("p (g n) -> p g n", g=3)
        gtri = ub.rearrange("p a b n -> p (a b n)")[:, 0:TT * HEADS * P].rearrange(
            "p (t h n) -> p t h n", t=TT, h=HEADS)
        oT = kT
        S, Sg, vnew = state[:, 0], state[:, 1], state[:, 2]
        upa = ring[:, GU_UNITS:GU_UNITS + 2, :].rearrange("p u n -> p (u n)").rearrange(
            "p (k n) -> p k n", k=4)
        upb = ring[:, GU_UNITS + 2:GU_UNITS + 4, :].rearrange("p u n -> p (u n)").rearrange(
            "p (k n) -> p k n", k=4)
        mo = wout.rearrange("p k n -> p (k n)")
        xn2 = mo[:, 0:2048].rearrange("p (t n) -> p t n", t=TT)
        xe = mo[:, 2048:2560].rearrange("p (k n) -> p k n", k=KD)
        gmin, sig, act_t, act_a, actT, outS = (mo[:, 2560 + 512 * i:3072 + 512 * i] for i in range(6))
        ctS = mo[:, 5632:5888]
        selw = mo[:, 5888:6144].rearrange("p (t n) -> p t n", t=TT)
        sel = mo[:, 6144:6272].rearrange("p (t n) -> p t n", t=TT)
        NPOS = ROUNDS * E + 1
        pos = mo[:, 6272:6272 + TT * NPOS].rearrange("p (t n) -> p t n", t=TT)
        comb = mo[:, 6600:6600 + TT * NPOS].rearrange("p (t n) -> p t n", t=TT)
        combT = mo[0:E, 6912:6912 + L]
        rt = mo[:, 7168:8192]
        h2T = hT
        wf = wring.rearrange("p s k n -> p (s k n)")
        b_gu = wf[0:1, 0:2 * F]
        b_dn = wf[0:E, 2 * F:3 * F]
        gfin = wf[:, 3 * F:4 * F]

        def cc(name):
            a, w = CONSTS[name]
            return cst[:, a:a + w]

        def pp(name):
            a, w = PARAMS[name]
            return par[:, a:a + w]

        ident, ones, ones_blk, tri, eye = cc("ident"), cc("ones"), cc("ones_blk"), cc("tri"), cc("eye")
        ssx, rstd = sm[:, 0:2], sm[:, 2:4]
        ones_c = sm[:, 4:5]
        eps_c = sm[:, 5:6]
        av, ab, sp_, gtok, beta_t = (sm[:, 16 + 16 * i:32 + 16 * i].rearrange("p (t h) -> p t h", t=TT)
                                     for i in range(5))
        ea = sm[:, 96:104]
        colG, colB, colL, eG, bEG, kdf, egl = (sm[:, 112 + 16 * i:128 + 16 * i] for i in range(7))

        x_landed = [sem(f"x_landed{t}") for t in range(TT)]
        tables_landed = sem("tables_landed")
        small_landed = sem("small_landed")
        w_landed = [sem(f"w_landed{s}") for s in range(W_SLOTS)]
        upa_landed, upb_landed, wout_landed = sem("upa_landed"), sem("upb_landed"), sem("wout_landed")
        late_landed = sem("late_landed")
        out_landed = sem("out_landed")
        pads_zeroed = sem("pads_zeroed")
        ss_ready, var_sqrt, rstd_ready = sem("ss_ready"), sem("var_sqrt"), sem("rstd_ready")
        xn_ready, xT_done, hT_ready = sem("xn_ready"), sem("xT_done"), sem("hT_ready")
        w_done, w_act, w_dve = sem("w_done"), sem("w_act"), sem("w_dve")
        conv_ready, sig_ready, silu_ready = sem("conv_ready"), sem("sig_ready"), sem("silu_ready")
        sq_ready, sumsq_done, norm_sqrt, normed = (sem("sq_ready"), sem("sumsq_done"),
                                                   sem("norm_sqrt"), sem("normed"))
        ba_done, ba_read, sp_exp, decay_act = sem("ba_done"), sem("ba_read"), sem("sp_exp"), sem("decay_act")
        g_ready, cols_done, cols_ready, cols_exp, cols_all = (sem("g_ready"), sem("cols_done"),
                                                              sem("cols_ready"), sem("cols_exp"), sem("cols_all"))
        rows_done, rows_exp, rows_diff, f_exp, f_ready = (sem("rows_done"), sem("rows_exp"),
                                                          sem("rows_diff"), sem("f_exp"), sem("f_ready"))
        dn_pe, dn_dve, dn_act = sem("dn_pe"), sem("dn_dve"), sem("dn_act")
        tok_scaled, base_ready, lt_ready = sem("tok_scaled"), sem("base_ready"), sem("lt_ready")
        qg_ready, s_ready = sem("qg_ready"), sem("s_ready")
        z_ready, pooled_ready, pool_step = sem("z_ready"), sem("pooled_ready"), sem("pool_step")
        o_sq, o_sumsq, o_sqrt, o_ready = sem("o_sq"), sem("o_sumsq"), sem("o_sqrt"), sem("o_ready")
        mix_ready, x1_ready, xn2_ready = sem("mix_ready"), sem("x1_ready"), sem("xn2_ready")
        x2T_done, h2T_ready, logits_done = sem("x2T_done"), sem("h2T_ready"), sem("logits_done")
        soft_in, soft_exp, mask_ready, count_done, route_ready = (
            sem("soft_in"), sem("soft_exp"), sem("mask_ready"), sem("count_done"), sem("route_ready"))
        combT_done, combT_ready, zero_ready = sem("combT_done"), sem("combT_ready"), sem("zero_ready")
        flag_ready = sem("flag_ready")
        dve_step = sem("dve_step")
        act_step = sem("act_step")
        gu_landed = [sem(f"gu_landed{u}") for u in range(GU_UNITS)]
        wd_landed = [sem(f"wd_landed{u}") for u in range(WD_UNITS)]
        bias_landed = sem("bias_landed")
        gu_used, wd_used, bias_used = sem("gu_used"), sem("wd_used"), sem("bias_used")
        sel_ready, selw_ready, gathered, xe_ready = sem("sel_ready"), sem("selw_ready"), sem("gathered"), sem("xe_ready")
        gmin_ready, gate_sig, gu_read, act_ready = sem("gmin_ready"), sem("gate_sig"), sem("gu_read"), sem("act_ready")
        ct_done, ct_copied, actT_done, actT_copied = sem("ct_done"), sem("ct_copied"), sem("actT_done"), sem("actT_copied")
        out_copied, scattered = sem("out_copied"), sem("scattered")
        up_ready = sem("up_ready")
        y_ready, ssf_ready, f_sqrt, fin_ready = sem("y_ready"), sem("ssf_ready"), sem("f_sqrt"), sem("fin_ready")

        def bank_q(job):
            r = JOB[job] % 3
            return [ps[0:C, 2 + 2 * r, :], ps[C:P, 3 + 2 * r, :]]

        def after_job(eng, job):
            eng.wait_ge(dn_dve, JOB[job] + 1)
            if on_act(job):
                eng.wait_ge(dn_act, act_number(job))

        def flat_banks(first, n):
            return ps[:, first:first + 2, :].rearrange("p b m -> p (b m)").rearrange(
                "p (s n) -> p s n", n=n)

        def hslots(a, h):
            return a[:, h * HALF:(h + 1) * HALF, :]

        def bc(a, n):
            return a.unsqueeze(2).to_broadcast([a.shape[0], a.shape[1], n])

        def rep(a, m):
            return a.unsqueeze(1).to_broadcast([a.shape[0], m, a.shape[1]])

        def chunk(a, n):
            return a.rearrange("p (hp n) c -> p hp n c", hp=HP)[:, :, n, :]

        block = ctx.enter_context(nc.Block())

        @block.sync
        def _(sp):
            sp.dma_start(cst[:], consts).then_inc(tables_landed, 16)
            sp.dma_start(par[:], params).then_inc(tables_landed, 16)
            for t in range(TT):
                sp.dma_start(xs[:, t], x[t * P:(t + 1) * P, :]).then_inc(x_landed[t], 16)
            w_rows = w_in.rearrange("(k p) n -> p k n", p=P)

            def load_group(g):
                if g >= W_SLOTS:
                    sp.wait_ge(w_done, wuse("in", g - W_SLOTS)[0] + 1)
                col = GROUPS[g][1]
                sp.dma_start(wring[:, g % W_SLOTS], w_rows[:, :, col:col + 256]).then_inc(
                    w_landed[g % W_SLOTS], 16)

            load_group(0)
            sp.dma_start(w_ba[:], w_rows[:, :, BA0:BA0 + 2 * HEADS]).then_inc(small_landed, 16)
            load_group(1)
            sp.dma_start(poolw[:], pool_w.rearrange("g c d -> c g d")).then_inc(small_landed, 16)
            sp.dma_start(wrt[:], w_router.rearrange("(k p) e -> p k e", p=P)).then_inc(small_landed, 16)
            for g in range(2, len(GROUPS)):
                load_group(g)
                if g == 6:
                    sp.dma_start(upb, w_up_b.rearrange("(k p) n -> p k n", p=P)).then_inc(upb_landed, 16)
                if g == 8:
                    sp.dma_start(upa, w_up_a.rearrange("(k p) n -> p k n", p=P)).then_inc(upa_landed, 16)
                if g in (9, 10):
                    a = (g - 9) * 4
                    sp.dma_start(wout[:, a:a + 4], w_out.rearrange("(k p) n -> p k n", p=P)[
                        :, a:a + 4, :]).then_inc(wout_landed, 16)

            def load_unit_gu(e, k):
                sp.dma_start(ring[:, k, :], w_gate_up[bass.ds(e, 1), k * P:(k + 1) * P, :].rearrange(
                    "a p n -> p (a n)")).then_inc(gu_landed[k], 16)

            def load_unit_wd(e, u):
                sp.dma_start(
                    ring[:, GU_UNITS + u, :].rearrange("p (k n) -> p k n", k=2),
                    w_down[bass.ds(e, 1), 2 * u * P:(2 * u + 2) * P, :].rearrange(
                        "a (k p) n -> p (a k) n", p=P)).then_inc(wd_landed[u], 16)

            def load_bias(e):
                sp.dma_start(b_gu, b_gate_up[bass.ds(e, 1), :]).then_inc(bias_landed, 16)

            sp.wait_ge(o_ready, HP)
            for k in range(GU_UNITS):
                load_unit_gu(0, k)
            sp.wait_ge(w_done, wuse("in", len(GROUPS) - 1)[0] + 1)
            load_bias(0)
            sp.dma_start(b_dn, b_down).then_inc(late_landed, 16)
            sp.dma_start(gfin, g_final.to_broadcast([P, D])).then_inc(late_landed, 16)
            sp.wait_ge(w_done, wuse("ua", 3)[0] + 1)
            for u in range(WD_UNITS):
                load_unit_wd(0, u)

            def load_expert(i, e):
                sp.wait_ge(bias_used, i)
                load_bias(e)
                for k in range(GU_UNITS):
                    sp.wait_ge(gu_used, GU_UNITS * (i - 1) + k + 1)
                    load_unit_gu(e, k)
                for u in range(WD_UNITS):
                    sp.wait_ge(wd_used, WD_UNITS * (i - 1) + u + 1)
                    load_unit_wd(e, u)

            with sp.Fori(1, E) as i:
                load_expert(i, i)
            sp.wait_ge(flag_ready, 1)
            over = sp.value_load(flag[0:1, 0:1], min_val=0, max_val=L)
            with sp.If(over > CAP):
                with sp.Fori(1, ROUNDS) as r:
                    with sp.Fori(0, E) as e:
                        load_expert(r * E + e, e)
                sp.nop()
            for t in range(TT):
                sp.wait_ge(fin_ready, t + 1)
                sp.dma_start(out[t * P:(t + 1) * P, :], xn2[:, t]).then_inc(out_landed, 16)
            sp.wait_ge(out_landed, 16 * TT)

        @block.tensor
        def _(pe):
            def bank_free(kind, i):
                n = wuse(kind, i)[0]
                if n >= 2:
                    k2, i2 = WUSE[n - 2]
                    pe.wait_ge(w_dve if k2 in W_ON_DVE else w_act, wuse(k2, i2)[1])
                return n % 2

            def project(g, b):
                bank = bank_free("in", g)
                if b == 0:
                    pe.wait_ge(w_landed[g % W_SLOTS], 16 * (g // W_SLOTS + 1))
                for k in range(KD):
                    mm = pe.matmul(ps[:, bank, b * L:(b + 1) * L],
                                   wring[:, g % W_SLOTS, k, b * P:(b + 1) * P], hT[:, k, :],
                                   start=k == 0, stop=k == KD - 1)
                if b == 1:
                    mm.then_inc(w_done, 1)

            def job(name, h):
                j = JOB[(name, h)]
                if j >= 3:
                    after_job(pe, JOBS[j - 3])
                banks = bank_q((name, h))
                level = name.lstrip("MTN")
                if name in ("WS", "O", "DS"):
                    n = h
                    if name == "WS":
                        pe.wait_ge(s_ready, n)
                    if name == "DS" or name == "O":
                        if n == 0:
                            after_job(pe, ("U", 0))
                            after_job(pe, ("U", 1))
                        else:
                            after_job(pe, ("WS", n))
                    if name == "O" and n == 0:
                        pe.wait_ge(qg_ready, 1)
                    vn = chunk(U, 0) if n == 0 else vnew
                    for hp in range(HP):
                        for q in range(2):
                            r = slice(q * C, (q + 1) * C)
                            o_ = banks[q][:, hp * C:(hp + 1) * C]
                            if name == "WS":
                                mm = pe.matmul(o_, chunk(WT, n)[r, hp], S[r, hp], start=True, stop=True)
                            elif name == "DS":
                                mm = pe.matmul(o_, chunk(kd, n)[r, hp], vn[r, hp], start=True, stop=True)
                            else:
                                if n:
                                    pe.matmul(o_, S[r, hp], chunk(egr, n)[r, hp], start=True, stop=False)
                                mm = pe.matmul(o_, vn[r, hp], chunk(qkT, n)[r, hp], start=n == 0, stop=True)
                    mm.then_inc(dn_pe, 1)
                    return
                if (name, h) == ("KT", 0):
                    pe.wait_ge(normed, HP)
                    pe.wait_ge(rows_diff, 1)
                    pe.wait_ge(rows_exp, 1)
                    pe.wait_ge(norm_sqrt, 2)
                if name == "VT":
                    pe.wait_ge(silu_ready, 6)
                if (name, h) == ("VT", 0):
                    pe.wait_ge(cols_ready, 1)
                if name == "KQ":
                    pe.wait_ge(normed, 2 * HP)
                if name == "AT":
                    after_job(pe, ("KK", h))
                if name[0] == "M":
                    pe.wait_ge(base_ready, 2 * (h + 1))
                    pe.wait_ge(lt_ready, 2 * LEVELS.index(int(level)) + h + 1)
                    if level != "2":
                        after_job(pe, (f"TN{int(level) // 2}", h))
                if name[0:2] in ("TN", "NT"):
                    after_job(pe, (f"M{level}", h))
                    if level != "2":
                        after_job(pe, (f"NT{int(level) // 2}", h))
                if name in ("WT", "U"):
                    after_job(pe, ("NT32", h))
                    pe.wait_ge(tok_scaled, 2 * (h + 1) if name == "WT" else 4 + h + 1)
                for s in range(HALF):
                    sl = h * HALF + s
                    hp, n = sl // NCH, sl % NCH
                    tok = slice(n * C, (n + 1) * C)
                    for q in range(2):
                        r = slice(q * C, (q + 1) * C)
                        lt = LT[LEVELS.index(int(level)) % 2] if name[0] == "M" else None
                        a, b = {
                            "KT": lambda: (kT[r, hp, tok], eye[r]), "VT": lambda: (vT[r, hp, tok], eye[r]),
                            "KK": lambda: (kT[r, hp, tok], kT[r, hp, tok]),
                            "KQ": lambda: (kT[r, hp, tok], qT[r, hp, tok]),
                            "AT": lambda: (A[r, sl], eye[r]), "M": lambda: (lt[r, sl], T[r, sl]),
                            "TN": lambda: (TTm[r, sl], N[r, sl]), "NT": lambda: (N[r, sl], TTm[r, sl]),
                            "WT": lambda: (Kb[r, sl], TTm[r, sl]), "U": lambda: (TTm[r, sl], vtok[r, sl]),
                        }[name.rstrip("0123456789")]()
                        mm = pe.matmul(banks[q][:, s * C:(s + 1) * C], a, b, start=True, stop=True)
                mm.then_inc(dn_pe, 1)

            pe.wait_ge(tables_landed, 32)
            for t in range(TT):
                pe.wait_ge(xn_ready, t + 1)
                for k in range(KD):
                    mm = pe.transpose(ps[:, 2 + 2 * t + k // 4, (k % 4) * P:(k % 4 + 1) * P],
                                      xn[:, t, k * P:(k + 1) * P], ident)
                    if k % 4 == 3:
                        mm.then_inc(xT_done, 1)
            pe.wait_ge(hT_ready, 4)

            def group(g):
                project(g, 0)
                project(g, 1)

            def sums_of_squares(i):
                pe.wait_ge(sq_ready, i + 1)
                if i:
                    pe.wait_ge(norm_sqrt, 1)
                for hp in range(HP):
                    mm = pe.matmul(ps[:, 2 + hp // 2, (hp % 2) * L:(hp % 2 + 1) * L], ones_blk,
                                   sq[:, hp], start=True, stop=True)
                mm.then_inc(sumsq_done, 1)

            group(0)
            pe.wait_ge(small_landed, 48)
            for t in range(TT):
                for k in range(KD):
                    mm = pe.matmul(ps[:, 6, t * 16:t * 16 + 16], hT[:, k, t * P:(t + 1) * P], w_ba[:, k],
                                   start=k == 0, stop=k == KD - 1)
            mm.then_inc(ba_done, 1)
            group(1)
            group(2)
            pe.wait_ge(g_ready, 1)
            pe.wait_ge(decay_act, 1)
            for t in range(TT):
                for r in range(2):
                    n = 2 * t + r
                    for q in range(2):
                        for i, (m, v) in enumerate(((tri, gtok), (ident, beta_t), (ones_blk, gtok))):
                            o_ = ps[q * C:(q + 1) * C, 6, 64 + 16 * i:80 + 16 * i].rearrange(
                                "p (hp n) -> p hp n", hp=HP)[:, :, n]
                            mm = pe.matmul(o_, m[:, r * C:(r + 1) * C],
                                           v[:, t].rearrange("p (hp q) -> p hp q", q=2)[:, :, q],
                                           start=True, stop=True)
            mm.then_inc(cols_done, 1)
            group(3)
            sums_of_squares(0)
            group(4)
            pe.wait_ge(g_ready, 2)
            for hp in range(HP):
                for t in range(TT):
                    for q in range(2):
                        mm = pe.matmul(ps[q * C:(q + 1) * C, 4 + hp // 2,
                                          (hp % 2) * L + t * P:(hp % 2) * L + (t + 1) * P],
                                       ones[:, 0:C], gtri[:, t, 2 * hp + q], start=True, stop=True)
            mm.then_inc(rows_done, 1)
            group(5)
            sums_of_squares(1)

            def up_project(kind, i, w, v):
                bank = bank_free(kind, i)
                for b in range(2):
                    m = 2 * i + b
                    for k in range(4):
                        mm = pe.matmul(ps[:, bank, b * L:(b + 1) * L], w[:, k, m * P:(m + 1) * P],
                                       v[:, k], start=k == 0, stop=k == 3)
                mm.then_inc(w_done, 1)

            for what, *which in ORDER:
                if what == "job":
                    job(*which)
                elif what == "in":
                    project(*which)
                elif what == "pool":
                    i = which[0]
                    bank = bank_free("pool", i)
                    pe.wait_ge(pooled_ready, 4)
                    for g in (2 * i, 2 * i + 1):
                        mm = pe.matmul(ps[:, bank, (g % 2) * L:(g % 2 + 1) * L], poolw[:, g],
                                       ub[:, 0, g, UPAD:], start=True, stop=True)
                    mm.then_inc(w_done, 1)
                elif what == "ub":
                    if which[0] == 0:
                        pe.wait_ge(upb_landed, 16)
                        pe.wait_ge(w_act, wuse("pool", 1)[1])
                    up_project("ub", which[0], upb, ub[:, 1, :, UPAD:])
                elif what == "osum":
                    pe.wait_ge(o_sq, 1)
                    for hp in range(HP):
                        mm = pe.matmul(ps[:, 2 + hp // 2, (hp % 2) * L:(hp % 2 + 1) * L], ones_blk,
                                       sq[:, hp], start=True, stop=True)
                    mm.then_inc(o_sumsq, 1)
            pe.wait_ge(upa_landed, 16)
            pe.wait_ge(o_ready, HP)
            for i in range(4):
                up_project("ua", i, upa, zT)
            pe.wait_ge(wout_landed, 32)
            for i in range(4):
                t, c = i // 2, i % 2
                bank = bank_free("wo", i)
                for k in range(KD):
                    pe.wait_ge(mix_ready, k // 2 + 1)
                    mm = pe.matmul(ps[:, bank, :], gates[:, 0, k, t * P:(t + 1) * P],
                                   wout[:, k, c * 512:(c + 1) * 512], start=k == 0, stop=k == KD - 1)
                mm.then_inc(w_done, 1)
            for t in range(TT):
                pe.wait_ge(xn2_ready, t + 1)
                for k in range(KD):
                    mm = pe.transpose(ps[:, 2 + 2 * t + k // 4, (k % 4) * P:(k % 4 + 1) * P],
                                      xn2[:, t, k * P:(k + 1) * P], ident)
                    if k % 4 == 3:
                        mm.then_inc(x2T_done, 1)
            for t in range(TT):
                pe.wait_ge(h2T_ready, 2 * t + 2)
                for k in range(KD):
                    mm = pe.matmul(ps[:, 6, t * E:(t + 1) * E], h2T[:, k, t * P:(t + 1) * P], wrt[:, k],
                                   start=k == 0, stop=k == KD - 1)
                mm.then_inc(logits_done, 1)
            mask = rt[:, 64:64 + TT * E].rearrange("p (t e) -> p t e", t=TT)
            pe.wait_ge(mask_ready, 1)
            pe.matmul(ps[:, 7, 0:E], cc("before"), mask[:, 0], start=True, stop=True)
            pe.matmul(ps[:, 7, E:2 * E], ones, mask[:, 0], start=True, stop=False)
            pe.matmul(ps[:, 7, E:2 * E], cc("before"), mask[:, 1], start=False, stop=True)
            pe.matmul(ps[0:1, 7, 64:64 + E], ones[:, 0:1], mask[:, 0], start=True, stop=False)
            pe.matmul(ps[0:1, 7, 64:64 + E], ones[:, 0:1], mask[:, 1], start=False, stop=True).then_inc(
                count_done, 1)
            pe.wait_ge(flag_ready, 1)
            for t in range(TT):
                mm = pe.transpose(ps[0:E, 6, 128 + t * P:128 + (t + 1) * P], comb[:, t, 0:E], ident)
            mm.then_inc(combT_done, 1)
            pe.wait_ge(combT_ready, 1)
            pe.wait_ge(late_landed, 32)

            def y(t, c):
                return ps[:, 4 + 2 * t + c, :]

            for t in range(TT):
                for c in range(2):
                    pe.matmul(y(t, c), combT[:, t * P:(t + 1) * P], b_dn[:, c * 512:(c + 1) * 512],
                              start=True, stop=False, skip_group_check=True)

            pe.wait_ge(zero_ready, 2)

            def gather(i):
                pe.wait_ge(sel_ready, i + 1)
                for k in range(KD):
                    for t in range(TT):
                        mm = pe.matmul(ps[:, 3, k * CAP:(k + 1) * CAP], xn2[:, t, k * P:(k + 1) * P],
                                       sel[:, t, :], start=t == 0, stop=t == TT - 1)
                mm.then_inc(gathered, 1)

            def scatter():
                for t in range(TT):
                    for c in range(2):
                        r = slice(c * CAP, (c + 1) * CAP)
                        mm = pe.matmul(y(t, c), ctS[r, t * P:(t + 1) * P], outS[r, :],
                                       start=False, stop=False, skip_group_check=True)
                mm.then_inc(scattered, 1)

            def expert(i):
                pe.wait_ge(xe_ready, i + 1)
                pe.wait_ge(bias_landed, 16 * (i + 1))
                for a in range(4):
                    r = slice((a % 2) * CAP, (a % 2 + 1) * CAP)
                    mm = pe.matmul(ps[r, a // 2, :], ones[0:1, 0:CAP], b_gu[:, a * 512:(a + 1) * 512],
                                   start=True, stop=False)
                mm.then_inc(bias_used, 1)
                for k in range(GU_UNITS):
                    pe.wait_ge(gu_landed[k], 16 * (i + 1))
                    for a in range(4):
                        r = slice((a % 2) * CAP, (a % 2 + 1) * CAP)
                        mm = pe.matmul(ps[r, a // 2, :], xe[:, k, :], ring[:, k, a * 512:(a + 1) * 512],
                                       start=False, stop=k == GU_UNITS - 1)
                    mm.then_inc(gu_used, 1)
                pe.wait_ge(selw_ready, i + 1)
                for t in range(TT):
                    mm = pe.transpose(ps[:, 2, t * P:(t + 1) * P], selw[:, t, :], ident)
                mm.then_inc(ct_done, 1)
                pe.wait_ge(out_copied, i + 1)
                scatter()
                gather(i + 1)
                pe.wait_ge(ct_copied, i + 1)
                pe.wait_ge(act_ready, i + 1)
                for j in range(4):
                    mm = pe.transpose(ps[:, 2, j * P:(j + 1) * P], act_a[:, j * P:(j + 1) * P], ident)
                mm.then_inc(actT_done, 1)
                pe.wait_ge(actT_copied, i + 1)
                pe.wait_ge(xe_ready, i + 2)
                for k in range(KD):
                    if k % 2 == 0:
                        pe.wait_ge(wd_landed[k // 2], 16 * (i + 1))
                    half, j = k // 4, k % 4
                    lhs = actT[:, j * P + half * CAP:j * P + (half + 1) * CAP]
                    for c in range(2):
                        w = ring[:, GU_UNITS + k // 2, (k % 2) * D + c * 512:(k % 2) * D + (c + 1) * 512]
                        mm = pe.matmul(ps[c * CAP:(c + 1) * CAP, 3, :], lhs, w, start=k == 0, stop=k == KD - 1)
                    if k % 2 == 1:
                        mm.then_inc(wd_used, 1)

            gather(0)
            with pe.Fori(0, E) as i:
                expert(i)
            pe.wait_ge(flag_ready, 1)
            over = pe.value_load(flag[0:1, 0:1], min_val=0, max_val=L)
            with pe.If(over > CAP):
                with pe.Fori(E, ROUNDS * E) as i:
                    expert(i)
                pe.wait_ge(out_copied, ROUNDS * E + 1)
            pe.wait_ge(out_copied, E + 1)
            scatter()

        @block.vector
        def _(dve):
            steps = [0]

            def step(ins):
                steps[0] += 1
                ins.then_inc(dve_step, 1)
                dve.wait_ge(dve_step, steps[0])

            def add_scaled(o_, a, s, b, o0=ALU.mult, o1=ALU.add):
                return dve.scalar_tensor_tensor(out=o_, in0=a, scalar=s, in1=b, op0=o0, op1=o1)

            dve.memset(eps_c, EPS).then_inc(zero_ready, 1)
            junk = zT.rearrange("p b n -> p (b n)")
            for t in range(TT):
                dve.wait_ge(x_landed[t], 16)
                step(dve.tensor_tensor_reduce(out=junk, in0=xs[:, t], in1=xs[:, t], scale=1.0, scalar=0.0,
                                              op0=ALU.mult, op1=ALU.add, accum_out=ssx[:, t:t + 1]))
            dve.tensor_scalar(ssx, ssx, 1.0 / D, EPS, ALU.mult, ALU.add).then_inc(ss_ready, 1)
            dve.wait_ge(var_sqrt, 1)
            step(dve.reciprocal(rstd, rstd))
            for t in range(TT):
                dve.tensor_scalar(xn[:, t], xs[:, t], rstd[:, t:t + 1], None, ALU.mult).then_inc(xn_ready, 1)
            dve.wait_ge(tables_landed, 32)
            for t in range(TT):
                for h in range(2):
                    dve.wait_ge(xT_done, 2 * t + h + 1)
                    dve.tensor_tensor(
                        hT[:, 4 * h:4 * h + 4, t * P:(t + 1) * P],
                        ps[:, 2 + 2 * t + h, :].rearrange("p (k n) -> p k n", k=4),
                        bc(pp("gmix")[:, 4 * h:4 * h + 4], P), ALU.mult).then_inc(hT_ready, 1)

            conv = pp("conv").rearrange("p (b j) -> p b j", b=12)

            def convolve(g):
                dve.wait_ge(w_act, g + 1)
                if g == 0:
                    dve.wait_ge(pads_zeroed, 1)
                for b in (2 * g, 2 * g + 1):
                    step(dve.tensor_scalar(cq[:, b], cpad[:, b, 1:1 + L], conv[:, b, 0:1], None, ALU.mult))
                    for j in range(1, TAPS):
                        ins = add_scaled(cq[:, b], cpad[:, b, 1 + j:1 + j + L], conv[:, b, j:j + 1], cq[:, b])
                        if j < TAPS - 1:
                            step(ins)
                    ins.then_inc(conv_ready, 1)

            def silu(g):
                dve.wait_ge(sig_ready, g + 1)
                dve.tensor_tensor(cq[:, 2 * g:2 * g + 2], cq[:, 2 * g:2 * g + 2], sg, ALU.mult).then_inc(
                    silu_ready, 1)

            def normalise(i):
                dve.wait_ge(norm_sqrt, i + 1)
                step(dve.reciprocal(sq, sq))
                for hp in range(HP):
                    v = (kT, qT)[i][:, hp]
                    add_scaled(v, v, (1.0, HD ** -0.5)[i], sq[:, hp], ALU.mult, ALU.mult).then_inc(normed, 1)

            convolve(0)
            dve.wait_ge(ba_done, 1)
            bav = ps[:, 6, 0:32].rearrange("p (t n) -> p t n", t=TT)
            step(dve.tensor_tensor(av, bav[:, :, HEADS:], rep(pp("dtb"), TT), ALU.add))
            add_scaled(ab, av, -1.0, av, ALU.mult, ALU.max).then_inc(ba_read, 1)
            convolve(1)
            silu(0)
            silu(1)
            dve.wait_ge(sp_exp, 1)
            step(add_scaled(sp_, av, 0.0, ab, ALU.max, ALU.add))
            add_scaled(gtok, sp_, -1.0, rep(ea, TT), ALU.mult, ALU.mult).then_inc(g_ready, 1)
            dve.wait_ge(g_ready, 1)
            for t in range(TT):
                ins = dve.tensor_tensor(gtri[:, t], rep(tri, HEADS), bc(gtok[:, t], P), ALU.mult)
            ins.then_inc(g_ready, 1)
            convolve(2)
            dve.wait_ge(cols_done, 1)
            dve.tensor_copy(sm[:, 112:160], ps[:, 6, 64:112]).then_inc(cols_ready, 1)
            dve.wait_ge(cols_ready, 1)
            dve.tensor_tensor(kdf, colL, colG, ALU.subtract).then_inc(cols_ready, 1)
            silu(2)
            convolve(3)
            silu(3)
            dve.wait_ge(cols_exp, 1)
            dve.tensor_tensor(bEG, colB, eG, ALU.mult).then_inc(cols_all, 1)
            normalise(0)
            convolve(4)
            dve.wait_ge(rows_done, 1)
            diff = Kb
            step(dve.tensor_tensor(diff, flat_banks(4, C),
                                   bc(colG, C), ALU.subtract))
            dve.tensor_scalar(F2, diff, 0.0, None, ALU.min).then_inc(rows_diff, 1)
            dve.tensor_scalar(F1, diff, 0.0, None, ALU.max).then_inc(rows_diff, 1)
            silu(4)
            convolve(5)
            silu(5)
            normalise(1)
            dve.wait_ge(rows_exp, 1)
            dve.wait_ge(normed, 2 * HP)
            dve.tensor_tensor(egr, egr, qT.rearrange("p b (n c) -> p (b n) c", c=C), ALU.mult).then_inc(qg_ready, 1)

            dest = {"KT": ktok, "VT": vtok, "AT": AT, "TN": T, "NT": TTm, "WT": WT, "U": U}

            def empty(name, h):
                banks = bank_q((name, h))
                kind = name.rstrip("0123456789")
                dve.wait_ge(dn_pe, JOB[(name, h)] + 1)
                if kind == "WT" and h == 0:
                    dve.wait_ge(lt_ready, 2 * len(LEVELS))
                if kind in dest:
                    ins = dve.tensor_copy(dest[kind][0:C, h * HALF:(h + 1) * HALF],
                                          banks[0].rearrange("p (s n) -> p s n", n=C))
                elif kind == "O":
                    ins = dve.tensor_copy(oT[0:C, :, h * C:(h + 1) * C],
                                          banks[0][:, 0:HP * C].rearrange("p (s n) -> p s n", n=C))
                elif kind in ("WS", "DS"):
                    for q in range(2):
                        r = slice(q * C, (q + 1) * C)
                        v = banks[q][:, 0:HP * C].rearrange("p (s n) -> p s n", n=C)
                        if kind == "WS":
                            ins = dve.tensor_tensor(vnew[r], chunk(U, h)[r], v, ALU.subtract)
                        elif h == 0:
                            ins = dve.tensor_copy(S[r], v)
                        else:
                            ins = dve.tensor_tensor(S[r], Sg[r], v, ALU.add)
                    if kind == "DS":
                        ins.then_inc(s_ready, 1)
                        dve.wait_ge(s_ready, h + 1)
                        ins = dve.tensor_tensor(Sg, S, bc(egl.rearrange("p (hp n) -> p hp n", hp=HP)[
                            :, :, h + 1], C), ALU.mult)
                else:
                    for q in range(2):
                        r = slice(q * C, (q + 1) * C)
                        sl = slice(h * HALF, (h + 1) * HALF)
                        v = banks[q].rearrange("p (s n) -> p s n", n=C)
                        if kind == "M":
                            ins = add_scaled(N[r, sl], v, -1.0, rep(eye[r], HALF))
                        else:
                            ins = dve.tensor_tensor((A if kind == "KK" else qkT)[r, sl], v,
                                                    (F1 if kind == "KK" else F2)[r, sl], ALU.mult)
                ins.then_inc(dn_dve, 1)

            def gated(kind, i):
                n, count = wuse(kind, i)
                dve.wait_ge(w_done, n + 1)
                side = 1 if kind == "ub" else 0
                if i == 0 and kind == "ub":
                    dve.wait_ge(w_act, wuse("in", 13)[1])
                if i == 0 and kind == "ua":
                    dve.wait_ge(w_act, wuse("in", 17)[1])
                v = gates[:, side, 2 * i:2 * i + 2]
                dve.tensor_tensor(v, v, ps[:, n % 2, :].rearrange("p (b n) -> p b n", b=2),
                                  ALU.mult).then_inc(w_dve, 1)

            dve.wait_ge(f_ready, 2)
            for what, *which in ORDER:
                if what == "job":
                    empty(*which)
                elif what == "ub":
                    gated("ub", which[0])
                elif (what, *which) == ("in", 11, 1):
                    dve.wait_ge(w_act, wuse("in", 9)[1])
                    dve.tensor_tensor(zT[:], zT[:], zsig, ALU.mult).then_inc(z_ready, 1)
                elif what == "onorm":
                    dve.wait_ge(o_sqrt, 1)
                    step(dve.reciprocal(sq, sq))
                    dve.wait_ge(z_ready, 1)
                    for hp in range(HP):
                        step(add_scaled(zT[:, hp], zT[:, hp], pp("dn"), sq[:, hp], ALU.mult, ALU.mult))
                        dve.tensor_tensor(zT[:, hp], oT[:, hp], zT[:, hp], ALU.mult).then_inc(o_ready, 1)
            for i in range(4):
                gated("ua", i)
                dve.wait_ge(w_dve, wuse("ua", i)[1])
                dve.tensor_tensor(gates[:, 0, 2 * i:2 * i + 2], gates[:, 0, 2 * i:2 * i + 2],
                                  gates[:, 1, 2 * i:2 * i + 2], ALU.add).then_inc(mix_ready, 1)
            for i in range(4):
                t, c = i // 2, i % 2
                n, count = wuse("wo", i)
                dve.wait_ge(w_done, n + 1)
                v = xs[:, t, c * 512:(c + 1) * 512]
                dve.tensor_tensor(v, v, ps[:, n % 2, :], ALU.add).then_inc(w_dve, 1)
                if c == 1:
                    dve.wait_ge(w_dve, count)
                    step(dve.tensor_tensor_reduce(out=junk, in0=xs[:, t], in1=xs[:, t], scale=1.0, scalar=0.0,
                                                  op0=ALU.mult, op1=ALU.add, accum_out=ssx[:, t:t + 1]))
            dve.tensor_scalar(ssx, ssx, 1.0 / D, EPS, ALU.mult, ALU.add).then_inc(ss_ready, 1)
            dve.wait_ge(var_sqrt, 2)
            step(dve.reciprocal(rstd, rstd))
            for t in range(TT):
                dve.tensor_scalar(xn2[:, t], xs[:, t], rstd[:, t:t + 1], None, ALU.mult).then_inc(xn2_ready, 1)
            for t in range(TT):
                for h in range(2):
                    dve.wait_ge(x2T_done, 2 * t + h + 1)
                    dve.tensor_tensor(
                        h2T[:, 4 * h:4 * h + 4, t * P:(t + 1) * P],
                        ps[:, 2 + 2 * t + h, :].rearrange("p (k n) -> p k n", k=4),
                        bc(pp("gffn")[:, 4 * h:4 * h + 4], P), ALU.mult).then_inc(h2T_ready, 1)
            logit = rt[:, 512:512 + TT * (E + 4)].rearrange("p (t e) -> p t e", t=TT)
            mask = rt[:, 64:128].rearrange("p (t e) -> p t e", t=TT)
            left = rt[:, 640:640 + TT * (E + 4)].rearrange("p (t e) -> p t e", t=TT)
            top = rt[:, 192:208].rearrange("p (t e) -> p t e", t=TT)
            soft = rt[:, 224:288].rearrange("p (t e) -> p t e", t=TT)
            den = rt[:, 288:290]
            where = rt[:, 320:384].rearrange("p (t e) -> p t e", t=TT)
            dve.memset(rt[:, 480:488], MARK)
            dve.memset(pos[:, :, NPOS - 1:NPOS], -1.0)
            dve.memset(comb[:, :, NPOS - 1:NPOS], 0.0)
            dve.memset(outS, 0.0).then_inc(out_copied, 1)
            dve.memset(ctS, 0.0).then_inc(zero_ready, 1)
            for t in range(TT):
                dve.wait_ge(logits_done, TT)
                step(dve.tensor_tensor(logit[:, t, 0:E], ps[:, 6, t * E:(t + 1) * E], pp("brouter"), ALU.add))
                step(dve.tensor_copy(logit[:, t, E:E + 4], rt[:, 480:484]))
                step(dve.max(out=top[:, t], in_=logit[:, t, 0:E]))
                dve.tensor_scalar(soft[:, t], logit[:, t, 0:E], top[:, t, 0:1], None, ALU.subtract).then_inc(soft_in, 1)
                step(dve.tensor_copy(top[:, t, TOP_K:8], rt[:, 484:488]))
                step(dve.match_replace(out=left[:, t], in_to_replace=top[:, t], in_values=logit[:, t],
                                       imm_value=GONE))
                ins = dve.tensor_tensor(mask[:, t], logit[:, t, 0:E], left[:, t, 0:E], ALU.is_gt)
            ins.then_inc(mask_ready, 1)
            dve.wait_ge(mask_ready, 1)
            dve.wait_ge(soft_exp, 1)
            step(dve.tensor_tensor(soft, soft, mask, ALU.mult))
            step(dve.tensor_reduce(den, soft, AX.X, ALU.add))
            step(dve.reciprocal(den, den))
            for t in range(TT):
                step(dve.tensor_scalar(comb[:, t, 0:ROUNDS * E].rearrange("p (r e) -> p r e", r=ROUNDS),
                                       rep(soft[:, t], ROUNDS), den[:, t:t + 1], None, ALU.mult))
            dve.wait_ge(count_done, 1)
            step(add_scaled(where, ps[:, 7, 0:TT * E].rearrange("p (t e) -> p t e", t=TT), 1.0, mask,
                            ALU.add, ALU.mult))
            for r in range(ROUNDS):
                step(dve.tensor_scalar(pos[:, :, r * E:(r + 1) * E], where, -1.0 - r * CAP, None, ALU.add))
            step(dve.tensor_reduce(rt[0:1, 490:491], ps[0:1, 7, 64:64 + E], AX.X, ALU.max))
            dve.tensor_copy(flag[0:1, 0:1], rt[0:1, 490:491]).then_inc(flag_ready, 1)

            def build_sel(i):
                for t in range(TT):
                    ins = dve.tensor_scalar(sel[:, t], cc("iota")[:, 0:CAP], pos[:, t, bass.ds(i, 1)], None,
                                            ALU.is_equal)
                ins.then_inc(sel_ready, 1)

            def build_selw(i):
                for t in range(TT):
                    ins = dve.tensor_scalar(selw[:, t], cc("iota"), pos[:, t, bass.ds(i, 1)],
                                            comb[:, t, bass.ds(i, 1)], ALU.is_equal, ALU.mult)
                ins.then_inc(selw_ready, 1)

            def empty_gather(i):
                dve.wait_ge(gathered, i + 1)
                dve.tensor_tensor(xe, ps[:, 3, :].rearrange("p (k n) -> p k n", k=KD), bc(pp("gffn"), CAP),
                                  ALU.mult).then_inc(xe_ready, 1)

            def expert(i):
                dve.wait_ge(gathered, i + 1)
                build_sel(i + 1)
                dve.wait_ge(gu_used, GU_UNITS * (i + 1))
                dve.tensor_scalar(gmin, ps[:, 0, :], LIMIT, None, ALU.min).then_inc(gmin_ready, 1)
                dve.tensor_scalar(act_t, ps[:, 1, :], LIMIT, -LIMIT, ALU.min, ALU.max).then_inc(gu_read, 1)
                dve.wait_ge(gu_read, i + 1)
                add_scaled(act_t, act_t, 1.0, gmin, ALU.add, ALU.mult).then_inc(up_ready, 1)
                dve.wait_ge(up_ready, i + 1)
                dve.wait_ge(gate_sig, i + 1)
                dve.tensor_tensor(act_a, act_t, sig, ALU.mult).then_inc(act_ready, 1)
                dve.wait_ge(ct_done, i + 1)
                build_selw(i + 1)
                empty_gather(i + 1)

            dve.wait_ge(flag_ready, 1)
            dve.wait_ge(combT_done, 1)
            build_sel(0)
            build_selw(0)
            empty_gather(0)
            with dve.Fori(0, E) as i:
                expert(i)
            over = dve.value_load(flag[0:1, 0:1], min_val=0, max_val=L)
            with dve.If(over > CAP):
                with dve.Fori(E, ROUNDS * E) as i:
                    expert(i)
                dve.wait_ge(scattered, ROUNDS * E + 1)
            dve.wait_ge(scattered, E + 1)
            for t in range(TT):
                v = xs[:, t].rearrange("p (c n) -> p c n", c=2)
                dve.tensor_tensor(v, v, ps[:, 4 + 2 * t:6 + 2 * t, :], ALU.add).then_inc(y_ready, 1)
                dve.wait_ge(y_ready, t + 1)
                dve.tensor_tensor_reduce(out=junk, in0=xs[:, t], in1=xs[:, t], scale=1.0, scalar=0.0,
                                         op0=ALU.mult, op1=ALU.add,
                                         accum_out=ssx[:, t:t + 1]).then_inc(ssf_ready, 1)
                dve.wait_ge(f_sqrt, t + 1)
                dve.reciprocal(rstd[:, t:t + 1], rstd[:, t:t + 1]).then_inc(rstd_ready, 1)
                dve.wait_ge(rstd_ready, t + 1)
                add_scaled(xn2[:, t], xs[:, t], rstd[:, t:t + 1], gfin, ALU.mult, ALU.mult).then_inc(fin_ready, 1)

        @block.scalar
        def _(act):
            fn = act.activation

            def copy(o_, i_):
                return act.copy(o_, i_)

            act.wait_ge(zero_ready, 1)
            act.wait_ge(ss_ready, 1)
            fn(rstd, ssx, ACT.Sqrt).then_inc(var_sqrt, 1)

            def to_conv(g):
                act.wait_ge(w_done, g + 1)
                copy(cpad[:, 2 * g:2 * g + 2, 4:], ps[:, g % 2, :].rearrange("p (b n) -> p b n", b=2)).then_inc(
                    w_act, 1)

            def sigmoid(g):
                act.wait_ge(conv_ready, 2 * g + 2)
                act.wait_ge(silu_ready, g)
                fn(sg, cq[:, 2 * g:2 * g + 2], ACT.Sigmoid).then_inc(sig_ready, 1)

            def square(i):
                act.wait_ge(silu_ready, 2 * i + 2)
                act.wait_ge(normed, HP * i)
                fn(sq, (kT, qT)[i], ACT.Square).then_inc(sq_ready, 1)

            def norm_root(done, count, ready, scale=1.0):
                act.wait_ge(done, count)
                fn(sq, flat_banks(2, L), ACT.Sqrt, bias=eps_c,
                   scale=scale).then_inc(ready, 1)

            to_conv(0)
            act.wait_ge(ba_read, 1)
            act.wait_ge(tables_landed, 32)
            fn(ab, ab, ACT.Exp, scale=-1.0).then_inc(act_step, 1)
            fn(ea, pp("alog"), ACT.Exp)
            act.wait_ge(act_step, 1)
            fn(ab, ab, ACT.Ln, bias=1.0).then_inc(sp_exp, 1)
            fn(beta_t, ps[:, 6, 0:32].rearrange("p (t n) -> p t n", t=TT)[:, :, 0:HEADS],
               ACT.Sigmoid).then_inc(decay_act, 1)
            to_conv(1)
            sigmoid(0)
            sigmoid(1)
            square(0)
            to_conv(2)
            act.wait_ge(cols_ready, 2)
            fn(eG, colG, ACT.Exp)
            fn(kdf, kdf, ACT.Exp)
            fn(egl, colL, ACT.Exp).then_inc(cols_exp, 1)
            sigmoid(2)
            to_conv(3)
            sigmoid(3)
            norm_root(sumsq_done, 1, norm_sqrt)
            square(1)
            to_conv(4)
            act.wait_ge(rows_diff, 1)
            fn(egr, flat_banks(4, C), ACT.Exp).then_inc(rows_exp, 1)
            fn(F2, F2, ACT.Exp).then_inc(f_exp, 1)
            act.wait_ge(rows_diff, 2)
            fn(F1, F1, ACT.Exp, scale=-1.0).then_inc(f_exp, 1)
            sigmoid(4)
            to_conv(5)
            sigmoid(5)
            norm_root(sumsq_done, 2, norm_sqrt)

            dest = {"KT": ktok, "VT": vtok, "AT": AT, "TN": T, "NT": TTm, "WT": WT, "U": U}
            for what, *which in ORDER:
                if what == "job" and on_act(tuple(which)):
                    name, h = which
                    act.wait_ge(dn_pe, JOB[(name, h)] + 1)
                    kind = name.rstrip("0123456789")
                    if kind == "WT" and h == 0:
                        act.wait_ge(lt_ready, 2 * len(LEVELS))
                    bank = bank_q((name, h))[1]
                    if kind == "O":
                        ins = copy(oT[C:P, :, h * C:(h + 1) * C],
                                   bank[:, 0:HP * C].rearrange("p (s n) -> p s n", n=C))
                    else:
                        ins = copy(dest[kind][C:P, h * HALF:(h + 1) * HALF],
                                   bank.rearrange("p (s n) -> p s n", n=C))
                    ins.then_inc(dn_act, 1)
                elif what == "in" and which[1] == 1:
                    g = which[0]
                    kind = GROUPS[g][0]
                    n = wuse("in", g)[0]
                    act.wait_ge(w_done, n + 1)
                    v = ps[:, n % 2, :].rearrange("p (b n) -> p b n", b=2)
                    at = 2 * sum(k == kind for k, _ in GROUPS[:g])
                    if kind == "u":
                        ins = copy(ub[:, 0, at:at + 2, UPAD:], v)
                    elif kind == "z":
                        copy(zT[:, at:at + 2], v)
                        after_job(act, ("KK", 1))
                        ins = fn(zsig[:, at:at + 2], v, ACT.Sigmoid)
                    else:
                        if kind == "ga" and at == 0:
                            act.wait_ge(dn_pe, JOB[("M32", 1)] + 1)
                        ins = fn(gates[:, 1 if kind == "gb" else 0, at:at + 2], v, ACT.Sigmoid)
                    ins.then_inc(w_act, 1)
                elif what == "pool":
                    i = which[0]
                    n = wuse("pool", i)[0]
                    act.wait_ge(w_done, n + 1)
                    if i == 0:
                        act.wait_ge(pooled_ready, 4)
                    for b in range(2):
                        g = 2 * i + b
                        ins = fn(ub[:, 1, g, UPAD:], ps[:, n % 2, b * L:(b + 1) * L], ACT.Copy,
                                 scale=pp("pscale")[:, g:g + 1])
                    ins.then_inc(w_act, 1)
                elif what == "osquare":
                    act.wait_ge(dn_dve, len(JOBS))
                    act.wait_ge(dn_act, act_number(("O", NCH - 1)))
                    fn(sq, oT, ACT.Square).then_inc(o_sq, 1)
                elif what == "osum":
                    norm_root(o_sumsq, 1, o_sqrt, 1.0 / HD)
            act.wait_ge(ss_ready, 2)
            fn(rstd, ssx, ACT.Sqrt).then_inc(var_sqrt, 1)
            soft = rt[:, 224:288].rearrange("p (t e) -> p t e", t=TT)
            act.wait_ge(soft_in, TT)
            fn(soft, soft, ACT.Exp).then_inc(soft_exp, 1)
            act.wait_ge(combT_done, 1)
            copy(combT, ps[0:E, 6, 128:128 + L]).then_inc(combT_ready, 1)

            def expert(i):
                act.wait_ge(gmin_ready, i + 1)
                fn(sig, gmin, ACT.Sigmoid, scale=ALPHA).then_inc(gate_sig, 1)
                act.wait_ge(ct_done, i + 1)
                act.wait_ge(scattered, i + 1)
                copy(ctS, ps[:, 2, 0:L]).then_inc(ct_copied, 1)
                act.wait_ge(actT_done, i + 1)
                copy(actT, ps[:, 2, :]).then_inc(actT_copied, 1)
                act.wait_ge(wd_used, WD_UNITS * (i + 1))
                copy(outS, ps[:, 3, :]).then_inc(out_copied, 1)

            with act.Fori(0, E) as i:
                expert(i)
            act.wait_ge(flag_ready, 1)
            over = act.value_load(flag[0:1, 0:1], min_val=0, max_val=L)
            with act.If(over > CAP):
                with act.Fori(E, ROUNDS * E) as i:
                    expert(i)
                act.nop()
            for t in range(TT):
                act.wait_ge(ssf_ready, t + 1)
                fn(rstd[:, t:t + 1], ssx[:, t:t + 1], ACT.Sqrt, bias=eps_c, scale=1.0 / D).then_inc(f_sqrt, 1)

        @block.gpsimd
        def _(pool):
            steps = [0]

            def step(ins):
                steps[0] += 1
                ins.then_inc(pool_step, 1)
                pool.wait_ge(pool_step, steps[0])

            tt = pool.tensor_tensor
            pool.memset(cpad[:, :, 0:4], 0.0).then_inc(pads_zeroed, 1)
            pool.wait_ge(tables_landed, 32)
            pool.wait_ge(f_exp, 1)
            tt(F2, F2, rep(cc("upper"), SLOTS), ALU.mult).then_inc(f_ready, 1)
            pool.wait_ge(f_exp, 2)
            step(tt(F1, F1, rep(cc("lower"), SLOTS), ALU.mult))
            tt(F1, F1, bc(colB, C), ALU.mult).then_inc(f_ready, 1)
            step(pool.memset(ub[:, :, :, 0:UPAD], 0.0))
            pool.wait_ge(cols_all, 1)
            for h in range(2):
                after_job(pool, ("KT", h))
                tt(hslots(Kb, h), hslots(ktok, h), bc(bEG[:, h * HALF:(h + 1) * HALF], C), ALU.mult).then_inc(
                    tok_scaled, 1)
                tt(hslots(kd, h), hslots(ktok, h), bc(kdf[:, h * HALF:(h + 1) * HALF], C), ALU.mult).then_inc(
                    tok_scaled, 1)
            for h in range(2):
                after_job(pool, ("VT", h))
                tt(hslots(vtok, h), hslots(vtok, h), bc(colB[:, h * HALF:(h + 1) * HALF], C), ALU.mult).then_inc(
                    tok_scaled, 1)
            for h in range(2):
                for src, jobname, m, o_ in ((A, "KK", "m1", T), (AT, "AT", "m1t", TTm)):
                    after_job(pool, (jobname, h))
                    step(tt(hslots(o_, h), hslots(src, h), rep(cc(m), HALF), ALU.mult))
                    tt(hslots(o_, h), rep(eye, HALF), hslots(o_, h), ALU.subtract).then_inc(base_ready, 1)
            for n, b in enumerate(LEVELS):
                for h in range(2):
                    if n >= 2:
                        pool.wait_ge(dn_pe, JOB[(f"M{LEVELS[n - 2]}", h)] + 1)
                    tt(hslots(LT[n % 2], h), hslots(AT, h), rep(cc(f"lt{b}"), HALF), ALU.mult).then_inc(lt_ready, 1)
                if n != 1:
                    continue
                pool.wait_ge(w_act, wuse("in", 7)[1])
                after_job(pool, ("KQ", 1))
                u, s2, W = ub[:, 0], ub[:, 1], UPAD + L
                step(tt(s2[:, :, 1:], u[:, :, 1:], u[:, :, :W - 1], ALU.add))
                step(tt(usum[:, :, 3:], s2[:, 1:, 3:], s2[:, 1:, 1:W - 2], ALU.add))
                step(tt(s2[:, 2:, 7:], usum[:, 1:, 7:], usum[:, 1:, 3:W - 4], ALU.add))
                step(tt(usum[:, 2:, 15:], s2[:, 3:, 15:], s2[:, 3:, 7:W - 8], ALU.add))
                inv = cc("inv").rearrange("p (g n) -> p g n", g=4)
                for g in range(4):
                    s_ = (s2[:, 0], usum[:, 0], s2[:, 2], usum[:, 2])[g]
                    step(tt(s_[:, UPAD:2 * UPAD], s_[:, UPAD:2 * UPAD], inv[:, g], ALU.mult))
                    step(pool.tensor_scalar(s_[:, 2 * UPAD:], s_[:, 2 * UPAD:], 1.0 / POOLS[g], None, ALU.mult))
                    tt(u[:, g, UPAD:], s_[:, UPAD:], u[:, g, UPAD:], ALU.subtract).then_inc(pooled_ready, 1)


INPUTS = ("x", "consts", "params", "w_in", "pool_w", "w_up_a", "w_up_b", "w_out", "w_router",
          "w_gate_up", "b_gate_up", "w_down", "b_down", "g_final")


def kernel(**inputs):
    import concourse.bacc as bacc
    from concourse.bass_utils import run_bass_kernel_spmd

    a = {k: np.asarray(v) for k, v in inputs.items()}

    def rows(v):
        return np.broadcast_to(v.reshape(1, -1), (P, v.size))

    conv = a["conv_w"][0].T.reshape(3, HP, P, TAPS)[[1, 0, 2]].reshape(12, P, TAPS)
    parts = {
        "conv": conv.transpose(1, 0, 2).reshape(P, -1),
        "dn": np.concatenate([a["dn_norm"][0]] * 2)[:, None],
        "pscale": a["pool_scale"][0].reshape(4, P).T,
        "alog": rows(a["a_log"][0]), "dtb": rows(a["dt_bias"][0]), "brouter": rows(a["b_router"][0]),
        "gmix": a["g_mix"][0].reshape(KD, P).T, "gffn": a["g_ffn"][0].reshape(KD, P).T,
    }
    arrays = {
        "x": a["x"][0], "consts": const_table(),
        "params": np.concatenate([parts[k] for k in PARAMS], axis=1), "g_final": a["g_final"][None, :],
    }
    for name in INPUTS:
        if name not in arrays:
            arrays[name] = a[name][0]
    nc = bacc.Bacc("TRN2", target_bir_lowering=False, num_devices=1)
    launch, args = {}, []
    for name in INPUTS:
        v = np.ascontiguousarray(arrays[name])
        launch[f"in_{name}"] = v
        args.append(nc.dram_tensor(f"in_{name}", v.shape, mybir.dt.from_np(v.dtype), kind="ExternalInput").ap())
    out = nc.dram_tensor("out", (L, D), F32, kind="ExternalOutput").ap()
    build_program(nc, *args, out)
    r = run_bass_kernel_spmd(nc, [launch], core_ids=[0])
    return r.results[0]["out"].reshape(1, L, D)
```

```python
from contextlib import ExitStack

import concourse.bass as bass
import numpy as np
from concourse import mybir

F32 = mybir.dt.float32
I32 = mybir.dt.int32
ALU = mybir.AluOpType
ACT = mybir.ActivationFunctionType
AX = mybir.AxisListType

P = 128
D = 1024
L = 256
TT = L // P
KD = D // P
HEADS, HD = 8, 64
HP = HEADS // 2
C = 64
NCH = L // C
SLOTS = HP * NCH
HALF = SLOTS // 2
DN = HEADS * HD
TAPS = 4
POOLS = (2, 4, 8, 16)
UPAD = 16
E = 32
TOP_K = 4
F = D
LIMIT, ALPHA = 7.0, 1.702
EPS = 1e-6
CAP = 64
ROUNDS = L // CAP
UNIT = 2 * D
GU_UNITS = KD
WD_UNITS = F // P // 2
LEVELS = (2, 4, 8, 16, 32)

CONSTS, _at = {}, 0
for _n, _w in (("ident", P), ("tri", P), ("ones_blk", P), ("ones", P), ("before", P), ("iota", P),
               ("eye", C), ("lower", C), ("upper", C), ("m1", C), ("m1t", C),
               ("lt2", C), ("lt4", C), ("lt8", C), ("lt16", C), ("lt32", C), ("inv", 4 * UPAD),
               ("head_sum", HP * HEADS), ("head_row", HP * P)):
    CONSTS[_n] = (_at, _w)
    _at += _w
NCONST = _at
PARAMS, _at = {}, 0
for _n, _w in (("conv", 12 * TAPS), ("dn", 1), ("pscale", 4), ("alog", HEADS), ("dtb", HEADS),
               ("brouter", E), ("gmix", KD), ("gffn", KD)):
    PARAMS[_n] = (_at, _w)
    _at += _w
NPARAM = _at
MARK, GONE = -3.2e38, -3.3e38


def const_table():
    t = np.zeros((P, NCONST), np.float32)
    p = np.arange(P)[:, None]
    j = np.arange(P)[None, :]
    e = np.arange(C)[None, :]
    r, c = p // C, p % C

    def put(name, value):
        a, w = CONSTS[name]
        t[:, a:a + w] = value

    put("ident", p == j)
    put("tri", (r == j // C) & (c <= j % C))
    put("ones_blk", r == j // C)
    put("ones", 1.0)
    put("before", p < j)
    put("iota", np.broadcast_to(j % CAP, (P, P)))
    put("eye", c == e)
    put("lower", e < c)
    put("upper", e >= c)
    put("m1", (c % 2 == 1) & (e == c - 1))
    put("m1t", (e % 2 == 1) & (c == e - 1))
    for b in LEVELS:
        put(f"lt{b}", ((e // b) % 2 == 1) & (c // b == e // b - 1))
    for hp in range(HP):
        a, at = CONSTS["head_sum"][0] + hp * HEADS, CONSTS["head_row"][0] + hp * P
        t[:, a:a + HEADS] = np.arange(HEADS)[None, :] == 2 * hp + r
        t[:, at:at + P] = p == 2 * hp + j // C
    tok = np.arange(UPAD)
    put("inv", np.concatenate([1.0 / np.minimum(tok + 1, w) for w in POOLS])[None, :])
    return t


K0, Q0, V0, Z0, BA0, U0, GA0 = DN, 0, 2 * DN, 3 * DN, 4 * DN, 4 * DN + 16, 4 * DN + 16 + D // 2
GB0 = GA0 + D
GROUPS = ([("k", K0), ("k", K0 + 256), ("q", Q0), ("q", Q0 + 256), ("v", V0), ("v", V0 + 256),
           ("u", U0), ("u", U0 + 256)] + [("gb", GB0 + 256 * i) for i in range(4)]
          + [("z", Z0), ("z", Z0 + 256)] + [("ga", GA0 + 256 * i) for i in range(4)])
W_SLOTS = 4

WUSE = ([("in", g) for g in range(len(GROUPS))] + [("pool", 0), ("pool", 1)]
        + [("ub", i) for i in range(4)] + [("ua", i) for i in range(4)]
        + [("wo", i) for i in range(4)])
W_ON_DVE = ("ub", "ua", "wo")


def wuse(kind, i):
    n = WUSE.index((kind, i))
    dve = kind in W_ON_DVE
    return n, sum((k in W_ON_DVE) == dve for k, _ in WUSE[:n + 1])


JOBS = ([(n, h) for n in ("KT", "VT", "KK", "KQ", "AT") for h in (0, 1)]
        + [j for b in LEVELS for j in
           [(f"M{b}", 0), (f"M{b}", 1)]
           + ([(f"TN{b}", 0), (f"TN{b}", 1)] if b != LEVELS[-1] else [])
           + [(f"NT{b}", 0), (f"NT{b}", 1)]]
        + [(n, h) for n in ("WT", "U") for h in (0, 1)]
        + [("O", 0), ("DS", 0), ("WS", 1), ("O", 1), ("DS", 1), ("WS", 2), ("O", 2), ("DS", 2),
           ("WS", 3), ("O", 3)])
JOB = {j: n for n, j in enumerate(JOBS)}


def schedule():
    blocks = iter([("in", g, b) for g in range(6, len(GROUPS)) for b in range(2)]
                  + [("pool", i, 1) for i in range(2)] + [("ub", i, 1) for i in range(4)])
    order = []

    def jobs(*names):
        order.extend(("job",) + n for n in names)

    def filler(count=1):
        order.extend(b for b in [next(blocks, None) for _ in range(count)] if b)

    filler()
    order.append(("qsum",))
    filler(2)
    order.append(("qspread",))
    filler(2)
    for name in ("KT", "VT", "KK"):
        jobs((name, 0), (name, 1))
        filler()
    jobs(("KQ", 0), ("KQ", 1), ("AT", 0), ("AT", 1))
    filler(2)
    for b in LEVELS:
        jobs((f"M{b}", 0), (f"M{b}", 1))
        filler()
        if b != LEVELS[-1]:
            jobs((f"TN{b}", 0), (f"TN{b}", 1))
        jobs((f"NT{b}", 0), (f"NT{b}", 1))
        filler()
    jobs(("WT", 0), ("WT", 1), ("U", 0), ("U", 1))
    filler()
    for n in range(NCH):
        if n:
            jobs(("WS", n))
            filler()
        jobs(("O", n))
        if n < NCH - 1:
            jobs(("DS", n))
            filler()
    order.append(("osquare",))
    filler()
    order.append(("osum",))
    filler()
    order.append(("ospread",))
    filler(30)
    return order


ORDER = schedule()


def on_act(job):
    return job[0][0:2] in ("KT", "VT", "AT", "TN", "NT", "WT", "U", "O")


def act_number(job):
    return sum(on_act(j) for j in JOBS[:JOB[job] + 1])


def build_program(nc, x, consts, params, w_in, pool_w, w_up_a, w_up_b, w_out, w_router,
                  w_gate_up, b_gate_up, w_down, b_down, g_final, out):
    with ExitStack() as ctx:
        def sb(name, shape, dt=F32):
            return ctx.enter_context(nc.sbuf_tensor(name, shape, dt))

        def sem(name):
            return ctx.enter_context(nc.semaphore(name))

        ps = ctx.enter_context(nc.psum_tensor("ps", [P, 8, 512], F32))

        ring = sb("ring", [P, GU_UNITS + WD_UNITS, UNIT])
        cst = sb("cst", [P, NCONST])
        par = sb("par", [P, NPARAM])
        xs = sb("xs", [P, TT, D])
        hT = sb("hT", [P, KD, L])
        wring = sb("wring", [P, 2, KD, 256])
        wout = sb("wout", [P, KD, D])
        gates = sb("gates", [P, 2, KD, L])
        zT = sb("zT", [P, HP, L])
        ub = sb("ub", [P, 2, 4, UPAD + L])
        TTm = sb("TTm", [P, SLOTS, C])
        wrt = sb("wrt", [P, KD, E])
        state = sb("state", [P, 3, HP, C])
        sm = sb("sm", [P, 512])
        flag = sb("flag", [1, 2], I32)
        scr = ring[:, 0:GU_UNITS, :].rearrange("p u n -> p (u n)")
        CP = 4 + L
        cpad = scr[:, 0:12 * CP].rearrange("p (b n) -> p b n", b=12)
        o = 12 * CP
        cq = scr[:, o:o + 12 * L].rearrange("p (b n) -> p b n", b=12)
        kT, qT, vT = cq[:, 0:4], cq[:, 4:8], cq[:, 8:12]
        o += 12 * L

        def slots(at):
            return scr[:, at:at + SLOTS * C].rearrange("p (s n) -> p s n", s=SLOTS)

        Kb, kd, vtok, F1, F2, A, qkT, egr = (slots(o + i * SLOTS * C) for i in range(8))
        o += 8 * SLOTS * C
        LT = [slots(o), slots(0)]
        AT, N = slots(SLOTS * C), slots(2 * SLOTS * C)
        T, ktok = (wout[:, i].rearrange("p (s n) -> p s n", s=SLOTS) for i in range(2))
        wslot = [wring[:, 0], wring[:, 1]] + [
            wout[:, i:i + 2].rearrange("p a n -> p (a n)").rearrange("p (k n) -> p k n", k=KD) for i in (2, 4)]
        poolw = wout[:, 6, 0:4 * P].rearrange("p (g n) -> p g n", g=4)
        w_ba = wout[:, 6, 4 * P:5 * P].rearrange("p (k n) -> p k n", k=KD)
        WT, U = A, AT
        xn = cq.rearrange("p b n -> p (b n)")[:, 0:TT * D].rearrange("p (t n) -> p t n", t=TT)
        sq = TTm.rearrange("p s n -> p (s n)").rearrange("p (b n) -> p b n", b=HP)
        sg = zT[:, 0:2, :]
        zsig = F1.rearrange("p s n -> p (s n)").rearrange("p (b n) -> p b n", b=HP)
        usum = F2.rearrange("p s n -> p (s n)")[:, 0:3 * (UPAD + L)].rearrange("p (g n) -> p g n", g=3)
        gtri = ub.rearrange("p a b n -> p (a b n)")[:, 0:TT * HEADS * P].rearrange(
            "p (t h n) -> p t h n", t=TT, h=HEADS)
        oT = kT
        S, Sg, vnew = state[:, 0], state[:, 1], state[:, 2]
        upa = ring[:, GU_UNITS:GU_UNITS + 2, :].rearrange("p u n -> p (u n)").rearrange(
            "p (k n) -> p k n", k=4)
        upb = ring[:, GU_UNITS + 2:GU_UNITS + 4, :].rearrange("p u n -> p (u n)").rearrange(
            "p (k n) -> p k n", k=4)
        mo = wout.rearrange("p k n -> p (k n)")
        zx = ub.rearrange("p a b n -> p (a b n)")
        xn2 = zx[:, 0:2048].rearrange("p (t n) -> p t n", t=TT)
        xe = mo[:, 2048:2560].rearrange("p (k n) -> p k n", k=KD)
        gmin, sig, act_t, act_a, actT, outS = (mo[:, 2560 + 512 * i:3072 + 512 * i] for i in range(6))
        ctS = mo[:, 5632:5888]
        selw = mo[:, 5888:6144].rearrange("p (t n) -> p t n", t=TT)
        sel = mo[:, 6144:6272].rearrange("p (t n) -> p t n", t=TT)
        NPOS = ROUNDS * E + 1
        pos = mo[:, 6272:6272 + TT * NPOS].rearrange("p (t n) -> p t n", t=TT)
        comb = mo[:, 6600:6600 + TT * NPOS].rearrange("p (t n) -> p t n", t=TT)
        combT = mo[0:E, 6912:6912 + L]
        rt = mo[:, 7168:8192]
        h2T = hT
        xrows = hT[:, 0:2].rearrange("p k n -> p (k n)")
        wf = wring.rearrange("p s k n -> p (s k n)")
        b_gu = wf[0:1, 0:2 * F]
        b_dn = wf[0:E, 2 * F:3 * F]
        gfin = wf[:, 3 * F:4 * F]

        def cc(name):
            a, w = CONSTS[name]
            return cst[:, a:a + w]

        def pp(name):
            a, w = PARAMS[name]
            return par[:, a:a + w]

        ident, ones, ones_blk, tri, eye = cc("ident"), cc("ones"), cc("ones_blk"), cc("tri"), cc("eye")
        head_sum, head_row = cc("head_sum"), cc("head_row")
        inv_rows = sm[0:HEADS, 256:512]
        ssx, rstd = sm[:, 0:2], sm[:, 2:4]
        ones_c = sm[:, 4:5]
        eps_c = sm[:, 5:6]
        av, ab, sp_, gtok, beta_t = (sm[:, 16 + 16 * i:32 + 16 * i].rearrange("p (t h) -> p t h", t=TT)
                                     for i in range(5))
        ea = sm[:, 96:104]
        colG, colB, colL, eG, bEG, kdf, egl = (sm[:, 112 + 16 * i:128 + 16 * i] for i in range(7))

        x_landed = [sem(f"x_landed{t}") for t in range(TT)]
        tables_landed = sem("tables_landed")
        small_landed = sem("small_landed")
        w_landed = [sem(f"w_landed{s}") for s in range(W_SLOTS)]
        upa_landed, upb_landed, wout_landed = sem("upa_landed"), sem("upb_landed"), sem("wout_landed")
        late_landed = sem("late_landed")
        out_landed = sem("out_landed")
        pads_zeroed = sem("pads_zeroed")
        ss_ready, var_sqrt, rstd_ready = sem("ss_ready"), sem("var_sqrt"), sem("rstd_ready")
        xn_ready, xT_done, hT_ready = sem("xn_ready"), sem("xT_done"), sem("hT_ready")
        w_done, w_act, w_dve = sem("w_done"), sem("w_act"), sem("w_dve")
        conv_ready, sig_ready, silu_ready = sem("conv_ready"), sem("sig_ready"), sem("silu_ready")
        sq_ready, sumsq_done, norm_sqrt, normed = (sem("sq_ready"), sem("sumsq_done"),
                                                   sem("norm_sqrt"), sem("normed"))
        ba_done, ba_read, sp_exp, decay_act = sem("ba_done"), sem("ba_read"), sem("sp_exp"), sem("decay_act")
        g_ready, cols_done, cols_ready, cols_exp, cols_all = (sem("g_ready"), sem("cols_done"),
                                                              sem("cols_ready"), sem("cols_exp"), sem("cols_all"))
        rows_done, rows_exp, rows_diff, f_exp, f_ready = (sem("rows_done"), sem("rows_exp"),
                                                          sem("rows_diff"), sem("f_exp"), sem("f_ready"))
        dn_pe, dn_dve, dn_act = sem("dn_pe"), sem("dn_dve"), sem("dn_act")
        tok_scaled, base_ready, lt_ready = sem("tok_scaled"), sem("base_ready"), sem("lt_ready")
        qg_ready, s_ready = sem("qg_ready"), sem("s_ready")
        z_ready, pooled_ready, pool_step = sem("z_ready"), sem("pooled_ready"), sem("pool_step")
        inv_ready, norms_spread, o_ready = sem("inv_ready"), sem("norms_spread"), sem("o_ready")
        mix_ready, x1_ready, xn2_ready = sem("mix_ready"), sem("x1_ready"), sem("xn2_ready")
        x2T_done, h2T_ready, logits_done = sem("x2T_done"), sem("h2T_ready"), sem("logits_done")
        soft_in, soft_exp, mask_ready, count_done, route_ready = (
            sem("soft_in"), sem("soft_exp"), sem("mask_ready"), sem("count_done"), sem("route_ready"))
        combT_done, combT_ready, zero_ready = sem("combT_done"), sem("combT_ready"), sem("zero_ready")
        flag_ready = sem("flag_ready")
        dve_step = sem("dve_step")
        act_step = sem("act_step")
        gu_landed = [sem(f"gu_landed{u}") for u in range(GU_UNITS)]
        wd_landed = [sem(f"wd_landed{u}") for u in range(WD_UNITS)]
        bias_landed = sem("bias_landed")
        gu_used, wd_used, bias_used = sem("gu_used"), sem("wd_used"), sem("bias_used")
        sel_ready, selw_ready, gathered, xe_ready = sem("sel_ready"), sem("selw_ready"), sem("gathered"), sem("xe_ready")
        gmin_ready, gate_sig, gu_read, act_ready = sem("gmin_ready"), sem("gate_sig"), sem("gu_read"), sem("act_ready")
        ct_done, ct_copied, actT_done, actT_copied = sem("ct_done"), sem("ct_copied"), sem("actT_done"), sem("actT_copied")
        out_copied, scattered = sem("out_copied"), sem("scattered")
        up_ready, rows_copied, turned = sem("up_ready"), sem("rows_copied"), sem("turned")
        y_ready, ssf_ready, f_sqrt, fin_ready = sem("y_ready"), sem("ssf_ready"), sem("f_sqrt"), sem("fin_ready")

        def bank_q(job):
            r = JOB[job] % 3
            return [ps[0:C, 2 + 2 * r, :], ps[C:P, 3 + 2 * r, :]]

        def after_job(eng, job):
            eng.wait_ge(dn_dve, JOB[job] + 1)
            if on_act(job):
                eng.wait_ge(dn_act, act_number(job))

        def flat_banks(first, n):
            return ps[:, first:first + 2, :].rearrange("p b m -> p (b m)").rearrange(
                "p (s n) -> p s n", n=n)

        def hslots(a, h):
            return a[:, h * HALF:(h + 1) * HALF, :]

        def bc(a, n):
            return a.unsqueeze(2).to_broadcast([a.shape[0], a.shape[1], n])

        def rep(a, m):
            return a.unsqueeze(1).to_broadcast([a.shape[0], m, a.shape[1]])

        def chunk(a, n):
            return a.rearrange("p (hp n) c -> p hp n c", hp=HP)[:, :, n, :]

        block = ctx.enter_context(nc.Block())

        @block.sync
        def _(sp):
            for t in range(TT):
                sp.dma_start(xs[:, t], x[t * P:(t + 1) * P, :]).then_inc(x_landed[t], 16)
            sp.dma_start(cst[:], consts).then_inc(tables_landed, 16)
            sp.dma_start(par[:], params).then_inc(tables_landed, 16)
            w_rows = w_in.rearrange("(k p) n -> p k n", p=P)

            def load_group(g):
                if g >= W_SLOTS:
                    sp.wait_ge(w_done, wuse("in", g - W_SLOTS)[0] + 1)
                col = GROUPS[g][1]
                sp.dma_start(wslot[g % W_SLOTS], w_rows[:, :, col:col + 256]).then_inc(
                    w_landed[g % W_SLOTS], 16)

            load_group(0)
            sp.dma_start(w_ba, w_rows[:, :, BA0:BA0 + 2 * HEADS]).then_inc(small_landed, 16)
            load_group(1)
            sp.dma_start(poolw, pool_w.rearrange("g c d -> c g d")).then_inc(small_landed, 16)
            sp.dma_start(wrt[:], w_router.rearrange("(k p) e -> p k e", p=P)).then_inc(small_landed, 16)
            for g in range(2, len(GROUPS)):
                load_group(g)
                if g == 7:
                    sp.dma_start(upb, w_up_b.rearrange("(k p) n -> p k n", p=P)).then_inc(upb_landed, 16)
                if g == 9:
                    sp.dma_start(upa, w_up_a.rearrange("(k p) n -> p k n", p=P)).then_inc(upa_landed, 16)

            def load_unit_gu(e, k):
                sp.dma_start(ring[:, k, :], w_gate_up[bass.ds(e, 1), k * P:(k + 1) * P, :].rearrange(
                    "a p n -> p (a n)")).then_inc(gu_landed[k], 16)

            def load_unit_wd(e, u):
                sp.dma_start(
                    ring[:, GU_UNITS + u, :].rearrange("p (k n) -> p k n", k=2),
                    w_down[bass.ds(e, 1), 2 * u * P:(2 * u + 2) * P, :].rearrange(
                        "a (k p) n -> p (a k) n", p=P)).then_inc(wd_landed[u], 16)

            def load_bias(e):
                sp.dma_start(b_gu, b_gate_up[bass.ds(e, 1), :]).then_inc(bias_landed, 16)

            sp.wait_ge(w_done, wuse("pool", 1)[0] + 1)
            for a in (0, 4):
                sp.dma_start(wout[:, a:a + 4], w_out.rearrange("(k p) n -> p k n", p=P)[
                    :, a:a + 4, :]).then_inc(wout_landed, 16)
            sp.wait_ge(o_ready, HP)
            for k in range(GU_UNITS):
                load_unit_gu(0, k)
            load_bias(0)
            sp.dma_start(b_dn, b_down).then_inc(late_landed, 16)
            sp.dma_start(gfin, g_final.to_broadcast([P, D])).then_inc(late_landed, 16)
            sp.wait_ge(w_done, wuse("ua", 3)[0] + 1)
            for u in range(WD_UNITS):
                load_unit_wd(0, u)

            def load_expert(i, e):
                sp.wait_ge(bias_used, i)
                load_bias(e)
                for k in range(GU_UNITS):
                    sp.wait_ge(gu_used, GU_UNITS * (i - 1) + k + 1)
                    load_unit_gu(e, k)
                for u in range(WD_UNITS):
                    sp.wait_ge(wd_used, WD_UNITS * (i - 1) + u + 1)
                    load_unit_wd(e, u)

            with sp.Fori(1, E) as i:
                load_expert(i, i)
            sp.wait_ge(flag_ready, 1)
            over = sp.value_load(flag[0:1, 0:1], min_val=0, max_val=L)
            with sp.If(over > CAP):
                with sp.Fori(1, ROUNDS) as r:
                    with sp.Fori(0, E) as e:
                        load_expert(r * E + e, e)
                sp.nop()
            for t in range(TT):
                sp.wait_ge(fin_ready, t + 1)
                sp.dma_start(out[t * P:(t + 1) * P, :], xn2[:, t]).then_inc(out_landed, 16)
            sp.wait_ge(out_landed, 16 * TT)

        @block.tensor
        def _(pe):
            def bank_free(kind, i):
                n = wuse(kind, i)[0]
                if n >= 2:
                    k2, i2 = WUSE[n - 2]
                    pe.wait_ge(w_dve if k2 in W_ON_DVE else w_act, wuse(k2, i2)[1])
                return n % 2

            def project(g, b):
                bank = bank_free("in", g)
                if b == 0:
                    pe.wait_ge(w_landed[g % W_SLOTS], 16 * (g // W_SLOTS + 1))
                for k in range(KD):
                    mm = pe.matmul(ps[:, bank, b * L:(b + 1) * L],
                                   wslot[g % W_SLOTS][:, k, b * P:(b + 1) * P], hT[:, k, :],
                                   start=k == 0, stop=k == KD - 1)
                if b == 1:
                    mm.then_inc(w_done, 1)

            def job(name, h):
                j = JOB[(name, h)]
                if j >= 3:
                    after_job(pe, JOBS[j - 3])
                banks = bank_q((name, h))
                level = name.lstrip("MTN")
                if name in ("WS", "O", "DS"):
                    n = h
                    if name == "WS":
                        pe.wait_ge(s_ready, n)
                    if name == "DS" or name == "O":
                        if n == 0:
                            after_job(pe, ("U", 0))
                            after_job(pe, ("U", 1))
                        else:
                            after_job(pe, ("WS", n))
                    if name == "O" and n == 0:
                        pe.wait_ge(qg_ready, 1)
                    vn = chunk(U, 0) if n == 0 else vnew
                    for hp in range(HP):
                        for q in range(2):
                            r = slice(q * C, (q + 1) * C)
                            o_ = banks[q][:, hp * C:(hp + 1) * C]
                            if name == "WS":
                                mm = pe.matmul(o_, chunk(WT, n)[r, hp], S[r, hp], start=True, stop=True)
                            elif name == "DS":
                                mm = pe.matmul(o_, chunk(kd, n)[r, hp], vn[r, hp], start=True, stop=True)
                            else:
                                if n:
                                    pe.matmul(o_, S[r, hp], chunk(egr, n)[r, hp], start=True, stop=False)
                                mm = pe.matmul(o_, vn[r, hp], chunk(qkT, n)[r, hp], start=n == 0, stop=True)
                    mm.then_inc(dn_pe, 1)
                    return
                if (name, h) == ("KT", 0):
                    pe.wait_ge(normed, 2 * HP)
                    pe.wait_ge(rows_diff, 1)
                    pe.wait_ge(rows_exp, 1)
                if name == "VT":
                    pe.wait_ge(silu_ready, 6)
                if (name, h) == ("VT", 0):
                    pe.wait_ge(cols_ready, 1)
                if name == "KQ":
                    pe.wait_ge(normed, 2 * HP)
                if name == "AT":
                    after_job(pe, ("KK", h))
                if name[0] == "M":
                    pe.wait_ge(base_ready, 2 * (h + 1))
                    pe.wait_ge(lt_ready, 2 * LEVELS.index(int(level)) + h + 1)
                    if level != "2":
                        after_job(pe, (f"TN{int(level) // 2}", h))
                if name[0:2] in ("TN", "NT"):
                    after_job(pe, (f"M{level}", h))
                    if level != "2":
                        after_job(pe, (f"NT{int(level) // 2}", h))
                if name in ("WT", "U"):
                    after_job(pe, ("NT32", h))
                    pe.wait_ge(tok_scaled, 2 * (h + 1) if name == "WT" else 4 + h + 1)
                for s in range(HALF):
                    sl = h * HALF + s
                    hp, n = sl // NCH, sl % NCH
                    tok = slice(n * C, (n + 1) * C)
                    for q in range(2):
                        r = slice(q * C, (q + 1) * C)
                        lt = LT[LEVELS.index(int(level)) % 2] if name[0] == "M" else None
                        a, b = {
                            "KT": lambda: (kT[r, hp, tok], eye[r]), "VT": lambda: (vT[r, hp, tok], eye[r]),
                            "KK": lambda: (kT[r, hp, tok], kT[r, hp, tok]),
                            "KQ": lambda: (kT[r, hp, tok], qT[r, hp, tok]),
                            "AT": lambda: (A[r, sl], eye[r]), "M": lambda: (lt[r, sl], T[r, sl]),
                            "TN": lambda: (TTm[r, sl], N[r, sl]), "NT": lambda: (N[r, sl], TTm[r, sl]),
                            "WT": lambda: (Kb[r, sl], TTm[r, sl]), "U": lambda: (TTm[r, sl], vtok[r, sl]),
                        }[name.rstrip("0123456789")]()
                        mm = pe.matmul(banks[q][:, s * C:(s + 1) * C], a, b, start=True, stop=True)
                mm.then_inc(dn_pe, 1)

            pe.wait_ge(tables_landed, 32)
            for t in range(TT):
                pe.wait_ge(xn_ready, t + 1)
                for k in range(KD):
                    mm = pe.transpose(ps[:, 2 + 2 * t + k // 4, (k % 4) * P:(k % 4 + 1) * P],
                                      xn[:, t, k * P:(k + 1) * P], ident)
                    if k % 4 == 3:
                        mm.then_inc(xT_done, 1)
            pe.wait_ge(hT_ready, 4)

            def group(g):
                project(g, 0)
                project(g, 1)

            def sums_of_squares(i):
                pe.wait_ge(sq_ready, i + 1)
                if i:
                    pe.wait_ge(norm_sqrt, i)
                for hp in range(HP):
                    mm = pe.matmul(ps[0:HEADS, 7, 0:L], head_sum[:, hp * HEADS:(hp + 1) * HEADS],
                                   sq[:, hp], start=hp == 0, stop=hp == HP - 1)
                mm.then_inc(sumsq_done, 1)

            def spread_norms(i):
                pe.wait_ge(inv_ready, i + 1)
                if i == 1:
                    pe.wait_ge(normed, HP)
                for hp in range(HP):
                    mm = pe.matmul(ps[:, (2, 2, 6)[i] + hp // 2, (hp % 2) * L:(hp % 2 + 1) * L],
                                   head_row[0:HEADS, hp * P:(hp + 1) * P], inv_rows, start=True, stop=True)
                mm.then_inc(norms_spread, 1)

            group(0)
            pe.wait_ge(small_landed, 48)
            for t in range(TT):
                for k in range(KD):
                    mm = pe.matmul(ps[:, 6, t * 16:t * 16 + 16], hT[:, k, t * P:(t + 1) * P], w_ba[:, k],
                                   start=k == 0, stop=k == KD - 1)
            mm.then_inc(ba_done, 1)
            group(1)
            group(2)
            pe.wait_ge(g_ready, 1)
            pe.wait_ge(decay_act, 1)
            for t in range(TT):
                for r in range(2):
                    n = 2 * t + r
                    for q in range(2):
                        for i, (m, v) in enumerate(((tri, gtok), (ident, beta_t), (ones_blk, gtok))):
                            o_ = ps[q * C:(q + 1) * C, 6, 64 + 16 * i:80 + 16 * i].rearrange(
                                "p (hp n) -> p hp n", hp=HP)[:, :, n]
                            mm = pe.matmul(o_, m[:, r * C:(r + 1) * C],
                                           v[:, t].rearrange("p (hp q) -> p hp q", q=2)[:, :, q],
                                           start=True, stop=True)
            mm.then_inc(cols_done, 1)
            group(3)
            sums_of_squares(0)
            group(4)
            spread_norms(0)
            pe.wait_ge(g_ready, 2)
            for hp in range(HP):
                for t in range(TT):
                    for q in range(2):
                        mm = pe.matmul(ps[q * C:(q + 1) * C, 4 + hp // 2,
                                          (hp % 2) * L + t * P:(hp % 2) * L + (t + 1) * P],
                                       ones[:, 0:C], gtri[:, t, 2 * hp + q], start=True, stop=True)
            mm.then_inc(rows_done, 1)
            group(5)

            def up_project(kind, i, w, v):
                bank = bank_free(kind, i)
                for b in range(2):
                    m = 2 * i + b
                    for k in range(4):
                        mm = pe.matmul(ps[:, bank, b * L:(b + 1) * L], w[:, k, m * P:(m + 1) * P],
                                       v[:, k], start=k == 0, stop=k == 3)
                mm.then_inc(w_done, 1)

            for what, *which in ORDER:
                if what == "job":
                    job(*which)
                elif what == "in":
                    project(*which)
                elif what == "pool":
                    i = which[0]
                    bank = bank_free("pool", i)
                    pe.wait_ge(pooled_ready, 4)
                    for g in (2 * i, 2 * i + 1):
                        mm = pe.matmul(ps[:, bank, (g % 2) * L:(g % 2 + 1) * L], poolw[:, g],
                                       ub[:, 0, g, UPAD:], start=True, stop=True)
                    mm.then_inc(w_done, 1)
                elif what == "ub":
                    if which[0] == 0:
                        pe.wait_ge(upb_landed, 16)
                        pe.wait_ge(w_act, wuse("pool", 1)[1])
                    up_project("ub", which[0], upb, ub[:, 1, :, UPAD:])
                elif what == "qsum":
                    sums_of_squares(1)
                elif what == "qspread":
                    spread_norms(1)
                elif what == "ospread":
                    spread_norms(2)
                elif what == "osum":
                    sums_of_squares(2)
            pe.wait_ge(upa_landed, 16)
            pe.wait_ge(o_ready, HP)
            for i in range(4):
                up_project("ua", i, upa, zT)
            pe.wait_ge(wout_landed, 32)
            def mix_out(i):
                t, c = i // 2, i % 2
                bank = bank_free("wo", i)
                for k in range(KD):
                    pe.wait_ge(mix_ready, k // 2 + 1)
                    mm = pe.matmul(ps[:, bank, :], gates[:, 0, k, t * P:(t + 1) * P],
                                   wout[:, k, c * 512:(c + 1) * 512], start=k == 0, stop=k == KD - 1)
                mm.then_inc(w_done, 1)

            def turn(t):
                pe.wait_ge(xn2_ready, t + 1)
                for k in range(KD):
                    mm = pe.transpose(ps[:, 2 + 2 * t + k // 4, (k % 4) * P:(k % 4 + 1) * P],
                                      xn2[:, t, k * P:(k + 1) * P], ident)
                    if k % 4 == 3:
                        mm.then_inc(x2T_done, 1)

            def route(t):
                pe.wait_ge(h2T_ready, 2 * t + 2)
                for k in range(KD):
                    mm = pe.matmul(ps[:, 6 + t, 0:E], h2T[:, k, t * P:(t + 1) * P], wrt[:, k],
                                   start=k == 0, stop=k == KD - 1)
                mm.then_inc(logits_done, 1)

            mix_out(0)
            mix_out(1)
            mix_out(2)
            turn(0)
            mix_out(3)
            route(0)
            turn(1)
            route(1)
            mask = rt[:, 64:64 + TT * E].rearrange("p (t e) -> p t e", t=TT)
            pe.wait_ge(mask_ready, 1)
            pe.matmul(ps[:, 2, 0:E], cc("before"), mask[:, 0], start=True, stop=True)
            pe.matmul(ps[:, 2, E:2 * E], ones, mask[:, 0], start=True, stop=False)
            pe.matmul(ps[:, 2, E:2 * E], cc("before"), mask[:, 1], start=False, stop=True)
            pe.matmul(ps[0:1, 2, 64:64 + E], ones[:, 0:1], mask[:, 0], start=True, stop=False)
            pe.matmul(ps[0:1, 2, 64:64 + E], ones[:, 0:1], mask[:, 1], start=False, stop=True).then_inc(
                count_done, 1)
            pe.wait_ge(flag_ready, 1)
            for t in range(TT):
                mm = pe.transpose(ps[0:E, 6, 128 + t * P:128 + (t + 1) * P], comb[:, t, 0:E], ident)
            mm.then_inc(combT_done, 1)
            pe.wait_ge(combT_ready, 1)
            pe.wait_ge(late_landed, 32)

            def y(t, c):
                return ps[:, 4 + 2 * t + c, :]

            for t in range(TT):
                for c in range(2):
                    pe.matmul(y(t, c), combT[:, t * P:(t + 1) * P], b_dn[:, c * 512:(c + 1) * 512],
                              start=True, stop=False, skip_group_check=True)

            pe.wait_ge(zero_ready, 2)

            def gather(i):
                pe.wait_ge(sel_ready, i + 1)
                for t in range(TT):
                    for c in range(2):
                        mm = pe.matmul(ps[c * CAP:(c + 1) * CAP, 3, :], sel[:, t, :],
                                       xn2[:, t, c * 512:(c + 1) * 512], start=t == 0, stop=t == TT - 1)
                mm.then_inc(gathered, 1)

            def turn_gathered(i):
                pe.wait_ge(rows_copied, i + 1)
                for j in range(4):
                    mm = pe.transpose(ps[:, 3, j * P:(j + 1) * P], xrows[:, j * P:(j + 1) * P], ident)
                mm.then_inc(turned, 1)

            def scatter():
                for t in range(TT):
                    for c in range(2):
                        r = slice(c * CAP, (c + 1) * CAP)
                        mm = pe.matmul(y(t, c), ctS[r, t * P:(t + 1) * P], outS[r, :],
                                       start=False, stop=False, skip_group_check=True)
                mm.then_inc(scattered, 1)

            def expert(i):
                pe.wait_ge(xe_ready, i + 1)
                pe.wait_ge(bias_landed, 16 * (i + 1))
                for a in range(4):
                    r = slice((a % 2) * CAP, (a % 2 + 1) * CAP)
                    mm = pe.matmul(ps[r, a // 2, :], ones[0:1, 0:CAP], b_gu[:, a * 512:(a + 1) * 512],
                                   start=True, stop=False)
                mm.then_inc(bias_used, 1)
                for k in range(GU_UNITS):
                    pe.wait_ge(gu_landed[k], 16 * (i + 1))
                    for a in range(4):
                        r = slice((a % 2) * CAP, (a % 2 + 1) * CAP)
                        mm = pe.matmul(ps[r, a // 2, :], xe[:, k, :], ring[:, k, a * 512:(a + 1) * 512],
                                       start=False, stop=k == GU_UNITS - 1)
                    mm.then_inc(gu_used, 1)
                pe.wait_ge(selw_ready, i + 1)
                for t in range(TT):
                    mm = pe.transpose(ps[:, 2, t * P:(t + 1) * P], selw[:, t, :], ident)
                mm.then_inc(ct_done, 1)
                pe.wait_ge(out_copied, i + 1)
                scatter()
                gather(i + 1)
                pe.wait_ge(ct_copied, i + 1)
                pe.wait_ge(act_ready, i + 1)
                for j in range(4):
                    mm = pe.transpose(ps[:, 2, j * P:(j + 1) * P], act_a[:, j * P:(j + 1) * P], ident)
                mm.then_inc(actT_done, 1)
                turn_gathered(i + 1)
                pe.wait_ge(actT_copied, i + 1)
                pe.wait_ge(xe_ready, i + 2)
                for k in range(KD):
                    if k % 2 == 0:
                        pe.wait_ge(wd_landed[k // 2], 16 * (i + 1))
                    half, j = k // 4, k % 4
                    lhs = actT[:, j * P + half * CAP:j * P + (half + 1) * CAP]
                    for c in range(2):
                        w = ring[:, GU_UNITS + k // 2, (k % 2) * D + c * 512:(k % 2) * D + (c + 1) * 512]
                        mm = pe.matmul(ps[c * CAP:(c + 1) * CAP, 3, :], lhs, w, start=k == 0, stop=k == KD - 1)
                    if k % 2 == 1:
                        mm.then_inc(wd_used, 1)

            gather(0)
            turn_gathered(0)
            with pe.Fori(0, E) as i:
                expert(i)
            pe.wait_ge(flag_ready, 1)
            over = pe.value_load(flag[0:1, 0:1], min_val=0, max_val=L)
            with pe.If(over > CAP):
                with pe.Fori(E, ROUNDS * E) as i:
                    expert(i)
                pe.wait_ge(out_copied, ROUNDS * E + 1)
            pe.wait_ge(out_copied, E + 1)
            scatter()

        @block.vector
        def _(dve):
            steps = [0]

            def step(ins):
                steps[0] += 1
                ins.then_inc(dve_step, 1)
                dve.wait_ge(dve_step, steps[0])

            def add_scaled(o_, a, s, b, o0=ALU.mult, o1=ALU.add):
                return dve.scalar_tensor_tensor(out=o_, in0=a, scalar=s, in1=b, op0=o0, op1=o1)

            dve.memset(eps_c, EPS).then_inc(zero_ready, 1)
            junk = zT.rearrange("p b n -> p (b n)")
            def mean_square(t):
                step(dve.tensor_tensor_reduce(out=junk, in0=xs[:, t], in1=xs[:, t], scale=1.0, scalar=0.0,
                                              op0=ALU.mult, op1=ALU.add, accum_out=ssx[:, t:t + 1]))
                dve.tensor_scalar(ssx[:, t:t + 1], ssx[:, t:t + 1], 1.0 / D, EPS, ALU.mult, ALU.add).then_inc(
                    ss_ready, 1)

            def scale_rows(n, t, o_, ready):
                dve.wait_ge(var_sqrt, n + 1)
                step(dve.reciprocal(rstd[:, t:t + 1], rstd[:, t:t + 1]))
                dve.tensor_scalar(o_[:, t], xs[:, t], rstd[:, t:t + 1], None, ALU.mult).then_inc(ready, 1)

            for t in range(TT):
                dve.wait_ge(x_landed[t], 16)
                mean_square(t)
            for t in range(TT):
                scale_rows(t, t, xn, xn_ready)
            dve.wait_ge(tables_landed, 32)
            for t in range(TT):
                for h in range(2):
                    dve.wait_ge(xT_done, 2 * t + h + 1)
                    dve.tensor_tensor(
                        hT[:, 4 * h:4 * h + 4, t * P:(t + 1) * P],
                        ps[:, 2 + 2 * t + h, :].rearrange("p (k n) -> p k n", k=4),
                        bc(pp("gmix")[:, 4 * h:4 * h + 4], P), ALU.mult).then_inc(hT_ready, 1)

            conv = pp("conv").rearrange("p (b j) -> p b j", b=12)

            def convolve(g):
                dve.wait_ge(w_act, g + 1)
                if g == 0:
                    dve.wait_ge(pads_zeroed, 1)
                for b in (2 * g, 2 * g + 1):
                    step(dve.tensor_scalar(cq[:, b], cpad[:, b, 1:1 + L], conv[:, b, 0:1], None, ALU.mult))
                    for j in range(1, TAPS):
                        ins = add_scaled(cq[:, b], cpad[:, b, 1 + j:1 + j + L], conv[:, b, j:j + 1], cq[:, b])
                        if j < TAPS - 1:
                            step(ins)
                    ins.then_inc(conv_ready, 1)

            def silu(g):
                dve.wait_ge(sig_ready, g + 1)
                dve.tensor_tensor(cq[:, 2 * g:2 * g + 2], cq[:, 2 * g:2 * g + 2], sg, ALU.mult).then_inc(
                    silu_ready, 1)

            def invert_norms(i):
                dve.wait_ge(norm_sqrt, i + 1)
                dve.reciprocal(inv_rows, inv_rows).then_inc(inv_ready, 1)

            def spread(i, hp):
                return ps[:, (2, 2, 6)[i] + hp // 2, (hp % 2) * L:(hp % 2 + 1) * L]

            def normalise(i):
                dve.wait_ge(norms_spread, i + 1)
                for hp in range(HP):
                    v = (kT, qT)[i][:, hp]
                    add_scaled(v, v, (1.0, HD ** -0.5)[i], spread(i, hp), ALU.mult, ALU.mult).then_inc(normed, 1)

            convolve(0)
            dve.wait_ge(ba_done, 1)
            bav = ps[:, 6, 0:32].rearrange("p (t n) -> p t n", t=TT)
            step(dve.tensor_tensor(av, bav[:, :, HEADS:], rep(pp("dtb"), TT), ALU.add))
            add_scaled(ab, av, -1.0, av, ALU.mult, ALU.max).then_inc(ba_read, 1)
            convolve(1)
            silu(0)
            silu(1)
            dve.wait_ge(sp_exp, 1)
            step(add_scaled(sp_, av, 0.0, ab, ALU.max, ALU.add))
            add_scaled(gtok, sp_, -1.0, rep(ea, TT), ALU.mult, ALU.mult).then_inc(g_ready, 1)
            dve.wait_ge(g_ready, 1)
            for t in range(TT):
                ins = dve.tensor_tensor(gtri[:, t], rep(tri, HEADS), bc(gtok[:, t], P), ALU.mult)
            ins.then_inc(g_ready, 1)
            convolve(2)
            dve.wait_ge(cols_done, 1)
            dve.tensor_copy(sm[:, 112:160], ps[:, 6, 64:112]).then_inc(cols_ready, 1)
            dve.wait_ge(cols_ready, 1)
            dve.tensor_tensor(kdf, colL, colG, ALU.subtract).then_inc(cols_ready, 1)
            silu(2)
            convolve(3)
            silu(3)
            dve.wait_ge(cols_exp, 1)
            dve.tensor_tensor(bEG, colB, eG, ALU.mult).then_inc(cols_all, 1)
            invert_norms(0)
            convolve(4)
            normalise(0)
            dve.wait_ge(rows_done, 1)
            diff = Kb
            step(dve.tensor_tensor(diff, flat_banks(4, C),
                                   bc(colG, C), ALU.subtract))
            dve.tensor_scalar(F2, diff, 0.0, None, ALU.min).then_inc(rows_diff, 1)
            dve.tensor_scalar(F1, diff, 0.0, None, ALU.max).then_inc(rows_diff, 1)
            silu(4)
            convolve(5)
            silu(5)

            dest = {"KT": ktok, "VT": vtok, "AT": AT, "TN": T, "NT": TTm, "WT": WT, "U": U}

            def empty(name, h):
                banks = bank_q((name, h))
                kind = name.rstrip("0123456789")
                dve.wait_ge(dn_pe, JOB[(name, h)] + 1)
                if kind == "WT" and h == 0:
                    dve.wait_ge(lt_ready, 2 * len(LEVELS))
                if kind in dest:
                    ins = dve.tensor_copy(dest[kind][0:C, h * HALF:(h + 1) * HALF],
                                          banks[0].rearrange("p (s n) -> p s n", n=C))
                elif kind == "O":
                    ins = dve.tensor_copy(oT[0:C, :, h * C:(h + 1) * C],
                                          banks[0][:, 0:HP * C].rearrange("p (s n) -> p s n", n=C))
                elif kind in ("WS", "DS"):
                    for q in range(2):
                        r = slice(q * C, (q + 1) * C)
                        v = banks[q][:, 0:HP * C].rearrange("p (s n) -> p s n", n=C)
                        if kind == "WS":
                            ins = dve.tensor_tensor(vnew[r], chunk(U, h)[r], v, ALU.subtract)
                        elif h == 0:
                            ins = dve.tensor_copy(S[r], v)
                        else:
                            ins = dve.tensor_tensor(S[r], Sg[r], v, ALU.add)
                    if kind == "DS":
                        ins.then_inc(s_ready, 1)
                        dve.wait_ge(s_ready, h + 1)
                        ins = dve.tensor_tensor(Sg, S, bc(egl.rearrange("p (hp n) -> p hp n", hp=HP)[
                            :, :, h + 1], C), ALU.mult)
                else:
                    for q in range(2):
                        r = slice(q * C, (q + 1) * C)
                        sl = slice(h * HALF, (h + 1) * HALF)
                        v = banks[q].rearrange("p (s n) -> p s n", n=C)
                        if kind == "M":
                            ins = add_scaled(N[r, sl], v, -1.0, rep(eye[r], HALF))
                        else:
                            ins = dve.tensor_tensor((A if kind == "KK" else qkT)[r, sl], v,
                                                    (F1 if kind == "KK" else F2)[r, sl], ALU.mult)
                ins.then_inc(dn_dve, 1)

            def gated(kind, i):
                n, count = wuse(kind, i)
                dve.wait_ge(w_done, n + 1)
                side = 1 if kind == "ub" else 0
                if i == 0:
                    dve.wait_ge(w_act, wuse("in", len(GROUPS) - 1)[1])
                v = gates[:, side, 2 * i:2 * i + 2]
                dve.tensor_tensor(v, v, ps[:, n % 2, :].rearrange("p (b n) -> p b n", b=2),
                                  ALU.mult).then_inc(w_dve, 1)

            dve.wait_ge(f_ready, 2)
            for what, *which in ORDER:
                if what == "job":
                    empty(*which)
                elif what == "ub":
                    gated("ub", which[0])
                elif (what, *which) == ("in", 14, 1):
                    dve.wait_ge(w_act, wuse("in", 13)[1])
                    dve.tensor_tensor(zT[:], zT[:], zsig, ALU.mult).then_inc(z_ready, 1)
                elif what == "qsum":
                    invert_norms(1)
                elif what == "qspread":
                    normalise(1)
                    dve.wait_ge(rows_exp, 1)
                    dve.wait_ge(normed, 2 * HP)
                    dve.tensor_tensor(egr, egr, qT.rearrange("p b (n c) -> p (b n) c", c=C),
                                      ALU.mult).then_inc(qg_ready, 1)
                elif what == "osum":
                    invert_norms(2)
                elif what == "ospread":
                    dve.wait_ge(norms_spread, 3)
                    dve.wait_ge(z_ready, 1)
                    for hp in range(HP):
                        step(add_scaled(zT[:, hp], zT[:, hp], pp("dn"), spread(2, hp), ALU.mult, ALU.mult))
                        dve.tensor_tensor(zT[:, hp], oT[:, hp], zT[:, hp], ALU.mult).then_inc(o_ready, 1)
            for i in range(4):
                gated("ua", i)
                dve.wait_ge(w_dve, wuse("ua", i)[1])
                dve.tensor_tensor(gates[:, 0, 2 * i:2 * i + 2], gates[:, 0, 2 * i:2 * i + 2],
                                  gates[:, 1, 2 * i:2 * i + 2], ALU.add).then_inc(mix_ready, 1)
            def add_mixer(i):
                t, c = i // 2, i % 2
                n, count = wuse("wo", i)
                dve.wait_ge(w_done, n + 1)
                v = xs[:, t, c * 512:(c + 1) * 512]
                dve.tensor_tensor(v, v, ps[:, n % 2, :], ALU.add).then_inc(w_dve, 1)
                if c == 1:
                    dve.wait_ge(w_dve, count)
                    mean_square(t)

            def empty_turned(t):
                for h in range(2):
                    dve.wait_ge(x2T_done, 2 * t + h + 1)
                    dve.tensor_tensor(
                        h2T[:, 4 * h:4 * h + 4, t * P:(t + 1) * P],
                        ps[:, 2 + 2 * t + h, :].rearrange("p (k n) -> p k n", k=4),
                        bc(pp("gffn")[:, 4 * h:4 * h + 4], P), ALU.mult).then_inc(h2T_ready, 1)

            add_mixer(0)
            add_mixer(1)
            scale_rows(2, 0, xn2, xn2_ready)
            add_mixer(2)
            empty_turned(0)
            add_mixer(3)
            scale_rows(3, 1, xn2, xn2_ready)
            empty_turned(1)
            logit = rt[:, 512:512 + TT * (E + 4)].rearrange("p (t e) -> p t e", t=TT)
            mask = rt[:, 64:128].rearrange("p (t e) -> p t e", t=TT)
            left = rt[:, 640:640 + TT * (E + 4)].rearrange("p (t e) -> p t e", t=TT)
            top = rt[:, 192:208].rearrange("p (t e) -> p t e", t=TT)
            soft = rt[:, 224:288].rearrange("p (t e) -> p t e", t=TT)
            den = rt[:, 288:290]
            where = rt[:, 320:384].rearrange("p (t e) -> p t e", t=TT)
            dve.memset(rt[:, 480:488], MARK)
            dve.memset(pos[:, :, NPOS - 1:NPOS], -1.0)
            dve.memset(comb[:, :, NPOS - 1:NPOS], 0.0)
            dve.memset(outS, 0.0).then_inc(out_copied, 1)
            dve.memset(ctS, 0.0).then_inc(zero_ready, 1)
            for t in range(TT):
                dve.wait_ge(logits_done, t + 1)
                step(dve.tensor_tensor(logit[:, t, 0:E], ps[:, 6 + t, 0:E], pp("brouter"), ALU.add))
                step(dve.tensor_copy(logit[:, t, E:E + 4], rt[:, 480:484]))
                step(dve.max(out=top[:, t], in_=logit[:, t, 0:E]))
                dve.tensor_scalar(soft[:, t], logit[:, t, 0:E], top[:, t, 0:1], None, ALU.subtract).then_inc(soft_in, 1)
                step(dve.tensor_copy(top[:, t, TOP_K:8], rt[:, 484:488]))
                step(dve.match_replace(out=left[:, t], in_to_replace=top[:, t], in_values=logit[:, t],
                                       imm_value=GONE))
                ins = dve.tensor_tensor(mask[:, t], logit[:, t, 0:E], left[:, t, 0:E], ALU.is_gt)
            ins.then_inc(mask_ready, 1)
            dve.wait_ge(mask_ready, 1)
            dve.wait_ge(soft_exp, 1)
            step(dve.tensor_tensor(soft, soft, mask, ALU.mult))
            step(dve.tensor_reduce(den, soft, AX.X, ALU.add))
            step(dve.reciprocal(den, den))
            for t in range(TT):
                step(dve.tensor_scalar(comb[:, t, 0:ROUNDS * E].rearrange("p (r e) -> p r e", r=ROUNDS),
                                       rep(soft[:, t], ROUNDS), den[:, t:t + 1], None, ALU.mult))
            dve.wait_ge(count_done, 1)
            step(add_scaled(where, ps[:, 2, 0:TT * E].rearrange("p (t e) -> p t e", t=TT), 1.0, mask,
                            ALU.add, ALU.mult))
            for r in range(ROUNDS):
                step(dve.tensor_scalar(pos[:, :, r * E:(r + 1) * E], where, -1.0 - r * CAP, None, ALU.add))
            step(dve.tensor_reduce(rt[0:1, 490:491], ps[0:1, 2, 64:64 + E], AX.X, ALU.max))
            dve.tensor_copy(flag[0:1, 0:1], rt[0:1, 490:491]).then_inc(flag_ready, 1)

            def build_sel(i):
                for t in range(TT):
                    ins = dve.tensor_scalar(sel[:, t], cc("iota")[:, 0:CAP], pos[:, t, bass.ds(i, 1)], None,
                                            ALU.is_equal)
                ins.then_inc(sel_ready, 1)

            def build_selw(i):
                for t in range(TT):
                    ins = dve.tensor_scalar(selw[:, t], cc("iota"), pos[:, t, bass.ds(i, 1)],
                                            comb[:, t, bass.ds(i, 1)], ALU.is_equal, ALU.mult)
                ins.then_inc(selw_ready, 1)

            def empty_gather(i):
                dve.wait_ge(turned, i + 1)
                for c in range(2):
                    ins = dve.tensor_tensor(
                        xe[:, 4 * c:4 * c + 4, :],
                        ps[:, 3, :].rearrange("p (j c n) -> p j c n", j=4, c=2)[:, :, c, :],
                        bc(pp("gffn")[:, 4 * c:4 * c + 4], CAP), ALU.mult)
                ins.then_inc(xe_ready, 1)

            def expert(i):
                dve.wait_ge(gathered, i + 1)
                build_sel(i + 1)
                dve.wait_ge(gu_used, GU_UNITS * (i + 1))
                dve.tensor_scalar(gmin, ps[:, 0, :], LIMIT, None, ALU.min).then_inc(gmin_ready, 1)
                dve.tensor_scalar(act_t, ps[:, 1, :], LIMIT, -LIMIT, ALU.min, ALU.max).then_inc(gu_read, 1)
                dve.wait_ge(gu_read, i + 1)
                add_scaled(act_t, act_t, 1.0, gmin, ALU.add, ALU.mult).then_inc(up_ready, 1)
                dve.wait_ge(up_ready, i + 1)
                dve.wait_ge(gate_sig, i + 1)
                dve.tensor_tensor(act_a, act_t, sig, ALU.mult).then_inc(act_ready, 1)
                dve.wait_ge(ct_done, i + 1)
                build_selw(i + 1)
                empty_gather(i + 1)

            dve.wait_ge(flag_ready, 1)
            dve.wait_ge(combT_done, 1)
            build_sel(0)
            build_selw(0)
            empty_gather(0)
            with dve.Fori(0, E) as i:
                expert(i)
            over = dve.value_load(flag[0:1, 0:1], min_val=0, max_val=L)
            with dve.If(over > CAP):
                with dve.Fori(E, ROUNDS * E) as i:
                    expert(i)
                dve.wait_ge(scattered, ROUNDS * E + 1)
            dve.wait_ge(scattered, E + 1)
            for t in range(TT):
                v = xs[:, t].rearrange("p (c n) -> p c n", c=2)
                dve.tensor_tensor(v, v, ps[:, 4 + 2 * t:6 + 2 * t, :], ALU.add).then_inc(y_ready, 1)
                dve.wait_ge(y_ready, t + 1)
                dve.tensor_tensor_reduce(out=junk, in0=xs[:, t], in1=xs[:, t], scale=1.0, scalar=0.0,
                                         op0=ALU.mult, op1=ALU.add,
                                         accum_out=ssx[:, t:t + 1]).then_inc(ssf_ready, 1)
                dve.wait_ge(f_sqrt, t + 1)
                dve.reciprocal(rstd[:, t:t + 1], rstd[:, t:t + 1]).then_inc(rstd_ready, 1)
                dve.wait_ge(rstd_ready, t + 1)
                add_scaled(xn2[:, t], xs[:, t], rstd[:, t:t + 1], gfin, ALU.mult, ALU.mult).then_inc(fin_ready, 1)

        @block.scalar
        def _(act):
            fn = act.activation

            def copy(o_, i_):
                return act.copy(o_, i_)

            act.wait_ge(zero_ready, 1)

            def root(n, t):
                act.wait_ge(ss_ready, n + 1)
                fn(rstd[:, t:t + 1], ssx[:, t:t + 1], ACT.Sqrt).then_inc(var_sqrt, 1)

            root(0, 0)
            root(1, 1)

            def to_conv(g):
                act.wait_ge(w_done, g + 1)
                copy(cpad[:, 2 * g:2 * g + 2, 4:], ps[:, g % 2, :].rearrange("p (b n) -> p b n", b=2)).then_inc(
                    w_act, 1)

            def sigmoid(g):
                act.wait_ge(conv_ready, 2 * g + 2)
                act.wait_ge(silu_ready, g)
                fn(sg, cq[:, 2 * g:2 * g + 2], ACT.Sigmoid).then_inc(sig_ready, 1)

            def square(i):
                act.wait_ge(silu_ready, 2 * i + 2)
                if i:
                    act.wait_ge(sumsq_done, i)
                fn(sq, (kT, qT)[i], ACT.Square).then_inc(sq_ready, 1)

            def norm_root(i, scale=1.0):
                act.wait_ge(sumsq_done, i + 1)
                if i:
                    act.wait_ge(norms_spread, i)
                fn(inv_rows, ps[0:HEADS, 7, 0:L], ACT.Sqrt, bias=eps_c[0:HEADS], scale=scale).then_inc(norm_sqrt, 1)

            to_conv(0)
            act.wait_ge(ba_read, 1)
            act.wait_ge(tables_landed, 32)
            fn(ab, ab, ACT.Exp, scale=-1.0).then_inc(act_step, 1)
            fn(ea, pp("alog"), ACT.Exp)
            act.wait_ge(act_step, 1)
            fn(ab, ab, ACT.Ln, bias=1.0).then_inc(sp_exp, 1)
            fn(beta_t, ps[:, 6, 0:32].rearrange("p (t n) -> p t n", t=TT)[:, :, 0:HEADS],
               ACT.Sigmoid).then_inc(decay_act, 1)
            to_conv(1)
            sigmoid(0)
            sigmoid(1)
            square(0)
            to_conv(2)
            act.wait_ge(cols_ready, 2)
            fn(eG, colG, ACT.Exp)
            fn(kdf, kdf, ACT.Exp)
            fn(egl, colL, ACT.Exp).then_inc(cols_exp, 1)
            sigmoid(2)
            to_conv(3)
            sigmoid(3)
            norm_root(0)
            square(1)
            to_conv(4)
            act.wait_ge(rows_diff, 1)
            fn(egr, flat_banks(4, C), ACT.Exp).then_inc(rows_exp, 1)
            fn(F2, F2, ACT.Exp).then_inc(f_exp, 1)
            act.wait_ge(rows_diff, 2)
            fn(F1, F1, ACT.Exp, scale=-1.0).then_inc(f_exp, 1)
            sigmoid(4)
            to_conv(5)
            sigmoid(5)

            dest = {"KT": ktok, "VT": vtok, "AT": AT, "TN": T, "NT": TTm, "WT": WT, "U": U}
            for what, *which in ORDER:
                if what == "job" and on_act(tuple(which)):
                    name, h = which
                    act.wait_ge(dn_pe, JOB[(name, h)] + 1)
                    kind = name.rstrip("0123456789")
                    if kind == "WT" and h == 0:
                        act.wait_ge(lt_ready, 2 * len(LEVELS))
                    bank = bank_q((name, h))[1]
                    if kind == "O":
                        ins = copy(oT[C:P, :, h * C:(h + 1) * C],
                                   bank[:, 0:HP * C].rearrange("p (s n) -> p s n", n=C))
                    else:
                        ins = copy(dest[kind][C:P, h * HALF:(h + 1) * HALF],
                                   bank.rearrange("p (s n) -> p s n", n=C))
                    ins.then_inc(dn_act, 1)
                elif what == "in" and which[1] == 1:
                    g = which[0]
                    kind = GROUPS[g][0]
                    n = wuse("in", g)[0]
                    act.wait_ge(w_done, n + 1)
                    v = ps[:, n % 2, :].rearrange("p (b n) -> p b n", b=2)
                    at = 2 * sum(k == kind for k, _ in GROUPS[:g])
                    if kind == "u":
                        ins = copy(ub[:, 0, at:at + 2, UPAD:], v)
                    elif kind == "z":
                        copy(zT[:, at:at + 2], v)
                        after_job(act, ("KK", 1))
                        ins = fn(zsig[:, at:at + 2], v, ACT.Sigmoid)
                    else:
                        ins = fn(gates[:, 1 if kind == "gb" else 0, at:at + 2], v, ACT.Sigmoid)
                    ins.then_inc(w_act, 1)
                elif what == "pool":
                    i = which[0]
                    n = wuse("pool", i)[0]
                    act.wait_ge(w_done, n + 1)
                    if i == 0:
                        act.wait_ge(pooled_ready, 4)
                    for b in range(2):
                        g = 2 * i + b
                        ins = fn(ub[:, 1, g, UPAD:], ps[:, n % 2, b * L:(b + 1) * L], ACT.Copy,
                                 scale=pp("pscale")[:, g:g + 1])
                    ins.then_inc(w_act, 1)
                elif what == "osquare":
                    act.wait_ge(dn_dve, len(JOBS))
                    act.wait_ge(dn_act, act_number(("O", NCH - 1)))
                    fn(sq, oT, ACT.Square).then_inc(sq_ready, 1)
                elif what == "qsum":
                    norm_root(1)
                elif what == "osum":
                    norm_root(2, 1.0 / HD)
            root(2, 0)
            root(3, 1)
            soft = rt[:, 224:288].rearrange("p (t e) -> p t e", t=TT)
            act.wait_ge(soft_in, TT)
            fn(soft, soft, ACT.Exp).then_inc(soft_exp, 1)
            act.wait_ge(combT_done, 1)
            copy(combT, ps[0:E, 6, 128:128 + L]).then_inc(combT_ready, 1)

            def copy_rows(i):
                act.wait_ge(gathered, i + 1)
                copy(xrows, ps[:, 3, :]).then_inc(rows_copied, 1)

            copy_rows(0)

            def expert(i):
                act.wait_ge(gmin_ready, i + 1)
                fn(sig, gmin, ACT.Sigmoid, scale=ALPHA).then_inc(gate_sig, 1)
                act.wait_ge(ct_done, i + 1)
                act.wait_ge(scattered, i + 1)
                copy(ctS, ps[:, 2, 0:L]).then_inc(ct_copied, 1)
                copy_rows(i + 1)
                act.wait_ge(actT_done, i + 1)
                copy(actT, ps[:, 2, :]).then_inc(actT_copied, 1)
                act.wait_ge(wd_used, WD_UNITS * (i + 1))
                copy(outS, ps[:, 3, :]).then_inc(out_copied, 1)

            with act.Fori(0, E) as i:
                expert(i)
            act.wait_ge(flag_ready, 1)
            over = act.value_load(flag[0:1, 0:1], min_val=0, max_val=L)
            with act.If(over > CAP):
                with act.Fori(E, ROUNDS * E) as i:
                    expert(i)
                act.nop()
            for t in range(TT):
                act.wait_ge(ssf_ready, t + 1)
                fn(rstd[:, t:t + 1], ssx[:, t:t + 1], ACT.Sqrt, bias=eps_c, scale=1.0 / D).then_inc(f_sqrt, 1)

        @block.gpsimd
        def _(pool):
            steps = [0]

            def step(ins):
                steps[0] += 1
                ins.then_inc(pool_step, 1)
                pool.wait_ge(pool_step, steps[0])

            tt = pool.tensor_tensor
            pool.memset(cpad[:, :, 0:4], 0.0).then_inc(pads_zeroed, 1)
            pool.wait_ge(tables_landed, 32)
            pool.wait_ge(f_exp, 1)
            tt(F2, F2, rep(cc("upper"), SLOTS), ALU.mult).then_inc(f_ready, 1)
            pool.wait_ge(f_exp, 2)
            step(tt(F1, F1, rep(cc("lower"), SLOTS), ALU.mult))
            tt(F1, F1, bc(colB, C), ALU.mult).then_inc(f_ready, 1)
            step(pool.memset(ub[:, :, :, 0:UPAD], 0.0))
            pool.wait_ge(cols_all, 1)
            for h in range(2):
                after_job(pool, ("KT", h))
                tt(hslots(Kb, h), hslots(ktok, h), bc(bEG[:, h * HALF:(h + 1) * HALF], C), ALU.mult).then_inc(
                    tok_scaled, 1)
                tt(hslots(kd, h), hslots(ktok, h), bc(kdf[:, h * HALF:(h + 1) * HALF], C), ALU.mult).then_inc(
                    tok_scaled, 1)
            for h in range(2):
                after_job(pool, ("VT", h))
                tt(hslots(vtok, h), hslots(vtok, h), bc(colB[:, h * HALF:(h + 1) * HALF], C), ALU.mult).then_inc(
                    tok_scaled, 1)
            for h in range(2):
                for src, jobname, m, o_ in ((A, "KK", "m1", T), (AT, "AT", "m1t", TTm)):
                    after_job(pool, (jobname, h))
                    step(tt(hslots(o_, h), hslots(src, h), rep(cc(m), HALF), ALU.mult))
                    tt(hslots(o_, h), rep(eye, HALF), hslots(o_, h), ALU.subtract).then_inc(base_ready, 1)
            for n, b in enumerate(LEVELS):
                for h in range(2):
                    if n >= 2:
                        pool.wait_ge(dn_pe, JOB[(f"M{LEVELS[n - 2]}", h)] + 1)
                    tt(hslots(LT[n % 2], h), hslots(AT, h), rep(cc(f"lt{b}"), HALF), ALU.mult).then_inc(lt_ready, 1)
                if n != len(LEVELS) - 1:
                    continue
                pool.wait_ge(w_act, wuse("in", 7)[1])
                after_job(pool, ("KQ", 1))
                u, s2, W = ub[:, 0], ub[:, 1], UPAD + L
                step(tt(s2[:, :, 1:], u[:, :, 1:], u[:, :, :W - 1], ALU.add))
                step(tt(usum[:, :, 3:], s2[:, 1:, 3:], s2[:, 1:, 1:W - 2], ALU.add))
                step(tt(s2[:, 2:, 7:], usum[:, 1:, 7:], usum[:, 1:, 3:W - 4], ALU.add))
                step(tt(usum[:, 2:, 15:], s2[:, 3:, 15:], s2[:, 3:, 7:W - 8], ALU.add))
                inv = cc("inv").rearrange("p (g n) -> p g n", g=4)
                for g in range(4):
                    s_ = (s2[:, 0], usum[:, 0], s2[:, 2], usum[:, 2])[g]
                    step(tt(s_[:, UPAD:2 * UPAD], s_[:, UPAD:2 * UPAD], inv[:, g], ALU.mult))
                    step(pool.tensor_scalar(s_[:, 2 * UPAD:], s_[:, 2 * UPAD:], 1.0 / POOLS[g], None, ALU.mult))
                    tt(u[:, g, UPAD:], s_[:, UPAD:], u[:, g, UPAD:], ALU.subtract).then_inc(pooled_ready, 1)


INPUTS = ("x", "consts", "params", "w_in", "pool_w", "w_up_a", "w_up_b", "w_out", "w_router",
          "w_gate_up", "b_gate_up", "w_down", "b_down", "g_final")


def kernel(**inputs):
    import concourse.bacc as bacc
    from concourse.bass_utils import run_bass_kernel_spmd

    a = {k: np.asarray(v) for k, v in inputs.items()}

    def rows(v):
        return np.broadcast_to(v.reshape(1, -1), (P, v.size))

    conv = a["conv_w"][0].T.reshape(3, HP, P, TAPS)[[1, 0, 2]].reshape(12, P, TAPS)
    parts = {
        "conv": conv.transpose(1, 0, 2).reshape(P, -1),
        "dn": np.concatenate([a["dn_norm"][0]] * 2)[:, None],
        "pscale": a["pool_scale"][0].reshape(4, P).T,
        "alog": rows(a["a_log"][0]), "dtb": rows(a["dt_bias"][0]), "brouter": rows(a["b_router"][0]),
        "gmix": a["g_mix"][0].reshape(KD, P).T, "gffn": a["g_ffn"][0].reshape(KD, P).T,
    }
    arrays = {
        "x": a["x"][0], "consts": const_table(),
        "params": np.concatenate([parts[k] for k in PARAMS], axis=1), "g_final": a["g_final"][None, :],
    }
    for name in INPUTS:
        if name not in arrays:
            arrays[name] = a[name][0]
    nc = bacc.Bacc("TRN2", target_bir_lowering=False, num_devices=1)
    launch, args = {}, []
    for name in INPUTS:
        v = np.ascontiguousarray(arrays[name])
        launch[f"in_{name}"] = v
        args.append(nc.dram_tensor(f"in_{name}", v.shape, mybir.dt.from_np(v.dtype), kind="ExternalInput").ap())
    out = nc.dram_tensor("out", (L, D), F32, kind="ExternalOutput").ap()
    build_program(nc, *args, out)
    r = run_bass_kernel_spmd(nc, [launch], core_ids=[0])
    return r.results[0]["out"].reshape(1, L, D)
```

```python
from contextlib import ExitStack

import concourse.bass as bass
import numpy as np
from concourse import mybir

F32 = mybir.dt.float32
F32R = mybir.dt.float32r
I32 = mybir.dt.int32
ALU = mybir.AluOpType
ACT = mybir.ActivationFunctionType
AX = mybir.AxisListType

P = 128
D = 1024
L = 256
TT = L // P
KD = D // P
HEADS, HD = 8, 64
HP = HEADS // 2
C = 64
NCH = L // C
SLOTS = HP * NCH
HALF = SLOTS // 2
DN = HEADS * HD
TAPS = 4
POOLS = (2, 4, 8, 16)
UPAD = 16
E = 32
TOP_K = 4
F = D
LIMIT, ALPHA = 7.0, 1.702
EPS = 1e-6
CAP = 64
ROUNDS = L // CAP
UNIT = 2 * D
GU_UNITS = KD
WD_UNITS = F // P // 2
UNITS = GU_UNITS + WD_UNITS
RING = 16
BATCH = 4
GROUP = 4
assert GROUP * UNITS % RING == 0 and E % GROUP == 0
LEVELS = (2, 4, 8, 16, 32)

CONSTS, _at = {}, 0
for _n, _w in (("ident", P), ("tri", P), ("ones_blk", P), ("ones", P), ("before", P), ("iota", P),
               ("eye", C), ("lower", C), ("upper", C), ("m1", C), ("m1t", C),
               ("lt2", C), ("lt4", C), ("lt8", C), ("lt16", C), ("lt32", C), ("inv", 4 * UPAD),
               ("head_sum", HP * HEADS), ("head_row", HP * P)):
    CONSTS[_n] = (_at, _w)
    _at += _w
NCONST = _at
PARAMS, _at = {}, 0
for _n, _w in (("conv", 12 * TAPS), ("dn", 1), ("pscale", 4), ("alog", HEADS), ("dtb", HEADS),
               ("brouter", E), ("gmix", KD), ("gffn", KD)):
    PARAMS[_n] = (_at, _w)
    _at += _w
NPARAM = _at
MARK, GONE = -3.2e38, -3.3e38


def const_table():
    t = np.zeros((P, NCONST), np.float32)
    p = np.arange(P)[:, None]
    j = np.arange(P)[None, :]
    e = np.arange(C)[None, :]
    r, c = p // C, p % C

    def put(name, value):
        a, w = CONSTS[name]
        t[:, a:a + w] = value

    put("ident", p == j)
    put("tri", (r == j // C) & (c <= j % C))
    put("ones_blk", r == j // C)
    put("ones", 1.0)
    put("before", p < j)
    put("iota", np.broadcast_to(j % CAP, (P, P)))
    put("eye", c == e)
    put("lower", e < c)
    put("upper", e >= c)
    put("m1", (c % 2 == 1) & (e == c - 1))
    put("m1t", (e % 2 == 1) & (c == e - 1))
    for b in LEVELS:
        put(f"lt{b}", ((e // b) % 2 == 1) & (c // b == e // b - 1))
    for hp in range(HP):
        a, at = CONSTS["head_sum"][0] + hp * HEADS, CONSTS["head_row"][0] + hp * P
        t[:, a:a + HEADS] = np.arange(HEADS)[None, :] == 2 * hp + r
        t[:, at:at + P] = p == 2 * hp + j // C
    tok = np.arange(UPAD)
    put("inv", np.concatenate([1.0 / np.minimum(tok + 1, w) for w in POOLS])[None, :])
    return t


K0, Q0, V0, Z0, BA0, U0, GA0 = DN, 0, 2 * DN, 3 * DN, 4 * DN, 4 * DN + 16, 4 * DN + 16 + D // 2
GB0 = GA0 + D
GROUPS = ([("k", K0), ("k", K0 + 256), ("q", Q0), ("q", Q0 + 256), ("v", V0), ("v", V0 + 256),
           ("u", U0), ("u", U0 + 256)] + [("gb", GB0 + 256 * i) for i in range(4)]
          + [("z", Z0), ("z", Z0 + 256)] + [("ga", GA0 + 256 * i) for i in range(4)])
W_SLOTS = 4
POOL_GROUPS = 8

WUSE = ([("in", g) for g in range(len(GROUPS))] + [("pool", 0), ("pool", 1)]
        + [("ub", i) for i in range(4)] + [("ua", i) for i in range(4)]
        + [("wo", i) for i in range(4)])
W_ON_DVE = ("ub", "ua", "wo")


def wuse(kind, i):
    n = WUSE.index((kind, i))
    dve = kind in W_ON_DVE
    return n, sum((k in W_ON_DVE) == dve for k, _ in WUSE[:n + 1])


JOBS = ([(n, h) for n in ("KT", "VT", "KK", "KQ", "AT") for h in (0, 1)]
        + [j for b in LEVELS for j in
           [(f"M{b}", 0), (f"M{b}", 1)]
           + ([(f"TN{b}", 0), (f"TN{b}", 1)] if b != LEVELS[-1] else [])
           + [(f"NT{b}", 0), (f"NT{b}", 1)]]
        + [(n, h) for n in ("WT", "U") for h in (0, 1)]
        + [("O", 0), ("DS", 0), ("WS", 1), ("O", 1), ("DS", 1), ("WS", 2), ("O", 2), ("DS", 2),
           ("WS", 3), ("O", 3)])
JOB = {j: n for n, j in enumerate(JOBS)}


def schedule():
    blocks = iter([("in", g, b) for g in range(6, len(GROUPS)) for b in range(2)]
                  + [("pool", i, 1) for i in range(2)] + [("ub", i, 1) for i in range(4)])
    order = []

    def jobs(*names):
        order.extend(("job",) + n for n in names)

    def filler(count=1):
        order.extend(b for b in [next(blocks, None) for _ in range(count)] if b)

    filler()
    order.append(("qsum",))
    filler(2)
    order.append(("qspread",))
    filler(2)
    for name, count in (("KT", 1), ("VT", 1), ("KK", 2)):
        jobs((name, 0), (name, 1))
        filler(count)
    jobs(("KQ", 0), ("KQ", 1), ("AT", 0), ("AT", 1))
    filler()
    for b in LEVELS:
        jobs((f"M{b}", 0), (f"M{b}", 1))
        filler()
        if b != LEVELS[-1]:
            jobs((f"TN{b}", 0), (f"TN{b}", 1))
        jobs((f"NT{b}", 0), (f"NT{b}", 1))
        filler()
    jobs(("WT", 0), ("WT", 1), ("U", 0), ("U", 1))
    filler()
    for n in range(NCH):
        if n:
            jobs(("WS", n))
            filler()
        jobs(("O", n))
        if n < NCH - 1:
            jobs(("DS", n))
            filler()
    order.append(("osquare",))
    filler()
    order.append(("osum",))
    filler()
    order.append(("ospread",))
    filler(30)
    return order


ORDER = schedule()


def on_act(job):
    return job[0][0:2] in ("KT", "VT", "AT", "TN", "NT", "WT", "U", "O")


def act_number(job):
    return sum(on_act(j) for j in JOBS[:JOB[job] + 1])


def build_program(nc, x, consts, params, w_in, pool_w, w_up_a, w_up_b, w_out, w_router,
                  w_gate_up, b_gate_up, w_down, b_down, g_final, out):
    with ExitStack() as ctx:
        below = GU_UNITS * UNIT
        with nc.sbuf_tensor("below_rounded", [P, below], F32):
            with nc.sbuf_tensor("rounded", [P, WD_UNITS * UNIT + (2 + 4 + 8 + 2) * D], F32R) as rounded:
                pass
        place, used = {}, [-below]

        def sb(name, shape, dt=F32):
            place[name] = used[0]
            used[0] += -(-int(np.prod(shape[1:])) // 8) * 8
            return ctx.enter_context(nc.sbuf_tensor(name, shape, dt))

        def rounded_at(name, first, size):
            return rounded[:, place[name] + first:place[name] + first + size]

        def sem(name):
            return ctx.enter_context(nc.semaphore(name))

        ps = ctx.enter_context(nc.psum_tensor("ps", [P, 8, 512], F32))

        ring = sb("ring", [P, UNITS, UNIT])
        hT = sb("hT", [P, KD, L])
        wring = sb("wring", [P, 2, KD, 256])
        wout = sb("wout", [P, KD, D])
        mo = sb("mo", [P, 6144])
        cst = sb("cst", [P, NCONST])
        par = sb("par", [P, NPARAM])
        xs = sb("xs", [P, TT, D])
        gates = mo[:, 0:4096].rearrange("p (s k n) -> p s k n", s=2, k=KD)
        zT = mo[:, 4096:5120].rearrange("p (b n) -> p b n", b=HP)
        TTm = mo[:, 5120:6144].rearrange("p (s n) -> p s n", s=SLOTS)
        ub = sb("ub", [P, 2, 4, UPAD + L])
        wrt = sb("wrt", [P, KD, E])
        state = sb("state", [P, 3, HP, C])
        sm = sb("sm", [P, 512])
        flag = sb("flag", [1, 2], I32)
        scr = ring[:, 0:GU_UNITS, :].rearrange("p u n -> p (u n)")
        CP = 4 + L
        cpad = scr[:, 0:12 * CP].rearrange("p (b n) -> p b n", b=12)
        o = 12 * CP
        cq = scr[:, o:o + 12 * L].rearrange("p (b n) -> p b n", b=12)
        kT, qT, vT = cq[:, 0:4], cq[:, 4:8], cq[:, 8:12]
        o += 12 * L

        def slots(at):
            return scr[:, at:at + SLOTS * C].rearrange("p (s n) -> p s n", s=SLOTS)

        Kb, kd, vtok, F1, F2, A, qkT, egr = (slots(o + i * SLOTS * C) for i in range(8))
        o += 8 * SLOTS * C
        LT = [slots(o), slots(0)]
        AT, N = slots(SLOTS * C), slots(2 * SLOTS * C)
        T, ktok = (wout[:, i].rearrange("p (s n) -> p s n", s=SLOTS) for i in range(2))

        def k_rows(a):
            return a.rearrange("p (k n) -> p k n", k=KD)

        wslot = [wring[:, 0], wring[:, 1]] + [k_rows(ring[:, GU_UNITS + u, :]) for u in (1, 3)]
        w_hi = [k_rows(rounded_at("wout", i * D, 2 * D)) for i in (2, 4)]
        w_lo = [k_rows(rounded_at(name, first, 2 * D)) for name, first in (
            ("wring", 0), ("wring", 2 * D), ("ring", (GU_UNITS + 1) * UNIT),
            ("ring", (GU_UNITS + 3) * UNIT))]
        hT_hi, hT_lo = k_rows(rounded_at("hT", 0, 2 * D)), k_rows(rounded_at("ring", GU_UNITS * UNIT, 2 * D))
        h_full = k_rows(ring[:, GU_UNITS + 2, :])
        wout_hi = k_rows(rounded_at("ring", GU_UNITS * UNIT, KD * D))
        wout_lo = k_rows(rounded_at("wout", 0, KD * D))
        mix_hi, mix_lo = hT_hi, k_rows(rounded_at("mo", 0, 2 * D))
        poolw = wout[:, 6, 0:4 * P].rearrange("p (g n) -> p g n", g=4)
        w_ba = k_rows(wout[:, 6, 4 * P:5 * P])
        WT, U = A, AT
        xn = cq.rearrange("p b n -> p (b n)")[:, 0:TT * D].rearrange("p (t n) -> p t n", t=TT)
        sq = TTm.rearrange("p s n -> p (s n)").rearrange("p (b n) -> p b n", b=HP)
        sg = zT[:, 0:2, :]
        zsig = F1.rearrange("p s n -> p (s n)").rearrange("p (b n) -> p b n", b=HP)
        usum = F2.rearrange("p s n -> p (s n)")[:, 0:3 * (UPAD + L)].rearrange("p (g n) -> p g n", g=3)
        gtri = ub.rearrange("p a b n -> p (a b n)")[:, 0:TT * HEADS * P].rearrange(
            "p (t h n) -> p t h n", t=TT, h=HEADS)
        oT = kT
        S, Sg, vnew = state[:, 0], state[:, 1], state[:, 2]
        upa = wring.rearrange("p s k n -> p (s k n)").rearrange("p (k n) -> p k n", k=4)
        upb = ring[:, GU_UNITS + 2:GU_UNITS + 4, :].rearrange("p u n -> p (u n)").rearrange(
            "p (k n) -> p k n", k=4)
        late_slots = wout.rearrange("p (u a) n -> p u (a n)", a=UNIT // D)

        def unit_slot(u):
            s = u % RING
            return ring[:, s, :] if s < UNITS else late_slots[:, s - UNITS, :]

        zx = ub.rearrange("p a b n -> p (a b n)")
        xn2 = zx[:, 0:2048].rearrange("p (t n) -> p t n", t=TT)
        xe = mo[:, 0:512].rearrange("p (k n) -> p k n", k=KD)
        gmin, sig, act_t, act_a, actT, outS = (mo[:, 512 + 512 * i:1024 + 512 * i] for i in range(6))
        ctS = mo[:, 3584:3840]
        selw = mo[:, 3840:4096].rearrange("p (t n) -> p t n", t=TT)
        sel = mo[:, 4096:4224].rearrange("p (t n) -> p t n", t=TT)
        NPOS = ROUNDS * E + 1
        pos = mo[:, 4224:4224 + TT * NPOS].rearrange("p (t n) -> p t n", t=TT)
        comb = mo[:, 4552:4552 + TT * NPOS].rearrange("p (t n) -> p t n", t=TT)
        combT = mo[0:E, 4864:4864 + L]
        rt = mo[:, 5120:6144]
        h2T = hT
        xrows = hT[:, 0:2].rearrange("p k n -> p (k n)")
        wf = wring.rearrange("p s k n -> p (s k n)")
        b_gu = wf[0:1, 0:2 * F]
        b_dn = wf[0:E, 2 * F:3 * F]
        gfin = wf[:, 3 * F:4 * F]

        def cc(name):
            a, w = CONSTS[name]
            return cst[:, a:a + w]

        def pp(name):
            a, w = PARAMS[name]
            return par[:, a:a + w]

        ident, ones, ones_blk, tri, eye = cc("ident"), cc("ones"), cc("ones_blk"), cc("tri"), cc("eye")
        head_sum, head_row = cc("head_sum"), cc("head_row")
        inv_rows = sm[0:HEADS, 256:512]
        ssx, rstd = sm[:, 0:2], sm[:, 2:4]
        half_ss = sm[:, 6:8]
        eps_c = sm[:, 5:6]
        av, ab, sp_, gtok, beta_t = (sm[:, 16 + 16 * i:32 + 16 * i].rearrange("p (t h) -> p t h", t=TT)
                                     for i in range(5))
        ea = sm[:, 96:104]
        colG, colB, colL, eG, bEG, kdf, egl = (sm[:, 112 + 16 * i:128 + 16 * i] for i in range(7))

        x_landed = [sem(f"x_landed{t}") for t in range(TT)]
        tables_landed = sem("tables_landed")
        small_landed = sem("small_landed")
        w_landed = [sem(f"w_landed{s}") for s in range(W_SLOTS)]
        upa_landed, upb_landed = sem("upa_landed"), sem("upb_landed")
        wout_landed = [sem(f"wout_landed{h}") for h in range(2)]
        late_landed = sem("late_landed")
        out_landed = sem("out_landed")
        pads_zeroed = sem("pads_zeroed")
        ss_ready, var_sqrt = sem("ss_ready"), sem("var_sqrt")
        h_hi_act, h_hi_dve, h_split = sem("h_hi_act"), sem("h_hi_dve"), sem("h_split")
        w_hi_ready, w_lo_pool, w_lo_dve = sem("w_hi_ready"), sem("w_lo_pool"), sem("w_lo_dve")
        wout_hi_ready, wout_lo_pool, wout_lo_dve = sem("wout_hi_ready"), sem("wout_lo_pool"), sem("wout_lo_dve")
        wout_used = sem("wout_used")
        mix_hi_ready, mix_lo_ready = sem("mix_hi_ready"), sem("mix_lo_ready")
        xn_ready, xT_done, hT_ready = sem("xn_ready"), sem("xT_done"), sem("hT_ready")
        w_done, w_act, w_dve = sem("w_done"), sem("w_act"), sem("w_dve")
        conv_ready, sig_ready, silu_ready = sem("conv_ready"), sem("sig_ready"), sem("silu_ready")
        sq_ready, sumsq_done, norm_sqrt, normed = (sem("sq_ready"), sem("sumsq_done"),
                                                   sem("norm_sqrt"), sem("normed"))
        ba_done, ba_read, sp_exp, decay_act = sem("ba_done"), sem("ba_read"), sem("sp_exp"), sem("decay_act")
        g_ready, cols_done, cols_ready, cols_exp, cols_all = (sem("g_ready"), sem("cols_done"),
                                                              sem("cols_ready"), sem("cols_exp"), sem("cols_all"))
        rows_done, rows_exp, rows_diff, f_exp, f_ready = (sem("rows_done"), sem("rows_exp"),
                                                          sem("rows_diff"), sem("f_exp"), sem("f_ready"))
        dn_pe, dn_dve, dn_act = sem("dn_pe"), sem("dn_dve"), sem("dn_act")
        tok_scaled, lt_ready = sem("tok_scaled"), sem("lt_ready")
        base_ready, base_t_ready = sem("base_ready"), sem("base_t_ready")
        qg_ready, s_ready = sem("qg_ready"), sem("s_ready")
        z_ready, pooled_ready, pool_step = sem("z_ready"), sem("pooled_ready"), sem("pool_step")
        inv_ready, norms_spread, o_ready = sem("inv_ready"), sem("norms_spread"), sem("o_ready")
        mix_ready, xn2_ready = sem("mix_ready"), sem("xn2_ready")
        x2T_done, h2T_ready, logits_done = sem("x2T_done"), sem("h2T_ready"), sem("logits_done")
        soft_in, soft_exp, mask_ready, count_done = (
            sem("soft_in"), sem("soft_exp"), sem("mask_ready"), sem("count_done"))
        combT_done, combT_ready, zero_ready = sem("combT_done"), sem("combT_ready"), sem("zero_ready")
        flag_ready = sem("flag_ready")
        dve_step = sem("dve_step")
        act_step = sem("act_step")
        unit_landed = [sem(f"unit_landed{s}") for s in range(RING)]
        bias_landed = sem("bias_landed")
        unit_used, bias_used = sem("unit_used"), sem("bias_used")
        sel_ready, selw_ready, gathered, xe_ready = sem("sel_ready"), sem("selw_ready"), sem("gathered"), sem("xe_ready")
        gmin_ready, gate_sig, gu_read, act_ready = sem("gmin_ready"), sem("gate_sig"), sem("gu_read"), sem("act_ready")
        ct_done, ct_copied, actT_done, actT_copied = sem("ct_done"), sem("ct_copied"), sem("actT_done"), sem("actT_copied")
        out_copied, scattered = sem("out_copied"), sem("scattered")
        up_ready, rows_copied, turned = sem("up_ready"), sem("rows_copied"), sem("turned")
        y_ready, ssf_ready, f_sqrt, fin_ready = sem("y_ready"), sem("ssf_ready"), sem("f_sqrt"), sem("fin_ready")

        def bank_q(job):
            r = JOB[job] % 3
            return [ps[0:C, 2 + 2 * r, :], ps[C:P, 3 + 2 * r, :]]

        def after_job(eng, job):
            eng.wait_ge(dn_dve, JOB[job] + 1)
            if on_act(job):
                eng.wait_ge(dn_act, act_number(job))

        def flat_banks(first, n):
            return ps[:, first:first + 2, :].rearrange("p b m -> p (b m)").rearrange(
                "p (s n) -> p s n", n=n)

        def hslots(a, h):
            return a[:, h * HALF:(h + 1) * HALF, :]

        def bc(a, n):
            return a.unsqueeze(2).to_broadcast([a.shape[0], a.shape[1], n])

        def rep(a, m):
            return a.unsqueeze(1).to_broadcast([a.shape[0], m, a.shape[1]])

        def chunk(a, n):
            return a.rearrange("p (hp n) c -> p hp n c", hp=HP)[:, :, n, :]

        def low_part(eng, g, ready):
            for b in range(2):
                eng.wait_ge(w_hi_ready, 2 * g + b + 1)
                c = slice(b * P, (b + 1) * P)
                eng.tensor_tensor(w_lo[g % W_SLOTS][:, :, c], wslot[g % W_SLOTS][:, :, c],
                                  w_hi[g % 2][:, :, c].bitcast(F32), ALU.subtract).then_inc(ready, 1)

        def wout_low(eng, k, ready):
            eng.wait_ge(wout_hi_ready, k + 1)
            eng.tensor_tensor(wout_lo[:, k], wout[:, k], wout_hi[:, k].bitcast(F32), ALU.subtract).then_inc(ready, 1)

        block = ctx.enter_context(nc.Block())

        @block.sync
        def _(sp):
            for t in range(TT):
                sp.dma_start(xs[:, t], x[t * P:(t + 1) * P, :]).then_inc(x_landed[t], 16)
            sp.dma_start(cst[:], consts).then_inc(tables_landed, 16)
            sp.dma_start(par[:], params).then_inc(tables_landed, 16)
            w_rows = w_in.rearrange("(k p) n -> p k n", p=P)

            def load_group(g):
                if g >= W_SLOTS:
                    sp.wait_ge(w_done, wuse("in", g - W_SLOTS)[0] + 1)
                col = GROUPS[g][1]
                sp.dma_start(wslot[g % W_SLOTS], w_rows[:, :, col:col + 256]).then_inc(
                    w_landed[g % W_SLOTS], 16)

            load_group(0)
            sp.dma_start(w_ba, w_rows[:, :, BA0:BA0 + 2 * HEADS]).then_inc(small_landed, 16)
            load_group(1)
            sp.dma_start(poolw, pool_w.rearrange("g c d -> c g d")).then_inc(small_landed, 16)
            sp.dma_start(wrt[:], w_router.rearrange("(k p) e -> p k e", p=P)).then_inc(small_landed, 16)
            for g in range(2, len(GROUPS)):
                load_group(g)
                if g == len(GROUPS) - 1:
                    sp.wait_ge(w_done, wuse("in", g - 2)[0] + 1)
                    sp.dma_start(upb, w_up_b.rearrange("(k p) n -> p k n", p=P)).then_inc(upb_landed, 16)

            def load_unit(e, u, slot):
                if u < GU_UNITS:
                    ins = sp.dma_start(unit_slot(slot), w_gate_up[bass.ds(e, 1), u * P:(u + 1) * P, :].rearrange(
                        "a p n -> p (a n)"))
                else:
                    k = 2 * (u - GU_UNITS)
                    ins = sp.dma_start(
                        unit_slot(slot).rearrange("p (k n) -> p k n", k=2),
                        w_down[bass.ds(e, 1), k * P:(k + 2) * P, :].rearrange("a (k p) n -> p (a k) n", p=P))
                ins.then_inc(unit_landed[slot % RING], 16)

            def load_bias(e):
                sp.dma_start(b_gu, b_gate_up[bass.ds(e, 1), :]).then_inc(bias_landed, 16)

            sp.wait_ge(w_done, wuse("pool", 1)[0] + 1)
            for a in (0, 4):
                sp.dma_start(wout[:, a:a + 4], w_out.rearrange("(k p) n -> p k n", p=P)[
                    :, a:a + 4, :]).then_inc(wout_landed[a // 4], 16)
            sp.dma_start(upa, w_up_a.rearrange("(k p) n -> p k n", p=P)).then_inc(upa_landed, 16)
            sp.wait_ge(o_ready, HP)
            for u in range(GU_UNITS):
                load_unit(0, u, u)
            sp.wait_ge(w_done, wuse("ua", 3)[0] + 1)
            load_bias(0)
            sp.dma_start(b_dn, b_down).then_inc(late_landed, 16)
            sp.dma_start(gfin, g_final.to_broadcast([P, D])).then_inc(late_landed, 16)
            for u in range(RING - UNITS):
                sp.wait_ge(wout_used, u + 1)
                load_unit(1, u, UNITS + u)
            for u in range(GU_UNITS, UNITS):
                if u < UNITS - 1:
                    sp.wait_ge(wout_used, RING - UNITS + u - GU_UNITS + 1)
                else:
                    sp.wait_ge(w_done, wuse("wo", 3)[0] + 1)
                load_unit(0, u, u)

            def load_expert(g, m, e, first=0):
                for u in range(first, UNITS):
                    n = UNITS * m + u
                    if u == RING - UNITS:
                        sp.wait_ge(bias_used, GROUP * g + m)
                        load_bias(e)
                    sp.wait_ge(unit_used, GROUP * UNITS * g + n - RING + 1)
                    load_unit(e, u, n)

            load_expert(0, 1, 1, RING - UNITS)
            for m in range(2, GROUP):
                load_expert(0, m, m)
            with sp.Fori(1, E // GROUP) as g:
                for m in range(GROUP):
                    load_expert(g, m, GROUP * g + m)
            sp.wait_ge(flag_ready, 2)
            over = sp.value_load(flag[0:1, 0:1], min_val=0, max_val=L)
            with sp.If(over > CAP):
                with sp.Fori(1, ROUNDS) as r:
                    with sp.Fori(0, E // GROUP) as g:
                        for m in range(GROUP):
                            load_expert(r * (E // GROUP) + g, m, GROUP * g + m)
                sp.nop()
            for t in range(TT):
                sp.wait_ge(fin_ready, t + 1)
                sp.dma_start(out[t * P:(t + 1) * P, :], xn2[:, t]).then_inc(out_landed, 16)
            sp.wait_ge(out_landed, 16 * TT)

        @block.tensor
        def _(pe):
            def bank_free(kind, i):
                n = wuse(kind, i)[0]
                if n >= 2:
                    k2, i2 = WUSE[n - 2]
                    pe.wait_ge(w_dve if k2 in W_ON_DVE else w_act, wuse(k2, i2)[1])
                return n % 2

            def project(g, b):
                bank = bank_free("in", g)
                o_ = ps[:, bank, b * L:(b + 1) * L]
                hi, lo = w_hi[g % 2][:, :, b * P:(b + 1) * P], w_lo[g % W_SLOTS][:, :, b * P:(b + 1) * P]
                pe.wait_ge(w_hi_ready, 2 * g + b + 1)
                for k in range(KD):
                    pe.matmul(o_, hi[:, k], hT_hi[:, k, :], start=k == 0, stop=False)
                if g < POOL_GROUPS:
                    pe.wait_ge(w_lo_pool, 2 * g + b + 1)
                else:
                    pe.wait_ge(w_lo_dve, 2 * (g - POOL_GROUPS) + b + 1)
                for k in range(KD):
                    pe.matmul(o_, lo[:, k], hT_hi[:, k, :], start=False, stop=False)
                if (g, b) == (0, 0):
                    pe.wait_ge(h_split, 4)
                for k in range(KD):
                    mm = pe.matmul(o_, hi[:, k], hT_lo[:, k, :], start=False, stop=k == KD - 1)
                if b == 1:
                    mm.then_inc(w_done, 1)

            def job(name, h):
                j = JOB[(name, h)]
                if j >= 3:
                    after_job(pe, JOBS[j - 3])
                banks = bank_q((name, h))
                level = name.lstrip("MTN")
                if name in ("WS", "O", "DS"):
                    n = h
                    if name == "WS":
                        pe.wait_ge(s_ready, n)
                    if name == "DS" or name == "O":
                        if n == 0:
                            after_job(pe, ("U", 0))
                            after_job(pe, ("U", 1))
                        else:
                            after_job(pe, ("WS", n))
                    if name == "O" and n == 0:
                        pe.wait_ge(qg_ready, 1)
                    vn = chunk(U, 0) if n == 0 else vnew
                    for hp in range(HP):
                        for q in range(2):
                            r = slice(q * C, (q + 1) * C)
                            o_ = banks[q][:, hp * C:(hp + 1) * C]
                            if name == "WS":
                                mm = pe.matmul(o_, chunk(WT, n)[r, hp], S[r, hp], start=True, stop=True)
                            elif name == "DS":
                                mm = pe.matmul(o_, chunk(kd, n)[r, hp], vn[r, hp], start=True, stop=True)
                            else:
                                if n:
                                    pe.matmul(o_, S[r, hp], chunk(egr, n)[r, hp], start=True, stop=False)
                                mm = pe.matmul(o_, vn[r, hp], chunk(qkT, n)[r, hp], start=n == 0, stop=True)
                    mm.then_inc(dn_pe, 1)
                    return
                if (name, h) == ("KT", 0):
                    pe.wait_ge(normed, 2 * HP)
                    pe.wait_ge(rows_diff, 1)
                    pe.wait_ge(rows_exp, 1)
                if name == "VT":
                    pe.wait_ge(silu_ready, 6)
                if (name, h) == ("VT", 0):
                    pe.wait_ge(cols_ready, 1)
                if name == "KQ":
                    pe.wait_ge(normed, 2 * HP)
                if name == "AT":
                    after_job(pe, ("KK", h))
                if name[0] == "M":
                    pe.wait_ge(base_ready, h + 1)
                    pe.wait_ge(lt_ready, 2 * LEVELS.index(int(level)) + h + 1)
                    if level != "2":
                        after_job(pe, (f"TN{int(level) // 2}", h))
                if name[0:2] in ("TN", "NT"):
                    pe.wait_ge(base_t_ready, h + 1)
                    after_job(pe, (f"M{level}", h))
                    if level != "2":
                        after_job(pe, (f"NT{int(level) // 2}", h))
                if name in ("WT", "U"):
                    after_job(pe, ("NT32", h))
                    pe.wait_ge(tok_scaled, 3 * (h + 1))
                for s in range(HALF):
                    sl = h * HALF + s
                    hp, n = sl // NCH, sl % NCH
                    tok = slice(n * C, (n + 1) * C)
                    for q in range(2):
                        r = slice(q * C, (q + 1) * C)
                        lt = LT[LEVELS.index(int(level)) % 2] if name[0] == "M" else None
                        a, b = {
                            "KT": lambda: (kT[r, hp, tok], eye[r]), "VT": lambda: (vT[r, hp, tok], eye[r]),
                            "KK": lambda: (kT[r, hp, tok], kT[r, hp, tok]),
                            "KQ": lambda: (kT[r, hp, tok], qT[r, hp, tok]),
                            "AT": lambda: (A[r, sl], eye[r]), "M": lambda: (lt[r, sl], T[r, sl]),
                            "TN": lambda: (TTm[r, sl], N[r, sl]), "NT": lambda: (N[r, sl], TTm[r, sl]),
                            "WT": lambda: (Kb[r, sl], TTm[r, sl]), "U": lambda: (TTm[r, sl], vtok[r, sl]),
                        }[name.rstrip("0123456789")]()
                        mm = pe.matmul(banks[q][:, s * C:(s + 1) * C], a, b, start=True, stop=True)
                mm.then_inc(dn_pe, 1)

            pe.wait_ge(tables_landed, 32)
            for t in range(TT):
                pe.wait_ge(xn_ready, t + 1)
                for k in range(KD):
                    mm = pe.transpose(ps[:, 2 + 2 * t + k // 4, (k % 4) * P:(k % 4 + 1) * P],
                                      xn[:, t, k * P:(k + 1) * P], ident)
                    if k % 4 == 3:
                        mm.then_inc(xT_done, 1)
            pe.wait_ge(h_hi_act, 2)
            pe.wait_ge(h_hi_dve, 2)

            def group(g):
                project(g, 0)
                project(g, 1)

            def sums_of_squares(i):
                pe.wait_ge(sq_ready, i + 1)
                if i:
                    pe.wait_ge(norm_sqrt, i)
                for hp in range(HP):
                    mm = pe.matmul(ps[0:HEADS, 7, 0:L], head_sum[:, hp * HEADS:(hp + 1) * HEADS],
                                   sq[:, hp], start=hp == 0, stop=hp == HP - 1)
                mm.then_inc(sumsq_done, 1)

            def spread_norms(i):
                pe.wait_ge(inv_ready, i + 1)
                if i == 1:
                    pe.wait_ge(normed, HP)
                for hp in range(HP):
                    mm = pe.matmul(ps[:, (2, 2, 6)[i] + hp // 2, (hp % 2) * L:(hp % 2 + 1) * L],
                                   head_row[0:HEADS, hp * P:(hp + 1) * P], inv_rows, start=True, stop=True)
                mm.then_inc(norms_spread, 1)

            group(0)
            pe.wait_ge(small_landed, 48)
            for t in range(TT):
                for k in range(KD):
                    mm = pe.matmul(ps[:, 6, t * 16:t * 16 + 16], h_full[:, k, t * P:(t + 1) * P], w_ba[:, k],
                                   start=k == 0, stop=k == KD - 1)
            mm.then_inc(ba_done, 1)
            group(1)
            group(2)
            group(3)
            pe.wait_ge(g_ready, 1)
            pe.wait_ge(decay_act, 1)
            for t in range(TT):
                for r in range(2):
                    n = 2 * t + r
                    for q in range(2):
                        for i, (m, v) in enumerate(((tri, gtok), (ident, beta_t), (ones_blk, gtok))):
                            o_ = ps[q * C:(q + 1) * C, 6, 64 + 16 * i:80 + 16 * i].rearrange(
                                "p (hp n) -> p hp n", hp=HP)[:, :, n]
                            mm = pe.matmul(o_, m[:, r * C:(r + 1) * C],
                                           v[:, t].rearrange("p (hp q) -> p hp q", q=2)[:, :, q],
                                           start=True, stop=True)
            mm.then_inc(cols_done, 1)
            sums_of_squares(0)
            group(4)
            pe.wait_ge(g_ready, 2)
            for hp in range(HP):
                for t in range(TT):
                    for q in range(2):
                        mm = pe.matmul(ps[q * C:(q + 1) * C, 4 + hp // 2,
                                          (hp % 2) * L + t * P:(hp % 2) * L + (t + 1) * P],
                                       ones[:, 0:C], gtri[:, t, 2 * hp + q], start=True, stop=True)
            mm.then_inc(rows_done, 1)
            group(5)
            spread_norms(0)

            def up_project(kind, i, w, v):
                bank = bank_free(kind, i)
                for b in range(2):
                    m = 2 * i + b
                    for k in range(4):
                        mm = pe.matmul(ps[:, bank, b * L:(b + 1) * L], w[:, k, m * P:(m + 1) * P],
                                       v[:, k], start=k == 0, stop=k == 3)
                mm.then_inc(w_done, 1)

            for what, *which in ORDER:
                if what == "job":
                    job(*which)
                elif what == "in":
                    project(*which)
                elif what == "pool":
                    i = which[0]
                    bank = bank_free("pool", i)
                    pe.wait_ge(pooled_ready, 4)
                    for g in (2 * i, 2 * i + 1):
                        mm = pe.matmul(ps[:, bank, (g % 2) * L:(g % 2 + 1) * L], poolw[:, g],
                                       ub[:, 0, g, UPAD:], start=True, stop=True)
                    mm.then_inc(w_done, 1)
                elif what == "ub":
                    if which[0] == 0:
                        pe.wait_ge(upb_landed, 16)
                        pe.wait_ge(w_act, wuse("pool", 1)[1])
                    up_project("ub", which[0], upb, ub[:, 1, :, UPAD:])
                elif what == "qsum":
                    sums_of_squares(1)
                elif what == "qspread":
                    spread_norms(1)
                elif what == "ospread":
                    spread_norms(2)
                elif what == "osum":
                    sums_of_squares(2)
            pe.wait_ge(upa_landed, 16)
            pe.wait_ge(o_ready, HP)
            for i in range(4):
                up_project("ua", i, upa, zT)

            def mix_out(i):
                t, c = i // 2, i % 2
                bank = bank_free("wo", i)
                o_, rows, cols = ps[:, bank, :], slice(t * P, (t + 1) * P), slice(c * 512, (c + 1) * 512)
                def low_weights(start):
                    for k in range(KD):
                        if i == 0:
                            if k < KD // 2:
                                pe.wait_ge(wout_lo_pool, k + 1)
                            else:
                                pe.wait_ge(wout_lo_dve, k - KD // 2 + 1)
                        mm = pe.matmul(o_, mix_hi[:, k, rows], wout_lo[:, k, cols], start=start and k == 0,
                                       stop=False)
                        if i == 3 and k % 2 == 1:
                            mm.then_inc(wout_used, 1)

                if i == 3:
                    low_weights(True)
                    for k in range(KD):
                        pe.matmul(o_, mix_hi[:, k, rows], wout_hi[:, k, cols], start=False, stop=False)
                        mm = pe.matmul(o_, mix_lo[:, k, rows], wout_hi[:, k, cols], start=False, stop=k == KD - 1)
                        if k % 2 == 1 and k < KD - 1:
                            mm.then_inc(wout_used, 1)
                    mm.then_inc(w_done, 1)
                    return
                for k in range(KD):
                    if i == 0:
                        pe.wait_ge(mix_hi_ready, k // 2 + 1)
                        pe.wait_ge(wout_hi_ready, k + 1)
                    pe.matmul(o_, mix_hi[:, k, rows], wout_hi[:, k, cols], start=k == 0, stop=False)
                low_weights(False)
                for k in range(KD):
                    if i == 0:
                        pe.wait_ge(mix_lo_ready, k // 2 + 1)
                    mm = pe.matmul(o_, mix_lo[:, k, rows], wout_hi[:, k, cols], start=False, stop=k == KD - 1)
                mm.then_inc(w_done, 1)

            def turn(t):
                pe.wait_ge(xn2_ready, t + 1)
                for k in range(KD):
                    mm = pe.transpose(ps[:, 2 + 2 * t + k // 4, (k % 4) * P:(k % 4 + 1) * P],
                                      xn2[:, t, k * P:(k + 1) * P], ident)
                    if k % 4 == 3:
                        mm.then_inc(x2T_done, 1)

            def route(t):
                for k in range(KD):
                    if k % 4 == 0:
                        pe.wait_ge(h2T_ready, 2 * t + k // 4 + 1)
                    mm = pe.matmul(ps[:, 6 + t, 0:E], h2T[:, k, t * P:(t + 1) * P], wrt[:, k],
                                   start=k == 0, stop=k == KD - 1)
                mm.then_inc(logits_done, 1)

            mix_out(0)
            mix_out(1)
            mix_out(2)
            turn(0)
            mix_out(3)
            route(0)
            turn(1)
            route(1)
            mask = rt[:, 64:64 + TT * E].rearrange("p (t e) -> p t e", t=TT)
            pe.wait_ge(mask_ready, 1)
            pe.matmul(ps[:, 2, 0:E], cc("before"), mask[:, 0], start=True, stop=True)
            pe.matmul(ps[:, 2, E:2 * E], ones, mask[:, 0], start=True, stop=False)
            pe.matmul(ps[0:1, 3, 0:E], ones[:, 0:1], mask[:, 0], start=True, stop=False)
            pe.wait_ge(mask_ready, 2)
            pe.matmul(ps[:, 2, E:2 * E], cc("before"), mask[:, 1], start=False, stop=True).then_inc(
                count_done, 1)
            pe.matmul(ps[0:1, 3, 0:E], ones[:, 0:1], mask[:, 1], start=False, stop=True).then_inc(
                count_done, 1)

            def y(t, c):
                return ps[:, 4 + 2 * t + c, :]

            def gather(i, first=False):
                pe.wait_ge(sel_ready, i + 1)
                if first:
                    pe.wait_ge(flag_ready, 1)
                for t in range(TT):
                    for c in range(2):
                        mm = pe.matmul(ps[c * CAP:(c + 1) * CAP, 3, :], sel[:, t, :],
                                       xn2[:, t, c * 512:(c + 1) * 512], start=t == 0, stop=t == TT - 1)
                mm.then_inc(gathered, 1)

            def turn_gathered(i):
                pe.wait_ge(rows_copied, i + 1)
                for j in range(4):
                    mm = pe.transpose(ps[:, 3, j * P:(j + 1) * P], xrows[:, j * P:(j + 1) * P], ident)
                mm.then_inc(turned, 1)

            def scatter():
                for t in range(TT):
                    for c in range(2):
                        r = slice(c * CAP, (c + 1) * CAP)
                        mm = pe.matmul(y(t, c), ctS[r, t * P:(t + 1) * P], outS[r, :],
                                       start=False, stop=False, skip_group_check=True)
                    mm.then_inc(scattered, 1)

            def start_gate_up(i, chunks=range(4)):
                pe.wait_ge(bias_landed, 16 * (i + 1))
                for a in chunks:
                    r = slice((a % 2) * CAP, (a % 2 + 1) * CAP)
                    mm = pe.matmul(ps[r, a // 2, :], ones[0:1, 0:CAP], b_gu[:, a * 512:(a + 1) * 512],
                                   start=True, stop=False)
                if chunks[-1] == 3:
                    mm.then_inc(bias_used, 1)

            def start_y():
                pe.wait_ge(combT_ready, 1)
                pe.wait_ge(late_landed, 32)
                for t in range(TT):
                    for c in range(2):
                        mm = pe.matmul(y(t, c), combT[:, t * P:(t + 1) * P], b_dn[:, c * 512:(c + 1) * 512],
                                       start=True, stop=False, skip_group_check=True)
                    mm.then_inc(scattered, 1)

            def wait_units(g, n, k, batch):
                if k % batch == 0:
                    for m in range(n, n + batch):
                        pe.wait_ge(unit_landed[m % RING], 16 * (GROUP * UNITS // RING * g + m // RING + 1))

            def expert(g, m, first=False, more=True):
                i = GROUP * g + m
                if not first:
                    start_gate_up(i)
                pe.wait_ge(xe_ready, i + 1)
                for k in range(GU_UNITS):
                    n = UNITS * m + k
                    wait_units(g, n, k, BATCH if more else 1)
                    for a in range(4):
                        r = slice((a % 2) * CAP, (a % 2 + 1) * CAP)
                        mm = pe.matmul(ps[r, a // 2, :], xe[:, k, :], unit_slot(n)[:, a * 512:(a + 1) * 512],
                                       start=False, stop=k == GU_UNITS - 1)
                    mm.then_inc(unit_used, 1)
                pe.wait_ge(selw_ready, i + 1)
                for t in range(TT):
                    mm = pe.transpose(ps[:, 2, t * P:(t + 1) * P], selw[:, t, :], ident)
                mm.then_inc(ct_done, 1)
                if first:
                    start_y()
                else:
                    pe.wait_ge(out_copied, i)
                    scatter()
                if more:
                    gather(i + 1)
                pe.wait_ge(ct_copied, i + 1)
                pe.wait_ge(act_ready, i + 1)
                for j in range(4):
                    mm = pe.transpose(ps[:, 2, j * P:(j + 1) * P], act_a[:, j * P:(j + 1) * P], ident)
                mm.then_inc(actT_done, 1)
                if more:
                    turn_gathered(i + 1)
                pe.wait_ge(actT_copied, i + 1)
                if more:
                    pe.wait_ge(xe_ready, i + 2)
                for k in range(KD):
                    n = UNITS * m + GU_UNITS + k // 2
                    if k % 2 == 0:
                        wait_units(g, n, k // 2, BATCH if more else 1)
                    half, j = k // 4, k % 4
                    lhs = actT[:, j * P + half * CAP:j * P + (half + 1) * CAP]
                    for c in range(2):
                        w = unit_slot(n)[:, (k % 2) * D + c * 512:(k % 2) * D + (c + 1) * 512]
                        mm = pe.matmul(ps[c * CAP:(c + 1) * CAP, 3, :], lhs, w, start=k == 0, stop=k == KD - 1)
                    if k % 2 == 1:
                        mm.then_inc(unit_used, 1)

            start_gate_up(0, (0, 1))
            gather(0, first=True)
            start_gate_up(0, (2, 3))
            turn_gathered(0)
            for t in range(TT):
                mm = pe.transpose(ps[0:E, 6, 128 + t * P:128 + (t + 1) * P], comb[:, t, 0:E], ident)
            mm.then_inc(combT_done, 1)
            last = E // GROUP - 1
            for m in range(GROUP):
                expert(0, m, first=m == 0)
            with pe.Fori(1, last) as g:
                for m in range(GROUP):
                    expert(g, m)
            for m in range(GROUP):
                expert(last, m, more=m < GROUP - 1)
            pe.wait_ge(flag_ready, 2)
            over = pe.value_load(flag[0:1, 0:1], min_val=0, max_val=L)
            with pe.If(over > CAP):
                pe.wait_ge(out_copied, E)
                gather(E)
                turn_gathered(E)
                with pe.Fori(last + 1, ROUNDS * E // GROUP - 1) as g:
                    for m in range(GROUP):
                        expert(g, m)
                for m in range(GROUP):
                    expert(ROUNDS * E // GROUP - 1, m, more=m < GROUP - 1)
                pe.wait_ge(out_copied, ROUNDS * E)
            pe.wait_ge(out_copied, E)
            scatter()

        @block.vector
        def _(dve):
            steps = [0]

            def step(ins):
                steps[0] += 1
                ins.then_inc(dve_step, 1)
                dve.wait_ge(dve_step, steps[0])

            def add_scaled(o_, a, s, b, o0=ALU.mult, o1=ALU.add):
                return dve.scalar_tensor_tensor(out=o_, in0=a, scalar=s, in1=b, op0=o0, op1=o1)

            dve.memset(eps_c, EPS).then_inc(zero_ready, 1)
            junk = zT.rearrange("p b n -> p (b n)")

            def square_sum(v, o_):
                return dve.tensor_tensor_reduce(out=junk[:, 0:v.shape[1]], in0=v, in1=v, scale=1.0, scalar=0.0,
                                                op0=ALU.mult, op1=ALU.add, accum_out=o_)

            def mean_square(t):
                step(square_sum(xs[:, t], ssx[:, t:t + 1]))
                dve.tensor_scalar(ssx[:, t:t + 1], ssx[:, t:t + 1], 1.0 / D, EPS, ALU.mult, ALU.add).then_inc(
                    ss_ready, 1)

            def scale_rows(n, t, o_, ready):
                dve.wait_ge(var_sqrt, n + 1)
                step(dve.reciprocal(rstd[:, t:t + 1], rstd[:, t:t + 1]))
                dve.tensor_scalar(o_[:, t], xs[:, t], rstd[:, t:t + 1], None, ALU.mult).then_inc(ready, 1)

            for t in range(TT):
                dve.wait_ge(x_landed[t], 16)
                mean_square(t)
            for t in range(TT):
                scale_rows(t, t, xn, xn_ready)
            dve.wait_ge(tables_landed, 32)
            for t in range(TT):
                for h in range(2):
                    dve.wait_ge(xT_done, 2 * t + h + 1)
                    dve.tensor_tensor(
                        h_full[:, 4 * h:4 * h + 4, t * P:(t + 1) * P],
                        ps[:, 2 + 2 * t + h, :].rearrange("p (k n) -> p k n", k=4),
                        bc(pp("gmix")[:, 4 * h:4 * h + 4], P), ALU.mult).then_inc(hT_ready, 1)

            for h in range(2):
                dve.wait_ge(hT_ready, 2 + h + 1)
                part = (slice(None), slice(4 * h, 4 * h + 4), slice(P, 2 * P))
                dve.tensor_copy(hT_hi[part], h_full[part]).then_inc(h_hi_dve, 1)
            for t in range(TT):
                for h in range(2):
                    dve.wait_ge((h_hi_act, h_hi_dve)[t], h + 1)
                    part = (slice(None), slice(4 * h, 4 * h + 4), slice(t * P, (t + 1) * P))
                    dve.tensor_tensor(hT_lo[part], h_full[part], hT_hi[part].bitcast(F32),
                                      ALU.subtract).then_inc(h_split, 1)

            conv = pp("conv").rearrange("p (b j) -> p b j", b=12)

            def convolve(g):
                dve.wait_ge(w_act, g + 1)
                if g == 0:
                    dve.wait_ge(pads_zeroed, 1)
                for b in (2 * g, 2 * g + 1):
                    step(dve.tensor_scalar(cq[:, b], cpad[:, b, 1:1 + L], conv[:, b, 0:1], None, ALU.mult))
                    for j in range(1, TAPS):
                        ins = add_scaled(cq[:, b], cpad[:, b, 1 + j:1 + j + L], conv[:, b, j:j + 1], cq[:, b])
                        if j < TAPS - 1:
                            step(ins)
                    ins.then_inc(conv_ready, 1)

            def silu(g):
                dve.wait_ge(sig_ready, g + 1)
                dve.tensor_tensor(cq[:, 2 * g:2 * g + 2], cq[:, 2 * g:2 * g + 2], sg, ALU.mult).then_inc(
                    silu_ready, 1)

            def invert_norms(i):
                dve.wait_ge(norm_sqrt, i + 1)
                dve.reciprocal(inv_rows, inv_rows).then_inc(inv_ready, 1)

            def spread(i, hp):
                return ps[:, (2, 2, 6)[i] + hp // 2, (hp % 2) * L:(hp % 2 + 1) * L]

            def normalise(i):
                dve.wait_ge(norms_spread, i + 1)
                for hp in range(HP):
                    v = (kT, qT)[i][:, hp]
                    add_scaled(v, v, (1.0, HD ** -0.5)[i], spread(i, hp), ALU.mult, ALU.mult).then_inc(normed, 1)

            convolve(0)
            dve.wait_ge(ba_done, 1)
            bav = ps[:, 6, 0:32].rearrange("p (t n) -> p t n", t=TT)
            step(dve.tensor_tensor(av, bav[:, :, HEADS:], rep(pp("dtb"), TT), ALU.add))
            add_scaled(ab, av, -1.0, av, ALU.mult, ALU.max).then_inc(ba_read, 1)
            convolve(1)
            silu(0)
            silu(1)
            dve.wait_ge(sp_exp, 1)
            step(add_scaled(sp_, av, 0.0, ab, ALU.max, ALU.add))
            add_scaled(gtok, sp_, -1.0, rep(ea, TT), ALU.mult, ALU.mult).then_inc(g_ready, 1)
            dve.wait_ge(g_ready, 1)
            for t in range(TT):
                ins = dve.tensor_tensor(gtri[:, t], rep(tri, HEADS), bc(gtok[:, t], P), ALU.mult)
            ins.then_inc(g_ready, 1)
            convolve(2)
            dve.wait_ge(cols_done, 1)
            dve.tensor_copy(sm[:, 112:160], ps[:, 6, 64:112]).then_inc(cols_ready, 1)
            dve.wait_ge(cols_ready, 1)
            dve.tensor_tensor(kdf, colL, colG, ALU.subtract).then_inc(cols_ready, 1)
            silu(2)
            convolve(3)
            silu(3)
            dve.wait_ge(cols_exp, 1)
            dve.tensor_tensor(bEG, colB, eG, ALU.mult).then_inc(cols_all, 1)
            convolve(4)
            invert_norms(0)
            dve.wait_ge(rows_done, 1)
            diff = Kb
            step(dve.tensor_tensor(diff, flat_banks(4, C),
                                   bc(colG, C), ALU.subtract))
            dve.tensor_scalar(F2, diff, 0.0, None, ALU.min).then_inc(rows_diff, 1)
            dve.tensor_scalar(F1, diff, 0.0, None, ALU.max).then_inc(rows_diff, 1)
            silu(4)
            convolve(5)
            normalise(0)
            silu(5)

            dest = {"KT": ktok, "VT": vtok, "AT": AT, "TN": T, "NT": TTm, "WT": WT, "U": U}

            def empty(name, h):
                banks = bank_q((name, h))
                kind = name.rstrip("0123456789")
                dve.wait_ge(dn_pe, JOB[(name, h)] + 1)
                if kind == "WT" and h == 0:
                    dve.wait_ge(lt_ready, 2 * len(LEVELS))
                if kind in dest:
                    ins = dve.tensor_copy(dest[kind][0:C, h * HALF:(h + 1) * HALF],
                                          banks[0].rearrange("p (s n) -> p s n", n=C))
                elif kind == "O":
                    ins = dve.tensor_copy(oT[0:C, :, h * C:(h + 1) * C],
                                          banks[0][:, 0:HP * C].rearrange("p (s n) -> p s n", n=C))
                elif kind in ("WS", "DS"):
                    for q in range(2):
                        r = slice(q * C, (q + 1) * C)
                        v = banks[q][:, 0:HP * C].rearrange("p (s n) -> p s n", n=C)
                        if kind == "WS":
                            ins = dve.tensor_tensor(vnew[r], chunk(U, h)[r], v, ALU.subtract)
                        elif h == 0:
                            ins = dve.tensor_copy(S[r], v)
                        else:
                            ins = dve.tensor_tensor(S[r], Sg[r], v, ALU.add)
                    if kind == "DS":
                        ins.then_inc(s_ready, 1)
                        dve.wait_ge(s_ready, h + 1)
                        ins = dve.tensor_tensor(Sg, S, bc(egl.rearrange("p (hp n) -> p hp n", hp=HP)[
                            :, :, h + 1], C), ALU.mult)
                else:
                    if kind == "KK":
                        dve.wait_ge(f_ready, 2)
                    for q in range(2):
                        r = slice(q * C, (q + 1) * C)
                        sl = slice(h * HALF, (h + 1) * HALF)
                        v = banks[q].rearrange("p (s n) -> p s n", n=C)
                        if kind == "M":
                            ins = add_scaled(N[r, sl], v, -1.0, rep(eye[r], HALF))
                        else:
                            ins = dve.tensor_tensor((A if kind == "KK" else qkT)[r, sl], v,
                                                    (F1 if kind == "KK" else F2)[r, sl], ALU.mult)
                ins.then_inc(dn_dve, 1)
                if kind == "KQ":
                    dve.wait_ge(dn_dve, JOB[("KK", h)] + 1)
                    step(dve.tensor_tensor(hslots(T, h), hslots(A, h), rep(cc("m1"), HALF), ALU.mult))
                    dve.tensor_tensor(hslots(T, h), rep(eye, HALF), hslots(T, h), ALU.subtract).then_inc(
                        base_ready, 1)

            def gated(kind, i):
                n, count = wuse(kind, i)
                dve.wait_ge(w_done, n + 1)
                side = 1 if kind == "ub" else 0
                if i == 0:
                    dve.wait_ge(w_act, wuse("in", len(GROUPS) - 1)[1])
                v = gates[:, side, 2 * i:2 * i + 2]
                dve.tensor_tensor(v, v, ps[:, n % 2, :].rearrange("p (b n) -> p b n", b=2),
                                  ALU.mult).then_inc(w_dve, 1)

            for what, *which in ORDER:
                if what == "job":
                    empty(*which)
                elif what == "ub":
                    gated("ub", which[0])
                elif what == "in" and which[1] == 0 and which[0] + 1 in range(POOL_GROUPS, len(GROUPS)):
                    low_part(dve, which[0] + 1, w_lo_dve)
                elif (what, *which) == ("in", 14, 1):
                    dve.wait_ge(w_act, wuse("in", 13)[1])
                    dve.tensor_tensor(zT[:], zT[:], zsig, ALU.mult).then_inc(z_ready, 1)
                elif what == "qsum":
                    invert_norms(1)
                elif what == "qspread":
                    normalise(1)
                    dve.wait_ge(rows_exp, 1)
                    dve.wait_ge(normed, 2 * HP)
                    dve.tensor_tensor(egr, egr, qT.rearrange("p b (n c) -> p (b n) c", c=C),
                                      ALU.mult).then_inc(qg_ready, 1)
                elif what == "osum":
                    invert_norms(2)
                elif what == "ospread":
                    dve.wait_ge(norms_spread, 3)
                    dve.wait_ge(z_ready, 1)
                    for hp in range(HP):
                        step(add_scaled(zT[:, hp], zT[:, hp], pp("dn"), spread(2, hp), ALU.mult, ALU.mult))
                        dve.tensor_tensor(zT[:, hp], oT[:, hp], zT[:, hp], ALU.mult).then_inc(o_ready, 1)

            def mix_low(i):
                dve.wait_ge(mix_hi_ready, i + 1)
                c = slice(2 * i, 2 * i + 2)
                dve.tensor_tensor(mix_lo[:, c], gates[:, 0, c], mix_hi[:, c].bitcast(F32),
                                  ALU.subtract).then_inc(mix_lo_ready, 1)

            for i in range(4):
                wout_low(dve, KD // 2 + i, wout_lo_dve)
                gated("ua", i)
                dve.wait_ge(w_dve, wuse("ua", i)[1])
                dve.tensor_tensor(gates[:, 0, 2 * i:2 * i + 2], gates[:, 0, 2 * i:2 * i + 2],
                                  gates[:, 1, 2 * i:2 * i + 2], ALU.add).then_inc(mix_ready, 1)
                if i:
                    mix_low(i - 1)
            mix_low(3)
            def add_mixer(i):
                t, c = i // 2, i % 2
                n, count = wuse("wo", i)
                dve.wait_ge(w_done, n + 1)
                v = xs[:, t, c * 512:(c + 1) * 512]
                dve.tensor_tensor(v, v, ps[:, n % 2, :], ALU.add).then_inc(w_dve, 1)
                dve.wait_ge(w_dve, count)
                step(square_sum(v, half_ss[:, c:c + 1]))
                if c == 1:
                    step(dve.tensor_tensor(ssx[:, t:t + 1], half_ss[:, 0:1], half_ss[:, 1:2], ALU.add))
                    dve.tensor_scalar(ssx[:, t:t + 1], ssx[:, t:t + 1], 1.0 / D, EPS, ALU.mult, ALU.add).then_inc(
                        ss_ready, 1)

            def empty_turned(t):
                for h in range(2):
                    dve.wait_ge(x2T_done, 2 * t + h + 1)
                    dve.tensor_tensor(
                        h2T[:, 4 * h:4 * h + 4, t * P:(t + 1) * P],
                        ps[:, 2 + 2 * t + h, :].rearrange("p (k n) -> p k n", k=4),
                        bc(pp("gffn")[:, 4 * h:4 * h + 4], P), ALU.mult).then_inc(h2T_ready, 1)

            add_mixer(0)
            add_mixer(1)
            scale_rows(2, 0, xn2, xn2_ready)
            add_mixer(2)
            empty_turned(0)
            add_mixer(3)
            scale_rows(3, 1, xn2, xn2_ready)
            empty_turned(1)
            logit = rt[:, 512:512 + TT * (E + 4)].rearrange("p (t e) -> p t e", t=TT)
            mask = rt[:, 64:128].rearrange("p (t e) -> p t e", t=TT)
            left = rt[:, 640:640 + TT * (E + 4)].rearrange("p (t e) -> p t e", t=TT)
            top = rt[:, 192:208].rearrange("p (t e) -> p t e", t=TT)
            soft = rt[:, 224:288].rearrange("p (t e) -> p t e", t=TT)
            den = rt[:, 288:290]
            where = rt[:, 320:384].rearrange("p (t e) -> p t e", t=TT)
            dve.memset(rt[:, 480:488], MARK)
            dve.memset(pos[:, :, NPOS - 1:NPOS], -1.0)
            dve.memset(comb[:, :, NPOS - 1:NPOS], 0.0)
            def build_sel(i):
                for t in range(TT):
                    ins = dve.tensor_scalar(sel[:, t], cc("iota")[:, 0:CAP], pos[:, t, bass.ds(i, 1)], None,
                                            ALU.is_equal)
                ins.then_inc(sel_ready, 1)

            def build_selw(i):
                for t in range(TT):
                    ins = dve.tensor_scalar(selw[:, t], cc("iota"), pos[:, t, bass.ds(i, 1)],
                                            comb[:, t, bass.ds(i, 1)], ALU.is_equal, ALU.mult)
                ins.then_inc(selw_ready, 1)

            for t in range(TT):
                dve.wait_ge(logits_done, t + 1)
                step(dve.tensor_tensor(logit[:, t, 0:E], ps[:, 6 + t, 0:E], pp("brouter"), ALU.add))
                step(dve.tensor_copy(logit[:, t, E:E + 4], rt[:, 480:484]))
                step(dve.max(out=top[:, t], in_=logit[:, t, 0:E]))
                dve.tensor_scalar(soft[:, t], logit[:, t, 0:E], top[:, t, 0:1], None, ALU.subtract).then_inc(soft_in, 1)
                step(dve.tensor_copy(top[:, t, TOP_K:8], rt[:, 484:488]))
                step(dve.match_replace(out=left[:, t], in_to_replace=top[:, t], in_values=logit[:, t],
                                       imm_value=GONE))
                ins = dve.tensor_tensor(mask[:, t], logit[:, t, 0:E], left[:, t, 0:E], ALU.is_gt)
                ins.then_inc(mask_ready, 1)
            dve.wait_ge(mask_ready, TT)
            dve.wait_ge(soft_exp, 1)
            step(dve.tensor_tensor(soft, soft, mask, ALU.mult))
            step(dve.tensor_reduce(den, soft, AX.X, ALU.add))
            step(dve.reciprocal(den, den))
            for t in range(TT):
                step(dve.tensor_scalar(comb[:, t, 0:ROUNDS * E].rearrange("p (r e) -> p r e", r=ROUNDS),
                                       rep(soft[:, t], ROUNDS), den[:, t:t + 1], None, ALU.mult))
            dve.wait_ge(count_done, 1)
            step(add_scaled(where, ps[:, 2, 0:TT * E].rearrange("p (t e) -> p t e", t=TT), 1.0, mask,
                            ALU.add, ALU.mult))
            for r in range(ROUNDS):
                ins = dve.tensor_scalar(pos[:, :, r * E:(r + 1) * E], where, -1.0 - r * CAP, None, ALU.add)
                if r == 0:
                    step(ins)
                    dve.wait_ge(count_done, 2)
                    dve.tensor_reduce(rt[0:1, 490:491], ps[0:1, 3, 0:E], AX.X, ALU.max).then_inc(flag_ready, 1)
                    build_sel(0)
            dve.wait_ge(flag_ready, 1)
            dve.tensor_copy(flag[0:1, 0:1], rt[0:1, 490:491]).then_inc(flag_ready, 1)
            build_selw(0)

            def empty_gather(i):
                dve.wait_ge(turned, i + 1)
                for c in range(2):
                    ins = dve.tensor_tensor(
                        xe[:, 4 * c:4 * c + 4, :],
                        ps[:, 3, :].rearrange("p (j c n) -> p j c n", j=4, c=2)[:, :, c, :],
                        bc(pp("gffn")[:, 4 * c:4 * c + 4], CAP), ALU.mult)
                ins.then_inc(xe_ready, 1)

            def expert(i, more=True):
                dve.wait_ge(gathered, i + 1)
                if more:
                    build_sel(i + 1)
                dve.wait_ge(unit_used, UNITS * i + GU_UNITS)
                dve.tensor_scalar(gmin, ps[:, 0, :], LIMIT, None, ALU.min).then_inc(gmin_ready, 1)
                dve.tensor_scalar(act_t, ps[:, 1, :], LIMIT, -LIMIT, ALU.min, ALU.max).then_inc(gu_read, 1)
                dve.wait_ge(gu_read, i + 1)
                add_scaled(act_t, act_t, 1.0, gmin, ALU.add, ALU.mult).then_inc(up_ready, 1)
                dve.wait_ge(up_ready, i + 1)
                dve.wait_ge(gate_sig, i + 1)
                dve.tensor_tensor(act_a, act_t, sig, ALU.mult).then_inc(act_ready, 1)
                if more:
                    dve.wait_ge(ct_done, i + 1)
                    build_selw(i + 1)
                    empty_gather(i + 1)

            def first_expert(i):
                build_sel(i)
                build_selw(i)
                empty_gather(i)

            empty_gather(0)
            with dve.Fori(0, E - 1) as i:
                expert(i)
            expert(E - 1, more=False)
            over = dve.value_load(flag[0:1, 0:1], min_val=0, max_val=L)
            with dve.If(over > CAP):
                dve.wait_ge(ct_done, E)
                first_expert(E)
                with dve.Fori(E, ROUNDS * E - 1) as i:
                    expert(i)
                expert(ROUNDS * E - 1, more=False)
                dve.wait_ge(scattered, TT * (ROUNDS * E + 1))
            for t in range(TT):
                dve.wait_ge(scattered, TT * E + t + 1)
                v = xs[:, t].rearrange("p (c n) -> p c n", c=2)
                dve.tensor_tensor(v, v, ps[:, 4 + 2 * t:6 + 2 * t, :], ALU.add).then_inc(y_ready, 1)
            for t in range(TT):
                dve.wait_ge(f_sqrt, t + 1)
                step(dve.reciprocal(rstd[:, t:t + 1], rstd[:, t:t + 1]))
                add_scaled(xn2[:, t], xs[:, t], rstd[:, t:t + 1], gfin, ALU.mult, ALU.mult).then_inc(fin_ready, 1)

        @block.scalar
        def _(act):
            fn = act.activation

            def copy(o_, i_):
                return act.copy(o_, i_)

            act.wait_ge(zero_ready, 1)

            def root(n, t):
                act.wait_ge(ss_ready, n + 1)
                fn(rstd[:, t:t + 1], ssx[:, t:t + 1], ACT.Sqrt).then_inc(var_sqrt, 1)

            root(0, 0)
            root(1, 1)

            def high_part(g, blocks=(0, 1)):
                if g >= 2:
                    act.wait_ge(w_done, wuse("in", g - 2)[0] + 1)
                act.wait_ge(w_landed[g % W_SLOTS], 16 * (g // W_SLOTS + 1))
                for b in blocks:
                    c = slice(b * P, (b + 1) * P)
                    copy(w_hi[g % 2][:, :, c], wslot[g % W_SLOTS][:, :, c]).then_inc(w_hi_ready, 1)

            high_part(0, (0,))
            for h in range(2):
                act.wait_ge(hT_ready, h + 1)
                part = (slice(None), slice(4 * h, 4 * h + 4), slice(0, P))
                copy(hT_hi[part], h_full[part]).then_inc(h_hi_act, 1)
            high_part(0, (1,))
            high_part(1)

            def to_conv(g):
                act.wait_ge(w_done, g + 1)
                copy(cpad[:, 2 * g:2 * g + 2, 4:], ps[:, g % 2, :].rearrange("p (b n) -> p b n", b=2)).then_inc(
                    w_act, 1)

            def sigmoid(g):
                act.wait_ge(conv_ready, 2 * g + 2)
                act.wait_ge(silu_ready, g)
                fn(sg, cq[:, 2 * g:2 * g + 2], ACT.Sigmoid).then_inc(sig_ready, 1)

            def square(i):
                act.wait_ge(silu_ready, 2 * i + 2)
                if i:
                    act.wait_ge(sumsq_done, i)
                fn(sq, (kT, qT)[i], ACT.Square).then_inc(sq_ready, 1)

            def norm_root(i, scale=1.0):
                act.wait_ge(sumsq_done, i + 1)
                if i:
                    act.wait_ge(norms_spread, i)
                fn(inv_rows, ps[0:HEADS, 7, 0:L], ACT.Sqrt, bias=eps_c[0:HEADS], scale=scale).then_inc(norm_sqrt, 1)

            to_conv(0)
            high_part(2)
            act.wait_ge(ba_read, 1)
            act.wait_ge(tables_landed, 32)
            fn(ab, ab, ACT.Exp, scale=-1.0).then_inc(act_step, 1)
            fn(ea, pp("alog"), ACT.Exp)
            act.wait_ge(act_step, 1)
            fn(ab, ab, ACT.Ln, bias=1.0).then_inc(sp_exp, 1)
            fn(beta_t, ps[:, 6, 0:32].rearrange("p (t n) -> p t n", t=TT)[:, :, 0:HEADS],
               ACT.Sigmoid).then_inc(decay_act, 1)
            to_conv(1)
            high_part(3)
            sigmoid(0)
            sigmoid(1)
            square(0)
            to_conv(2)
            high_part(4)
            act.wait_ge(cols_ready, 2)
            fn(eG, colG, ACT.Exp)
            fn(kdf, kdf, ACT.Exp)
            fn(egl, colL, ACT.Exp).then_inc(cols_exp, 1)
            sigmoid(2)
            to_conv(3)
            high_part(5)
            sigmoid(3)
            square(1)
            to_conv(4)
            high_part(6)
            norm_root(0)
            act.wait_ge(rows_diff, 1)
            fn(egr, flat_banks(4, C), ACT.Exp).then_inc(rows_exp, 1)
            fn(F2, F2, ACT.Exp).then_inc(f_exp, 1)
            act.wait_ge(rows_diff, 2)
            fn(F1, F1, ACT.Exp, scale=-1.0).then_inc(f_exp, 1)
            sigmoid(4)
            to_conv(5)
            high_part(7)
            sigmoid(5)

            dest = {"KT": ktok, "VT": vtok, "AT": AT, "TN": T, "NT": TTm, "WT": WT, "U": U}
            for what, *which in ORDER:
                if what == "job" and on_act(tuple(which)):
                    name, h = which
                    act.wait_ge(dn_pe, JOB[(name, h)] + 1)
                    kind = name.rstrip("0123456789")
                    if kind == "WT" and h == 0:
                        act.wait_ge(lt_ready, 2 * len(LEVELS))
                    bank = bank_q((name, h))[1]
                    if kind == "O":
                        ins = copy(oT[C:P, :, h * C:(h + 1) * C],
                                   bank[:, 0:HP * C].rearrange("p (s n) -> p s n", n=C))
                    else:
                        ins = copy(dest[kind][C:P, h * HALF:(h + 1) * HALF],
                                   bank.rearrange("p (s n) -> p s n", n=C))
                    ins.then_inc(dn_act, 1)
                elif what == "in" and which[1] == 1:
                    g = which[0]
                    kind = GROUPS[g][0]
                    n = wuse("in", g)[0]
                    act.wait_ge(w_done, n + 1)
                    v = ps[:, n % 2, :].rearrange("p (b n) -> p b n", b=2)
                    at = 2 * sum(k == kind for k, _ in GROUPS[:g])
                    if kind == "u":
                        ins = copy(ub[:, 0, at:at + 2, UPAD:], v)
                    elif kind == "z":
                        copy(zT[:, at:at + 2], v)
                        after_job(act, ("KK", 1))
                        ins = fn(zsig[:, at:at + 2], v, ACT.Sigmoid)
                    else:
                        ins = fn(gates[:, 1 if kind == "gb" else 0, at:at + 2], v, ACT.Sigmoid)
                    ins.then_inc(w_act, 1)
                    if g + 2 < len(GROUPS):
                        high_part(g + 2)
                elif what == "pool":
                    i = which[0]
                    n = wuse("pool", i)[0]
                    act.wait_ge(w_done, n + 1)
                    if i == 0:
                        act.wait_ge(pooled_ready, 4)
                    for b in range(2):
                        g = 2 * i + b
                        ins = fn(ub[:, 1, g, UPAD:], ps[:, n % 2, b * L:(b + 1) * L], ACT.Copy,
                                 scale=pp("pscale")[:, g:g + 1])
                    ins.then_inc(w_act, 1)
                elif what == "osquare":
                    act.wait_ge(dn_dve, len(JOBS))
                    act.wait_ge(dn_act, act_number(("O", NCH - 1)))
                    fn(sq, oT, ACT.Square).then_inc(sq_ready, 1)
                elif what == "qsum":
                    norm_root(1)
                elif what == "osum":
                    norm_root(2, 1.0 / HD)
            act.wait_ge(w_done, wuse("ub", 3)[0] + 1)
            for k in range(KD):
                act.wait_ge(wout_landed[k // 4], 16)
                copy(wout_hi[:, k], wout[:, k]).then_inc(wout_hi_ready, 1)
            for i in range(4):
                act.wait_ge(mix_ready, i + 1)
                copy(mix_hi[:, 2 * i:2 * i + 2], gates[:, 0, 2 * i:2 * i + 2]).then_inc(mix_hi_ready, 1)
            root(2, 0)
            root(3, 1)
            soft = rt[:, 224:288].rearrange("p (t e) -> p t e", t=TT)
            act.wait_ge(soft_in, TT)
            fn(soft, soft, ACT.Exp).then_inc(soft_exp, 1)

            def copy_rows(i):
                act.wait_ge(gathered, i + 1)
                copy(xrows, ps[:, 3, :]).then_inc(rows_copied, 1)

            copy_rows(0)
            act.wait_ge(combT_done, 1)
            copy(combT, ps[0:E, 6, 128:128 + L]).then_inc(combT_ready, 1)

            def expert(i, more=True):
                act.wait_ge(gmin_ready, i + 1)
                fn(sig, gmin, ACT.Sigmoid, scale=ALPHA).then_inc(gate_sig, 1)
                act.wait_ge(ct_done, i + 1)
                act.wait_ge(scattered, TT * (i + 1))
                copy(ctS, ps[:, 2, 0:L]).then_inc(ct_copied, 1)
                if more:
                    copy_rows(i + 1)
                act.wait_ge(actT_done, i + 1)
                copy(actT, ps[:, 2, :]).then_inc(actT_copied, 1)
                act.wait_ge(unit_used, UNITS * (i + 1))
                copy(outS, ps[:, 3, :]).then_inc(out_copied, 1)

            with act.Fori(0, E - 1) as i:
                expert(i)
            expert(E - 1, more=False)
            act.wait_ge(flag_ready, 2)
            over = act.value_load(flag[0:1, 0:1], min_val=0, max_val=L)
            with act.If(over > CAP):
                copy_rows(E)
                with act.Fori(E, ROUNDS * E - 1) as i:
                    expert(i)
                expert(ROUNDS * E - 1, more=False)
                act.nop()
            squares = mo[:, 0:D]
            fn(sm[:, 8:9], eps_c, ACT.Sqrt)
            for t in range(TT):
                act.wait_ge(y_ready, t + 1)
                fn(squares, xs[:, t], ACT.Square, accum_out=ssx[:, t:t + 1]).then_inc(ssf_ready, 1)
                act.wait_ge(ssf_ready, t + 1)
                fn(rstd[:, t:t + 1], ssx[:, t:t + 1], ACT.Sqrt, bias=eps_c, scale=1.0 / D).then_inc(f_sqrt, 1)

        @block.gpsimd
        def _(pool):
            steps = [0]

            def step(ins):
                steps[0] += 1
                ins.then_inc(pool_step, 1)
                pool.wait_ge(pool_step, steps[0])

            tt = pool.tensor_tensor
            pool.memset(cpad[:, :, 0:4], 0.0).then_inc(pads_zeroed, 1)
            for g in range(POOL_GROUPS - 1):
                low_part(pool, g, w_lo_pool)
            pool.wait_ge(tables_landed, 32)
            pool.wait_ge(f_exp, 1)
            tt(F2, F2, rep(cc("upper"), SLOTS), ALU.mult).then_inc(f_ready, 1)
            pool.wait_ge(f_exp, 2)
            step(tt(F1, F1, rep(cc("lower"), SLOTS), ALU.mult))
            tt(F1, F1, bc(colB, C), ALU.mult).then_inc(f_ready, 1)
            low_part(pool, POOL_GROUPS - 1, w_lo_pool)
            step(pool.memset(ub[:, :, :, 0:UPAD], 0.0))
            pool.wait_ge(cols_all, 1)

            def scale_tokens(h):
                for o_, src, jobname, f in ((Kb, ktok, "KT", bEG), (vtok, vtok, "VT", colB), (kd, ktok, "KT", kdf)):
                    after_job(pool, (jobname, h))
                    tt(hslots(o_, h), hslots(src, h), bc(f[:, h * HALF:(h + 1) * HALF], C), ALU.mult).then_inc(
                        tok_scaled, 1)

            for n, b in enumerate(LEVELS):
                for h in range(2):
                    if n >= 2:
                        pool.wait_ge(dn_pe, JOB[(f"M{LEVELS[n - 2]}", h)] + 1)
                    if n == 0:
                        after_job(pool, ("AT", h))
                    tt(hslots(LT[n % 2], h), hslots(AT, h), rep(cc(f"lt{b}"), HALF), ALU.mult).then_inc(lt_ready, 1)
                if n == 0:
                    for h in range(2):
                        step(tt(hslots(TTm, h), hslots(AT, h), rep(cc("m1t"), HALF), ALU.mult))
                        tt(hslots(TTm, h), rep(eye, HALF), hslots(TTm, h), ALU.subtract).then_inc(base_t_ready, 1)
                if n in (1, 2):
                    scale_tokens(n - 1)
                if n != len(LEVELS) - 1:
                    continue
                pool.wait_ge(w_act, wuse("in", 7)[1])
                after_job(pool, ("KQ", 1))
                u, s2, W = ub[:, 0], ub[:, 1], UPAD + L
                step(tt(s2[:, :, 1:], u[:, :, 1:], u[:, :, :W - 1], ALU.add))
                step(tt(usum[:, :, 3:], s2[:, 1:, 3:], s2[:, 1:, 1:W - 2], ALU.add))
                step(tt(s2[:, 2:, 7:], usum[:, 1:, 7:], usum[:, 1:, 3:W - 4], ALU.add))
                step(tt(usum[:, 2:, 15:], s2[:, 3:, 15:], s2[:, 3:, 7:W - 8], ALU.add))
                inv = cc("inv").rearrange("p (g n) -> p g n", g=4)
                for g in range(4):
                    s_ = (s2[:, 0], usum[:, 0], s2[:, 2], usum[:, 2])[g]
                    step(tt(s_[:, UPAD:2 * UPAD], s_[:, UPAD:2 * UPAD], inv[:, g], ALU.mult))
                    step(pool.tensor_scalar(s_[:, 2 * UPAD:], s_[:, 2 * UPAD:], 1.0 / POOLS[g], None, ALU.mult))
                    tt(u[:, g, UPAD:], s_[:, UPAD:], u[:, g, UPAD:], ALU.subtract).then_inc(pooled_ready, 1)

            for k in range(KD // 2):
                wout_low(pool, k, wout_lo_pool)


INPUTS = ("x", "consts", "params", "w_in", "pool_w", "w_up_a", "w_up_b", "w_out", "w_router",
          "w_gate_up", "b_gate_up", "w_down", "b_down", "g_final")


def kernel(**inputs):
    import concourse.bacc as bacc
    from concourse.bass_utils import run_bass_kernel_spmd

    a = {k: np.asarray(v) for k, v in inputs.items()}

    def rows(v):
        return np.broadcast_to(v.reshape(1, -1), (P, v.size))

    conv = a["conv_w"][0].T.reshape(3, HP, P, TAPS)[[1, 0, 2]].reshape(12, P, TAPS)
    parts = {
        "conv": conv.transpose(1, 0, 2).reshape(P, -1),
        "dn": np.concatenate([a["dn_norm"][0]] * 2)[:, None],
        "pscale": a["pool_scale"][0].reshape(4, P).T,
        "alog": rows(a["a_log"][0]), "dtb": rows(a["dt_bias"][0]), "brouter": rows(a["b_router"][0]),
        "gmix": a["g_mix"][0].reshape(KD, P).T, "gffn": a["g_ffn"][0].reshape(KD, P).T,
    }
    arrays = {
        "x": a["x"][0], "consts": const_table(),
        "params": np.concatenate([parts[k] for k in PARAMS], axis=1), "g_final": a["g_final"][None, :],
    }
    for name in INPUTS:
        if name not in arrays:
            arrays[name] = a[name][0]
    nc = bacc.Bacc("TRN2", target_bir_lowering=False, num_devices=1)
    launch, args = {}, []
    for name in INPUTS:
        v = np.ascontiguousarray(arrays[name])
        launch[f"in_{name}"] = v
        args.append(nc.dram_tensor(f"in_{name}", v.shape, mybir.dt.from_np(v.dtype), kind="ExternalInput").ap())
    out = nc.dram_tensor("out", (L, D), F32, kind="ExternalOutput").ap()
    build_program(nc, *args, out)
    r = run_bass_kernel_spmd(nc, [launch], core_ids=[0])
    return r.results[0]["out"].reshape(1, L, D)
```
